# Optimizing a Trainium2 kernel written in Bass

```python
import jax, jax.numpy as jnp
from jax import lax
import numpy as np

D_MODEL = 1024
BATCH = 1
SEQ = 256
DEPTH = 2

MLA_HEADS = 8
MLA_NOPE = 64
MLA_ROPE = 32
MLA_V = 64
MLA_Q_RANK = 256
MLA_KV_RANK = 128
Q_BLOCK = 128
CONV_CH = 512
CONV_WIDTH = 31
RET_HEADS = 4
RET_DK = 128
RET_DV = 256
RET_CHUNK = 128
FFN_HIDDEN = -(-8 * D_MODEL // (3 * 256)) * 256
N_BRANCH = 3
ROPE_BASE = 10000.0
EPS = 1e-6

IN_SPLITS = (MLA_Q_RANK, MLA_KV_RANK, MLA_ROPE, 2 * CONV_CH,
             RET_HEADS * RET_DK, RET_HEADS * RET_DK, RET_HEADS * RET_DV, RET_HEADS * RET_DV,
             N_BRANCH * D_MODEL)
IN_COLS = (MLA_Q_RANK + MLA_KV_RANK + MLA_ROPE + 2 * CONV_CH + 2 * RET_HEADS * RET_DK
           + 2 * RET_HEADS * RET_DV + N_BRANCH * D_MODEL)


def rms_norm(x, g):
    xf = x.astype(jnp.float32)
    y = xf * lax.rsqrt(jnp.mean(xf * xf, -1, keepdims=True) + EPS)
    return (y * g.astype(jnp.float32)).astype(x.dtype)

def layer_norm(x, g, b):
    xf = x.astype(jnp.float32)
    mu = jnp.mean(xf, -1, keepdims=True)
    var = jnp.mean(jnp.square(xf - mu), -1, keepdims=True)
    y = (xf - mu) * lax.rsqrt(var + EPS)
    return (y * g.astype(jnp.float32) + b.astype(jnp.float32)).astype(x.dtype)

def rope_tables(positions, dim):
    inv = ROPE_BASE ** (-jnp.arange(0, dim, 2, dtype=jnp.float32) / dim)
    ang = positions.astype(jnp.float32)[..., None] * inv
    return jnp.cos(ang), jnp.sin(ang)

def apply_rope(x, cos, sin):
    if x.ndim == 4:
        cos, sin = cos[:, :, None, :], sin[:, :, None, :]
    cos, sin = cos.astype(x.dtype), sin.astype(x.dtype)
    x1, x2 = jnp.split(x, 2, axis=-1)
    return jnp.concatenate([x1 * cos - x2 * sin, x2 * cos + x1 * sin], axis=-1)

def mla_branch(c_q, c_kv, k_pe, cos, sin, q_norm, w_uq, kv_norm, w_ukv, w_o):
    B, S, _ = c_q.shape
    q = (rms_norm(c_q, q_norm) @ w_uq).reshape(B, S, MLA_HEADS, MLA_NOPE + MLA_ROPE)
    q_nope = q[..., :MLA_NOPE]
    q_pe = apply_rope(q[..., MLA_NOPE:], cos, sin)
    kv = (rms_norm(c_kv, kv_norm) @ w_ukv).reshape(B, S, MLA_HEADS, MLA_NOPE + MLA_V)
    k_nope, v = kv[..., :MLA_NOPE], kv[..., MLA_NOPE:]
    k_pe = apply_rope(k_pe, cos, sin)
    scale = (MLA_NOPE + MLA_ROPE) ** -0.5
    nq = S // Q_BLOCK
    qn_b = q_nope.reshape(B, nq, Q_BLOCK, MLA_HEADS, MLA_NOPE).swapaxes(0, 1)
    qp_b = q_pe.reshape(B, nq, Q_BLOCK, MLA_HEADS, MLA_ROPE).swapaxes(0, 1)

    def block(args):
        qn, qp = args
        s = (jnp.einsum('bqhd,bkhd->bhqk', qn, k_nope)
             + jnp.einsum('bqhr,bkr->bhqk', qp, k_pe))
        p = jax.nn.softmax(s.astype(jnp.float32) * scale, axis=-1).astype(v.dtype)
        return jnp.einsum('bhqk,bkhd->bqhd', p, v)

    o = lax.map(block, (qn_b, qp_b))
    o = o.swapaxes(0, 1).reshape(B, S, MLA_HEADS * MLA_V)
    return o @ w_o

def conv_branch(u, w_dw, b_dw, ln_g, ln_b, w_pw):
    a, gate = jnp.split(u, 2, axis=-1)
    a = a * jax.nn.sigmoid(gate)
    y = lax.conv_general_dilated(
        a, w_dw[:, None, :].astype(a.dtype), window_strides=(1,),
        padding=[(CONV_WIDTH // 2, CONV_WIDTH // 2)],
        dimension_numbers=('NWC', 'WIO', 'NWC'), feature_group_count=CONV_CH) + b_dw
    y = jax.nn.silu(layer_norm(y, ln_g, ln_b))
    return y @ w_pw

def retention_direction(q, k, v, log_gamma, strict):
    C = q.shape[3]
    idx = jnp.arange(C, dtype=jnp.float32)
    diff = idx[:, None] - idx[None, :]
    mask = (diff > 0) if strict else (diff >= 0)
    lg = log_gamma[:, None, None]
    decay = jnp.where(mask, jnp.exp(jnp.where(mask, diff, 0.0) * lg), 0.0).astype(q.dtype)
    scores = jnp.einsum('bhnqd,bhnkd->bhnqk', q, k) * decay[None, :, None]
    inner = jnp.einsum('bhnqk,bhnke->bhnqe', scores, v)
    k_dec = k * jnp.exp((C - 1 - idx)[None, :] * log_gamma[:, None]).astype(k.dtype)[None, :, None, :, None]
    u = jnp.einsum('bhnkd,bhnke->nbhde', k_dec, v)
    chunk_decay = jnp.exp(C * log_gamma).astype(u.dtype)[None, :, None, None]

    def step(state, xs):
        q_c, u_c = xs
        out = jnp.einsum('bhqd,bhde->bhqe', q_c, state)
        return chunk_decay * state + u_c, out

    state0 = jnp.zeros(u.shape[1:], u.dtype)
    _, cross = lax.scan(step, state0, (jnp.moveaxis(q, 2, 0), u))
    cross = jnp.moveaxis(cross, 0, 2) * jnp.exp((idx + 1)[None, :] * log_gamma[:, None]).astype(q.dtype)[None, :, None, :, None]
    return inner + cross

def retention_branch(q, k, v, g, cos, sin, decay_logits, gn_g, w_o):
    B, S, _ = q.shape
    nc = S // RET_CHUNK
    q = apply_rope(q.reshape(B, S, RET_HEADS, RET_DK), cos, sin)
    k = apply_rope(k.reshape(B, S, RET_HEADS, RET_DK), cos, sin) * (RET_DK ** -0.5)
    v = v.reshape(B, S, RET_HEADS, RET_DV)

    def chunked(t):
        return t.reshape(B, nc, RET_CHUNK, RET_HEADS, -1).transpose(0, 3, 1, 2, 4)

    def unchunk(t):
        return t.transpose(0, 2, 3, 1, 4).reshape(B, S, RET_HEADS, -1)

    def flip(t):
        return jnp.flip(t, axis=1)

    log_gamma = jax.nn.log_sigmoid(decay_logits.astype(jnp.float32))
    fwd = retention_direction(chunked(q), chunked(k), chunked(v), log_gamma[0], False)
    bwd = retention_direction(chunked(flip(q)), chunked(flip(k)), chunked(flip(v)), log_gamma[1], True)
    o = unchunk(fwd) + flip(unchunk(bwd))
    of = o.astype(jnp.float32)
    mu = jnp.mean(of, -1, keepdims=True)
    var = jnp.mean(jnp.square(of - mu), -1, keepdims=True)
    on = ((of - mu) * lax.rsqrt(var + EPS)).reshape(B, S, RET_HEADS * RET_DV)
    on = (on * gn_g.astype(jnp.float32)).astype(g.dtype)
    return (jax.nn.silu(g) * on) @ w_o

def first_inputs(seed: int = 0) -> dict:
    key = jax.random.key(seed)
    ks = jax.random.split(key, 32)
    f32 = jnp.float32

    def w(k, shape, fan_in):
        return jax.random.normal(k, shape, f32) * (fan_in ** -0.5)

    def gain(k, shape):
        return 1.0 + 0.02 * jax.random.normal(k, shape, f32)

    def bias(k, shape):
        return 0.02 * jax.random.normal(k, shape, f32)

    L = DEPTH
    x = jax.random.normal(ks[0], (BATCH, SEQ, D_MODEL), f32)
    offset = jax.random.randint(ks[1], (BATCH, 1), 0, SEQ, dtype=jnp.int32)
    positions = offset + jnp.arange(SEQ, dtype=jnp.int32)[None, :]
    k_exp = 5.0 + jnp.arange(RET_HEADS, dtype=f32)
    base_logit = jnp.log(jnp.exp2(k_exp) - 1.0)
    ret_decay_logits = base_logit[None, None, :] + 0.1 * jax.random.normal(ks[2], (L, 2, RET_HEADS), f32)
    return {
        "x": x,
        "positions": positions,
        "ln_mix_pre": gain(ks[3], (L, D_MODEL)),
        "ln_mix_post": gain(ks[4], (L, D_MODEL)),
        "ln_ffn_pre": gain(ks[5], (L, D_MODEL)),
        "ln_ffn_post": gain(ks[6], (L, D_MODEL)),
        "w_in": w(ks[7], (L, D_MODEL, IN_COLS), D_MODEL),
        "mla_q_norm": gain(ks[8], (L, MLA_Q_RANK)),
        "mla_w_uq": w(ks[9], (L, MLA_Q_RANK, MLA_HEADS * (MLA_NOPE + MLA_ROPE)), MLA_Q_RANK),
        "mla_kv_norm": gain(ks[10], (L, MLA_KV_RANK)),
        "mla_w_ukv": w(ks[11], (L, MLA_KV_RANK, MLA_HEADS * (MLA_NOPE + MLA_V)), MLA_KV_RANK),
        "mla_w_o": w(ks[12], (L, MLA_HEADS * MLA_V, D_MODEL), MLA_HEADS * MLA_V),
        "conv_w_dw": w(ks[13], (L, CONV_WIDTH, CONV_CH), CONV_WIDTH),
        "conv_b_dw": bias(ks[14], (L, CONV_CH)),
        "conv_ln_g": gain(ks[15], (L, CONV_CH)),
        "conv_ln_b": bias(ks[16], (L, CONV_CH)),
        "conv_w_pw": w(ks[17], (L, CONV_CH, D_MODEL), CONV_CH),
        "ret_decay_logits": ret_decay_logits,
        "ret_gn_g": gain(ks[18], (L, RET_HEADS * RET_DV)),
        "ret_w_o": w(ks[19], (L, RET_HEADS * RET_DV, D_MODEL), RET_HEADS * RET_DV),
        "w_out": w(ks[20], (L, D_MODEL, D_MODEL), D_MODEL),
        "ffn_w_gate": w(ks[21], (L, D_MODEL, FFN_HIDDEN), D_MODEL),
        "ffn_w_up": w(ks[22], (L, D_MODEL, FFN_HIDDEN), D_MODEL),
        "ffn_w_down": w(ks[23], (L, FFN_HIDDEN, D_MODEL), FFN_HIDDEN),
    }

def first_block(x, positions, ln_mix_pre, ln_mix_post, ln_ffn_pre, ln_ffn_post, w_in,
              mla_q_norm, mla_w_uq, mla_kv_norm, mla_w_ukv, mla_w_o,
              conv_w_dw, conv_b_dw, conv_ln_g, conv_ln_b, conv_w_pw,
              ret_decay_logits, ret_gn_g, ret_w_o, w_out,
              ffn_w_gate, ffn_w_up, ffn_w_down):
    B, S, _ = x.shape
    points = np.cumsum(IN_SPLITS)[:-1].tolist()
    cos_m, sin_m = rope_tables(positions, MLA_ROPE)
    cos_r, sin_r = rope_tables(positions, RET_DK)
    for l in range(DEPTH):
        h = rms_norm(x, ln_mix_pre[l])
        proj = h @ w_in[l]
        c_q, c_kv, k_pe, conv_u, r_q, r_k, r_v, r_g, gate_logits = jnp.split(proj, points, axis=-1)
        y_mla = mla_branch(c_q, c_kv, k_pe, cos_m, sin_m, mla_q_norm[l], mla_w_uq[l],
                           mla_kv_norm[l], mla_w_ukv[l], mla_w_o[l])
        y_conv = conv_branch(conv_u, conv_w_dw[l], conv_b_dw[l], conv_ln_g[l], conv_ln_b[l], conv_w_pw[l])
        y_ret = retention_branch(r_q, r_k, r_v, r_g, cos_r, sin_r, ret_decay_logits[l],
                                 ret_gn_g[l], ret_w_o[l])
        gates = jax.nn.sigmoid(gate_logits).reshape(B, S, N_BRANCH, D_MODEL)
        merged = gates[:, :, 0] * y_mla + gates[:, :, 1] * y_conv + gates[:, :, 2] * y_ret
        x = x + rms_norm(merged @ w_out[l], ln_mix_post[l])
        h = rms_norm(x, ln_ffn_pre[l])
        f = (jax.nn.silu(h @ ffn_w_gate[l]) * (h @ ffn_w_up[l])) @ ffn_w_down[l]
        x = x + rms_norm(f, ln_ffn_post[l])
    return x


ATTN_HEADS = 16
HEAD_DIM = 64
ATTN_WIDTH = ATTN_HEADS * HEAD_DIM
IDX_HEADS = 8
IDX_DIM = 64
IDX_SCALE = (IDX_HEADS ** -0.5) * (IDX_DIM ** -0.5)
TOPK_MAX = 256
ROPE_THETA = 10000.0
D_INNER = 2 * D_MODEL
SSM_HEAD_DIM = 64
SSM_HEADS = D_INNER // SSM_HEAD_DIM
SSM_GROUPS = 4
HEADS_PER_GROUP = SSM_HEADS // SSM_GROUPS
D_STATE = 128
SSM_CONV = 4
SSM_CHUNK = 256
XBC_WIDTH = D_INNER + 2 * SSM_GROUPS * D_STATE
D_FF = 2816
FFN_CONV = 3
SPLITS = (ATTN_WIDTH, ATTN_WIDTH, ATTN_WIDTH, IDX_HEADS * IDX_DIM, IDX_DIM, IDX_HEADS,
          D_INNER, XBC_WIDTH, SSM_HEADS, D_MODEL, D_MODEL)
IN_WIDTH = sum(SPLITS)
SPLIT_POINTS = tuple(int(v) for v in np.cumsum(SPLITS)[:-1])


def rms_norm_2(x, g):
    xf = x.astype(jnp.float32)
    y = xf * lax.rsqrt(jnp.mean(xf * xf, axis=-1, keepdims=True) + EPS)
    return (y * g.astype(jnp.float32)).astype(x.dtype)

def rope_tables_2(positions, dim):
    inv = 1.0 / (ROPE_THETA ** (jnp.arange(0, dim, 2, dtype=jnp.float32) / dim))
    ang = positions.astype(jnp.float32)[..., None] * inv
    return jnp.cos(ang), jnp.sin(ang)

def apply_rope_2(x, cos, sin):
    xf = x.astype(jnp.float32)
    x1, x2 = jnp.split(xf, 2, axis=-1)
    c = cos[:, :, None, :]
    s = sin[:, :, None, :]
    return jnp.concatenate([x1 * c - x2 * s, x2 * c + x1 * s], axis=-1).astype(x.dtype)

def causal_dwconv(x, w, b):
    width = w.shape[0]
    y = lax.conv_general_dilated(
        x, w[:, None, :].astype(x.dtype), window_strides=(1,), padding=[(width - 1, 0)],
        dimension_numbers=("NWC", "WIO", "NWC"), feature_group_count=x.shape[-1])
    return y + b.astype(x.dtype)

def dsa_attention(q, k, v, iq, ik, iw, n_keep):
    bsz, seq = q.shape[:2]
    n_blocks = seq // Q_BLOCK
    kpos = jnp.arange(seq)
    scale = HEAD_DIM ** -0.5

    def block(i):
        start = i * Q_BLOCK
        qb = lax.dynamic_slice_in_dim(q, start, Q_BLOCK, axis=1)
        iqb = lax.dynamic_slice_in_dim(iq, start, Q_BLOCK, axis=1)
        iwb = lax.dynamic_slice_in_dim(iw, start, Q_BLOCK, axis=1)
        qpos = start + jnp.arange(Q_BLOCK)
        causal = kpos[None, :] <= qpos[:, None]
        logits = jnp.einsum("bqhd,bsd->bqhs", iqb, ik)
        score = jnp.einsum("bqh,bqhs->bqs", iwb, jax.nn.relu(logits)).astype(jnp.float32) * IDX_SCALE
        score = jnp.where(causal[None], score, -jnp.inf)
        _, sel = lax.top_k(score, n_keep)
        kg = jax.vmap(lambda kb, ib: kb[ib])(k, sel)
        vg = jax.vmap(lambda vb, ib: vb[ib])(v, sel)
        s = jnp.einsum("bqhd,bqkhd->bhqk", qb, kg).astype(jnp.float32) * scale
        valid = sel <= qpos[None, :, None]
        s = jnp.where(valid[:, None], s, -jnp.inf)
        p = jax.nn.softmax(s, axis=-1).astype(v.dtype)
        return jnp.einsum("bhqk,bqkhd->bqhd", p, vg)

    out = lax.map(block, jnp.arange(n_blocks))
    return out.transpose(1, 0, 2, 3, 4).reshape(bsz, seq, ATTN_WIDTH)

def segsum(a):
    t = a.shape[-1]
    cs = jnp.cumsum(a, axis=-1)
    seg = cs[..., :, None] - cs[..., None, :]
    mask = jnp.tril(jnp.ones((t, t), dtype=bool))
    return jnp.where(mask, seg, -jnp.inf)

def ssd_scan(xs, a, bm, cm):
    bsz, seq = xs.shape[:2]
    t = SSM_CHUNK
    pad = (-seq) % t
    if pad:
        padw = lambda z: jnp.pad(z, [(0, 0), (0, pad)] + [(0, 0)] * (z.ndim - 2))
        xs, a, bm, cm = padw(xs), padw(a), padw(bm), padw(cm)
    nc = (seq + pad) // t
    xs_c = xs.reshape(bsz, nc, t, SSM_GROUPS, HEADS_PER_GROUP, SSM_HEAD_DIM)
    bm_c = bm.reshape(bsz, nc, t, SSM_GROUPS, D_STATE)
    cm_c = cm.reshape(bsz, nc, t, SSM_GROUPS, D_STATE)
    a_c = a.reshape(bsz, nc, t, SSM_GROUPS, HEADS_PER_GROUP).transpose(0, 3, 4, 1, 2)
    a_cs = jnp.cumsum(a_c, axis=-1)
    decay = jnp.exp(segsum(a_c))
    cb = jnp.einsum("bclgn,bcsgn->bgcls", cm_c, bm_c)
    y_diag = jnp.einsum("bgcls,bgrcls,bcsgrp->bclgrp", cb, decay, xs_c)
    decay_states = jnp.exp(a_cs[..., -1:] - a_cs)
    states = jnp.einsum("bclgn,bgrcl,bclgrp->bcgrpn", bm_c, decay_states, xs_c)
    states = jnp.concatenate([jnp.zeros_like(states[:, :1]), states], axis=1)
    chunk_decay = jnp.exp(segsum(jnp.pad(a_cs[..., -1], ((0, 0), (0, 0), (0, 0), (1, 0)))))
    prev_states = jnp.einsum("bgrzc,bcgrpn->bzgrpn", chunk_decay, states)[:, :-1]
    y_off = jnp.einsum("bclgn,bcgrpn,bgrcl->bclgrp", cm_c, prev_states, jnp.exp(a_cs))
    y = (y_diag + y_off).reshape(bsz, nc * t, SSM_GROUPS, HEADS_PER_GROUP, SSM_HEAD_DIM)[:, :seq]
    return y.astype(xs.dtype)

def second_inputs(seed: int = 0) -> dict:
    key = jax.random.key(seed)
    ks = jax.random.split(key, 28)
    f32 = jnp.float32

    def nrm(k, shape, fan_in, gain=1.0):
        return jax.random.normal(k, shape, f32) * (gain * fan_in ** -0.5)

    def gain_vec(k, shape):
        return 1.0 + 0.1 * jax.random.normal(k, shape, f32)

    x = jax.random.normal(ks[0], (BATCH, SEQ, D_MODEL), f32)
    c = jax.random.normal(ks[1], (BATCH, D_MODEL), f32)
    start = jax.random.randint(ks[2], (BATCH, 1), 0, 4096, dtype=jnp.int32)
    positions = start + jnp.arange(SEQ, dtype=jnp.int32)[None, :]
    dt0 = jnp.exp(jax.random.uniform(ks[3], (DEPTH, SSM_HEADS), f32, np.log(1e-3), np.log(1e-1)))
    dt_bias = dt0 + jnp.log(-jnp.expm1(-dt0))
    a_log = jnp.log(jax.random.uniform(ks[4], (DEPTH, SSM_HEADS), f32, 1.0, 16.0))
    return {
        "x": x,
        "c": c,
        "positions": positions,
        "w_ada": nrm(ks[5], (DEPTH, D_MODEL, 6 * D_MODEL), D_MODEL, 0.5),
        "b_ada": 0.01 * jax.random.normal(ks[6], (DEPTH, 6 * D_MODEL), f32),
        "norm1_g": gain_vec(ks[7], (DEPTH, D_MODEL)),
        "w_in": nrm(ks[8], (DEPTH, D_MODEL, IN_WIDTH), D_MODEL),
        "q_norm_g": gain_vec(ks[9], (DEPTH, HEAD_DIM)),
        "k_norm_g": gain_vec(ks[10], (DEPTH, HEAD_DIM)),
        "ssm_conv_w": nrm(ks[11], (DEPTH, SSM_CONV, XBC_WIDTH), SSM_CONV),
        "ssm_conv_b": 0.01 * jax.random.normal(ks[12], (DEPTH, XBC_WIDTH), f32),
        "dt_bias": dt_bias,
        "a_log": a_log,
        "d_skip": gain_vec(ks[13], (DEPTH, SSM_HEADS)),
        "ssm_norm_g": gain_vec(ks[14], (DEPTH, D_INNER)),
        "w_attn_o": nrm(ks[15], (DEPTH, ATTN_WIDTH, D_MODEL), ATTN_WIDTH),
        "w_ssm_o": nrm(ks[16], (DEPTH, D_INNER, D_MODEL), D_INNER),
        "w_out": nrm(ks[17], (DEPTH, D_MODEL, D_MODEL), D_MODEL),
        "norm2_g": gain_vec(ks[18], (DEPTH, D_MODEL)),
        "w_up": nrm(ks[19], (DEPTH, D_MODEL, 2 * D_FF), D_MODEL),
        "ffn_conv_w": nrm(ks[20], (DEPTH, FFN_CONV, 2 * D_FF), FFN_CONV),
        "ffn_conv_b": 0.01 * jax.random.normal(ks[21], (DEPTH, 2 * D_FF), f32),
        "w_down": nrm(ks[22], (DEPTH, D_FF, D_MODEL), D_FF),
    }

def second_block(x, c, positions, w_ada, b_ada, norm1_g, w_in, q_norm_g, k_norm_g, ssm_conv_w, ssm_conv_b,
              dt_bias, a_log, d_skip, ssm_norm_g, w_attn_o, w_ssm_o, w_out, norm2_g, w_up, ffn_conv_w,
              ffn_conv_b, w_down):
    bsz, seq, _ = x.shape
    n_keep = min(TOPK_MAX, seq // 4)
    cos, sin = rope_tables_2(positions, HEAD_DIM)
    c_act = jax.nn.silu(c)

    for l in range(DEPTH):
        mod = c_act @ w_ada[l] + b_ada[l]
        sh1, sc1, g1, sh2, sc2, g2 = [m[:, None, :] for m in jnp.split(mod, 6, axis=-1)]

        h = rms_norm_2(x, norm1_g[l]) * (1.0 + sc1) + sh1
        proj = h @ w_in[l]
        q, k, v, iq, ik, iw, z, xbc, dt_raw, ga, gm = jnp.split(proj, SPLIT_POINTS, axis=-1)

        q = apply_rope_2(rms_norm_2(q.reshape(bsz, seq, ATTN_HEADS, HEAD_DIM), q_norm_g[l]), cos, sin)
        k = apply_rope_2(rms_norm_2(k.reshape(bsz, seq, ATTN_HEADS, HEAD_DIM), k_norm_g[l]), cos, sin)
        v = v.reshape(bsz, seq, ATTN_HEADS, HEAD_DIM)
        iq = apply_rope_2(iq.reshape(bsz, seq, IDX_HEADS, IDX_DIM), cos, sin)
        ik = apply_rope_2(ik[:, :, None, :], cos, sin)[:, :, 0, :]
        o_attn = dsa_attention(q, k, v, iq, ik, iw, n_keep) @ w_attn_o[l]

        xbc = jax.nn.silu(causal_dwconv(xbc, ssm_conv_w[l], ssm_conv_b[l]))
        xs, bm, cm = jnp.split(xbc, [D_INNER, D_INNER + SSM_GROUPS * D_STATE], axis=-1)
        xs = xs.reshape(bsz, seq, SSM_GROUPS, HEADS_PER_GROUP, SSM_HEAD_DIM)
        bm = bm.reshape(bsz, seq, SSM_GROUPS, D_STATE)
        cm = cm.reshape(bsz, seq, SSM_GROUPS, D_STATE)
        dt = jax.nn.softplus(dt_raw.astype(jnp.float32) + dt_bias[l].astype(jnp.float32))
        a_cont = -jnp.exp(a_log[l].astype(jnp.float32))
        a_dt = (dt * a_cont).reshape(bsz, seq, SSM_GROUPS, HEADS_PER_GROUP)
        dt_g = dt.reshape(bsz, seq, SSM_GROUPS, HEADS_PER_GROUP, 1).astype(xs.dtype)
        y = ssd_scan(xs * dt_g, a_dt, bm, cm)
        y = y + xs * d_skip[l].reshape(SSM_GROUPS, HEADS_PER_GROUP, 1)
        y = y.reshape(bsz, seq, D_INNER) * jax.nn.silu(z)
        y = rms_norm_2(y.reshape(bsz, seq, SSM_GROUPS, D_INNER // SSM_GROUPS),
                     ssm_norm_g[l].reshape(SSM_GROUPS, D_INNER // SSM_GROUPS)).reshape(bsz, seq, D_INNER)
        o_ssm = y @ w_ssm_o[l]

        mixed = (jax.nn.sigmoid(ga) * o_attn + jax.nn.sigmoid(gm) * o_ssm) @ w_out[l]
        x = x + g1 * mixed

        h = rms_norm_2(x, norm2_g[l]) * (1.0 + sc2) + sh2
        u = causal_dwconv(h @ w_up[l], ffn_conv_w[l], ffn_conv_b[l])
        val, gate = jnp.split(u, 2, axis=-1)
        x = x + g2 * ((jax.nn.silu(gate) * val) @ w_down[l])

    return x


def setup_inputs(seed=0):
    out = dict(first_inputs(seed))
    for name, value in second_inputs(seed + 1).items():
        if name != "x":
            out[name + "_2"] = value
    return out


def reference(
    x, positions, ln_mix_pre, ln_mix_post, ln_ffn_pre, ln_ffn_post, w_in, mla_q_norm, mla_w_uq,
    mla_kv_norm, mla_w_ukv, mla_w_o, conv_w_dw, conv_b_dw, conv_ln_g, conv_ln_b, conv_w_pw,
    ret_decay_logits, ret_gn_g, ret_w_o, w_out, ffn_w_gate, ffn_w_up, ffn_w_down, c_2,
    positions_2, w_ada_2, b_ada_2, norm1_g_2, w_in_2, q_norm_g_2, k_norm_g_2, ssm_conv_w_2,
    ssm_conv_b_2, dt_bias_2, a_log_2, d_skip_2, ssm_norm_g_2, w_attn_o_2, w_ssm_o_2, w_out_2,
    norm2_g_2, w_up_2, ffn_conv_w_2, ffn_conv_b_2, w_down_2,
):
    x = first_block(
        x, positions, ln_mix_pre, ln_mix_post, ln_ffn_pre, ln_ffn_post, w_in, mla_q_norm,
        mla_w_uq, mla_kv_norm, mla_w_ukv, mla_w_o, conv_w_dw, conv_b_dw, conv_ln_g, conv_ln_b,
        conv_w_pw, ret_decay_logits, ret_gn_g, ret_w_o, w_out, ffn_w_gate, ffn_w_up, ffn_w_down,
    )
    return second_block(
        x, c_2, positions_2, w_ada_2, b_ada_2, norm1_g_2, w_in_2, q_norm_g_2, k_norm_g_2,
        ssm_conv_w_2, ssm_conv_b_2, dt_bias_2, a_log_2, d_skip_2, ssm_norm_g_2, w_attn_o_2,
        w_ssm_o_2, w_out_2, norm2_g_2, w_up_2, ffn_conv_w_2, ffn_conv_b_2, w_down_2,
    )


_drawn_inputs = setup_inputs


def setup_inputs(seed=0):
    import zlib

    import numpy as np

    out = dict(_drawn_inputs(seed))
    spreads = {}
    factors = {'ln_ffn_post': 3.062,
     'mla_q_norm': 8.0,
     'mla_kv_norm': 8.0,
     'conv_ln_g': 2.676,
     'conv_ln_b': 3.098,
     'ret_gn_g': 3.384,
     'b_ada_2': 7.648,
     'norm1_g_2': 3.336,
     'q_norm_g_2': 8.0,
     'k_norm_g_2': 8.0,
     'ssm_conv_b_2': 23.479,
     'd_skip_2': 140.545,
     'ssm_norm_g_2': 5.506,
     'norm2_g_2': 2.863,
     'ffn_conv_b_2': 8.0}
    for name, (base, spread) in spreads.items():
        noise = np.random.default_rng([zlib.crc32(name.encode()), seed]).standard_normal(out[name].shape)
        drawn = base * np.exp(spread * noise) if base else spread * noise
        out[name] = __import__('jax').numpy.asarray(drawn.astype(out[name].dtype))
    for name, factor in factors.items():
        out[name] = (out[name] * factor).astype(out[name].dtype)
    return out
```

```python
from contextlib import ExitStack

import numpy as np

import concourse.bass as bass
from concourse import mybir

F32 = mybir.dt.float32
I32 = mybir.dt.int32
ALU = mybir.AluOpType
ACT = mybir.ActivationFunctionType
AX = mybir.AxisListType

P = 128
D = 1024
S = 256
DEPTH = 2
DT = D // P
TT = S // P
EPS = 1e-6

HEADS, NOPE, ROPE, VDIM = 8, 64, 32, 64
QK = NOPE + ROPE
Q_RANK, KV_RANK = 256, 128
CONV_CH, CONV_W = 512, 31
RET_H, RET_DK, RET_DV = 4, 128, 256
FFN = 2816
IN1 = [Q_RANK, KV_RANK, ROPE, 2 * CONV_CH, RET_H * RET_DK, RET_H * RET_DK, RET_H * RET_DV,
       RET_H * RET_DV, 3 * D]
(C_Q, C_KV, C_PE, C_CONV, C_RQ, C_RK, C_RV, C_RG, C_GATE, _E1) = [int(v) for v in np.cumsum([0] + IN1)]

AH, HD = 16, 64
IH, ID = 8, 64
IDX_SCALE = (IH ** -0.5) * (ID ** -0.5)
KEEP = 64
D_IN = 2 * D
SH = D_IN // 64
SG = 4
NST = 128
XBC = D_IN + 2 * SG * NST
D_FF = 2816
IN2 = [D, D, D, IH * ID, ID, IH, D_IN, XBC, SH, D, D]
(C2_Q, C2_K, C2_V, C2_IQ, C2_IK, C2_IW, C2_Z, C2_XBC, C2_DT, C2_GA, C2_GM, _E2) = [
    int(v) for v in np.cumsum([0] + IN2)]

NOT_KEPT = -1.0e30
TAKEN = -3.0e38
TWO_PI = 2 * np.pi
PI_1 = 6.28125
PI_2 = float(np.float32(round((TWO_PI - PI_1) * 2 ** 20) / 2 ** 20))
PI_3 = float(np.float32(TWO_PI - PI_1 - PI_2))
ROUND_MAGIC = 1.5 * 2 ** 23
PI_F = 3.1415925


def offsets(sizes):
    at, out = 0, {}
    for name, n in sizes:
        out[name] = (at, at + n)
        at += n
    return out, at


VEC1, NVEC1 = offsets([("mix_pre", 8), ("mix_post", 8), ("ffn_pre", 8), ("ffn_post", 8), ("q_norm", 2),
                       ("kv_norm", 1), ("conv_w", CONV_W * 4), ("conv_b", 4), ("conv_g", 4),
                       ("conv_beta", 4), ("gn_g", 8), ("decay", 2 * RET_H)])
VEC2, NVEC2 = offsets([("b_ada", 48), ("norm1", 8), ("norm2", 8), ("qn", 1), ("kn", 1), ("conv_w", 4 * 24),
                       ("conv_b", 24), ("dt_bias", 1), ("a_log", 1), ("d_skip", 16), ("ssm_norm", 16),
                       ("fconv_w", 3 * 44), ("fconv_b", 44)])
CON, NCON = offsets([("ident", P), ("ones", P), ("ones64", P), ("rot96", QK), ("rot128", P), ("rot64", P),
                     ("dup", P), ("rotdup", P), ("ahead", TT * S), ("behind", TT * S), ("tri", 384),
                     ("freq", 3), ("eps", 1), ("ones_row", S)])


def rotation(n, dim):
    m = np.zeros((n, n), np.float32)
    half = dim // 2
    for g in range(0, n, dim):
        for i in range(half):
            m[g + half + i, g + i] = -1.0
            m[g + i, g + half + i] = 1.0
    return m


def constants():
    c = np.zeros((P, NCON), np.float32)

    def put(name, v, r0=0):
        a, _ = CON[name]
        c[r0:r0 + v.shape[0], a:a + v.shape[1]] = v

    put("ident", np.eye(P, dtype=np.float32))
    put("ones", np.ones((P, P), np.float32))
    put("ones64", np.kron(np.eye(2, dtype=np.float32), np.ones((64, 64), np.float32)))
    r96 = np.zeros((QK, QK), np.float32)
    r96[NOPE:, NOPE:] = rotation(ROPE, ROPE)
    put("rot96", r96)
    put("rot128", rotation(P, RET_DK))
    put("rot64", rotation(P, HD))
    put("dup", np.tile(np.eye(64, dtype=np.float32), (1, 2)))
    put("rotdup", np.tile(rotation(64, 64), (1, 2)))
    m = (np.arange(P)[:, None] + P * np.arange(TT)[None, :])[:, :, None]
    diff = np.arange(S)[None, None, :] - m
    put("ahead", np.maximum(diff, 0).reshape(P, -1).astype(np.float32))
    put("behind", np.maximum(-diff, 0).reshape(P, -1).astype(np.float32))
    tri = (np.arange(P)[:, None] <= np.arange(P)[None, :]).astype(np.float32)
    put("tri", np.concatenate([tri, np.ones((P, P), np.float32), tri], 1))
    freq = np.zeros((P, 3), np.float32)

    def inv_freq(dim):
        k = np.arange(0, dim, 2, dtype=np.float32) / np.float32(dim)
        return k.astype(np.float64)

    for row in range(P):
        freq[row, 0] = np.float32(10000.0 ** -inv_freq(ROPE)[row % 16])
        freq[row, 1] = np.float32(10000.0 ** -inv_freq(RET_DK)[row % 64])
        freq[row, 2] = np.float32(1) / np.float32(10000.0 ** inv_freq(HD)[row % 32])
    put("freq", freq)
    put("eps", np.full((P, 1), EPS, np.float32))
    put("ones_row", np.ones((P, S), np.float32))
    return c


class Queue:

    def __init__(self, sem):
        self.sem, self.count, self.ops, self.seen = sem, 0, [], {}

    def wait(self, *tokens):
        for t in tokens:
            if t is None:
                continue
            if isinstance(t, list):
                self.wait(*t)
                continue
            sem, value = t
            if self.seen.get(sem.name, 0) < value:
                self.seen[sem.name] = value
                self.ops.append(lambda e, sem=sem, value=value: e.wait_ge(sem, value))

    def do(self, fn, *tokens, mark=True):
        self.wait(*tokens)
        if not mark:
            self.ops.append(fn)
            return None
        self.count += 1
        sem = self.sem
        self.ops.append(lambda e: fn(e).then_inc(sem, 1))
        return (sem, self.count)

    def play(self, eng):
        for op in self.ops:
            op(eng)


class Slot:

    def __init__(self, mem, ring=None):
        self.mem, self.ring, self.free, self.sem, self.loads = mem, ring, None, None, 0

    def release(self, token):
        self.free = token
        self.ring.idle.append(self)


class Ring:

    def __init__(self, mems):
        self.slots = [Slot(m, self) for m in mems]
        self.idle = list(self.slots)

    def take(self):
        return self.idle.pop(0)


def weave(main, filler, every=1, each=1):
    n = 0
    for _ in main:
        n += 1
        if n % every == 0:
            for _ in range(each):
                next(filler, None)


def run(steps):
    for _ in steps:
        pass


def build(nc, A):
    with ExitStack() as ctx:
        def sb(name, shape, dt=F32):
            return ctx.enter_context(nc.sbuf_tensor(name, shape, dt))

        def sem(name):
            return ctx.enter_context(nc.semaphore(name))

        pe, ve, ac, po, sp = (Queue(sem(n)) for n in ("pe_done", "ve_done", "ac_done", "po_done", "sp_done"))

        con = sb("con", [P, NCON])
        vec = sb("vec", [P, DEPTH * (NVEC1 + NVEC2)])
        xres = sb("xres", [P, DT, S])
        hid = sb("hid", [P, DT, S])
        rope_cs = sb("rope_cs", [P, 6, S])
        pos_i = sb("pos_i", [P, 2, S], I32)
        small = sb("small", [P, 256])
        mod = sb("mod", [P, DEPTH, 48])
        ccol = sb("ccol", [P, DT])
        cact = sb("cact", [P, DT])

        wring = Ring([sb(f"wslot{i}", [P, 2048]) for i in range(6)])
        for i, s in enumerate(wring.slots):
            s.sem = sem(f"w_landed{i}")
        tmp = Ring([sb(f"tmp{i}", [P, 2, S]) for i in range(6)])
        prob = Ring([sb(f"prob{i}", [P, 2, S]) for i in range(3)])
        probT = Ring([sb(f"probT{i}", [P, 2, S]) for i in range(2)])
        stat = Ring([sb(f"stat{i}", [P, 16]) for i in range(4)])
        arena = sb("arena", [P, 23 * 1024])

        def region(at, *shape):
            n = int(np.prod(shape))
            assert at + n <= 23 * 1024, (at, shape)
            v = arena[:, at:at + n]
            if len(shape) == 1:
                return v
            return v.rearrange("p (a b) -> p a b", a=shape[0])

        banks = [ctx.enter_context(nc.psum_tensor(f"bank{i}", [P, 2, S], F32)) for i in range(8)]
        big = Ring(banks[0:3])
        small_ps = Ring(banks[3:8])

        def cn(name, rows=P, r0=0):
            a, b = CON[name]
            return con[r0:r0 + rows, a:b]

        ident, ones, eps = cn("ident"), cn("ones"), cn("eps")

        def mm(out, lhsT, rhs, start, stop, *tokens, mark=None, skip=False):
            return pe.do(lambda e: e.matmul(out, lhsT, rhs, start=start, stop=stop, skip_group_check=skip),
                         *tokens, mark=stop if mark is None else mark)

        def tr(out, in_, idn, *tokens, mark=True):
            return pe.do(lambda e: e.transpose(out, in_, idn), *tokens, mark=mark)

        def act(out, in_, fn, *tokens, bias=0.0, scale=1.0, acc=None, mark=True):
            if fn == ACT.Copy:
                return ac.do(lambda e: e.activation(out, in_, fn, scale=scale), *tokens, mark=mark)
            if acc is None:
                return ac.do(lambda e: e.activation(out, in_, fn, bias=bias, scale=scale), *tokens, mark=mark)
            return ac.do(lambda e: e.activation(out, in_, fn, bias=bias, scale=scale, accum_out=acc),
                         *tokens, mark=mark)

        def ts(q, out, in0, s1, s2, op0, op1, *tokens, mark=True):
            if s2 is None:
                return q.do(lambda e: e.tensor_scalar(out, in0, s1, None, op0), *tokens, mark=mark)
            return q.do(lambda e: e.tensor_scalar(out, in0, s1, s2, op0, op1), *tokens, mark=mark)

        def tt(q, out, a, b, op, *tokens, mark=True):
            return q.do(lambda e: e.tensor_tensor(out, a, b, op), *tokens, mark=mark)

        def stt(out, in0, s, in1, op0, op1, *tokens, mark=True):
            return ve.do(lambda e: e.scalar_tensor_tensor(out, in0, s, in1, op0, op1), *tokens, mark=mark)

        def recip(out, in_, *tokens):
            return ve.do(lambda e: e.reciprocal(out, in_), *tokens)

        def load(dst, src, s, *tokens):
            sp.wait(*tokens)
            s.loads += 1
            landed = s.sem
            sp.ops.append(lambda e: e.dma_start(dst, src).then_inc(landed, 16))
            return (landed, 16 * s.loads)

        def load_weights(src, kts, width):
            s = wring.take()
            view = s.mem[:, 0:kts * width].rearrange("p (t n) -> p t n", t=kts)
            return s, view, load(view, src.rearrange("(t p) n -> p t n", p=P), s, s.free)

        def linear(w, cols, rhs, ready, sink, kts=DT):
            for i, c in enumerate(cols):
                bank = big.take()
                pe.wait(bank.free)
                for k0 in range(0, kts, 8):
                    n = min(8, kts - k0)
                    slot, view, landed = load_weights(w[k0 * P:(k0 + n) * P, c:c + 256], n, 256)
                    pe.wait(landed)
                    for half in range(2):
                        for k in range(n):
                            pe.wait(ready[k0 + k])
                            whole = kts <= 8
                            first = k0 + k == 0
                            done = mm(bank.mem[:, half, :], view[:, k, half * P:(half + 1) * P], rhs(k0 + k),
                                      first and (whole or half == 0), k0 + k == kts - 1,
                                      mark=k == n - 1 and half == 1, skip=not whole)
                    slot.release(done)
                bank.release(sink(i, bank.mem, done))
                yield

        def linear_tokens(w, cols, lhs, ready, sink):
            for i, c in enumerate(cols):
                bank = big.take()
                pe.wait(bank.free)
                slot, view, landed = load_weights(w[:, c:c + 256], DT, 256)
                pe.wait(landed)
                for t in range(TT):
                    for k in range(DT):
                        done = mm(bank.mem[:, t, :], lhs(k, t), view[:, k, :], k == 0, k == DT - 1,
                                  ready[k], mark=k == DT - 1 and t == 1)
                slot.release(done)
                bank.release(sink(i, bank.mem, done))
                yield

        first_loads = Slot(None)
        first_loads.sem = sem("small_landed")
        load(con[:, :], A["consts"], first_loads)
        load(vec[:, :], A["vectors"], first_loads)
        load(xres[:, :, :], A["x"].rearrange("p (t s) -> p t s", t=DT), first_loads)
        load(pos_i[:, :, :], A["positions"].rearrange("p (t s) -> p t s", t=2), first_loads)
        inputs = load(ccol[:, :], A["c"], first_loads)
        for q in (pe, ve, ac, po):
            q.wait(inputs)

        def v1(l, name, j=0, n=1, rows=P, r0=0):
            a = l * NVEC1 + VEC1[name][0] + j
            return vec[r0:r0 + rows, a:a + n]

        def v2(l, name, j=0, n=1, rows=P, r0=0):
            a = DEPTH * NVEC1 + l * NVEC2 + VEC2[name][0] + j
            return vec[r0:r0 + rows, a:a + n]

        tables = None
        for k in range(3):
            which = 0 if k < 2 else 1
            cos, sin = rope_cs[:, 2 * k, :], rope_cs[:, 2 * k + 1, :]
            t1, t2, t3 = tmp.take(), tmp.take(), tmp.take()
            ang, n, r = t1.mem[:, 0, :], t2.mem[:, 0, :], t3.mem[:, 0, :]
            w = ve.do(lambda e, o=ang, i=pos_i[:, which, :]: e.tensor_copy(o, i), t1.free, t2.free, t3.free)
            f = cn("freq")[:, k:k + 1]
            w = ts(ve, ang, ang, f, None, ALU.mult, None, w)
            w = ts(ve, n, ang, float(1 / TWO_PI), ROUND_MAGIC, ALU.mult, ALU.add, w)
            w = ts(ve, n, n, ROUND_MAGIC, None, ALU.subtract, None, w)
            w = stt(r, n, -PI_1, ang, ALU.mult, ALU.add, w)
            w = stt(r, n, -PI_2, r, ALU.mult, ALU.add, w)
            w = stt(r, n, -PI_3, r, ALU.mult, ALU.add, w)
            w = ts(ve, r, r, PI_F, -PI_F, ALU.min, ALU.max, w)
            wa = act(sin, r, ACT.Sin, w)
            wb = act(cos, r, ACT.Sin, w, scale=0.5)
            w = tt(ve, cos, cos, cos, ALU.mult, wb)
            tables = ts(ve, cos, cos, -2.0, 1.0, ALU.mult, ALU.add, w)
            for t in (t1, t2, t3):
                t.release([tables, wa])
        tables = [tables, wa]

        def both(ap):
            return ap.unsqueeze(1).to_broadcast([ap.shape[0], 2, S])

        def mean_square(tiles, ready, width, ones_m, out):
            ps = small_ps.take()
            pe.wait(ps.free)
            n = len(tiles)
            for i, t in enumerate(tiles):
                sq = tmp.take()
                squared = act(sq.mem[:, 0, :], t, ACT.Square, sq.free, ready[i]) if i % 2 else \
                    tt(ve, sq.mem[:, 0, :], t, t, ALU.mult, sq.free, ready[i])
                summed = mm(ps.mem[:, 0, :], ones_m, sq.mem[:, 0, :], i == 0, i == n - 1, squared, mark=True)
                sq.release(summed)
            return rstd(ps, ps.mem[:, 0, :], out, width, summed)

        def rstd(ps, sums, out, width, summed):
            root = act(out, sums, ACT.Sqrt, summed, scale=1.0 / width, bias=eps)
            ps.release(root)
            return recip(out, out, root)

        def norm_residual(ready, gain, shift, done_reading):
            r = tmp.take()
            ve.wait(r.free)
            ac.wait(r.free)
            rs = r.mem[:, 0, :]
            w = mean_square([xres[:, t, :] for t in range(DT)], ready, D, ones, rs)
            out = []
            for t in range(DT):
                h = stt(hid[:, t, :], xres[:, t, :], gain(t), rs, ALU.mult, ALU.mult, w, done_reading)
                last = h
                if shift is not None:
                    h = act(hid[:, t, :], hid[:, t, :], ACT.Identity, h, bias=shift(t))
                out.append(h)
            r.release(last)
            return out

        def hid_k(k):
            return hid[:, k, :]

        def hid_kt(k, t):
            return hid[:, k, t * P:(t + 1) * P]

        def log1p(e, u, shape):
            z, z2, acc = (tmp.take() for _ in range(3))
            zz, zz2, aa = (t.mem[0:shape[0], 0, 0:shape[1]] for t in (z, z2, acc))
            w = ts(ve, zz, u, 2.0, None, ALU.add, None, e, z.free, z2.free, acc.free)
            w = recip(zz, zz, w)
            w = tt(ve, zz, zz, u, ALU.mult, w)
            w = tt(ve, zz2, zz, zz, ALU.mult, w)
            w = ts(ve, aa, zz2, 2.0 / 17, 2.0 / 15, ALU.mult, ALU.add, w)
            for d in (13, 11, 9, 7, 5, 3, 1):
                w = tt(ve, aa, aa, zz2, ALU.mult, w)
                w = ts(ve, aa, aa, 2.0 / d, None, ALU.add, None, w)
            w = tt(ve, u, aa, zz, ALU.mult, w)
            for t in (z, z2, acc):
                t.release(w)
            return w

        def rotate(x, n_rows, r0, rot, table, ready, out=None, rows_out=None):
            cos = rope_cs[r0:r0 + n_rows, 2 * table, :]
            sin = rope_cs[r0:r0 + n_rows, 2 * table + 1, :]
            ps = small_ps.take()
            turned = mm(ps.mem[r0:r0 + n_rows, :, :], rot, x, True, True, ps.free, ready)
            a = tmp.take()
            am = a.mem[r0:r0 + n_rows, :, :]
            w1 = tt(ve, am, ps.mem[r0:r0 + n_rows, :, :], both(sin), ALU.mult, turned, a.free, tables)
            ps.release(w1)
            w2 = tt(po, x, x, both(cos), ALU.mult, turned, ready, tables)
            w3 = tt(ve, x, x, am, ALU.add, w1, w2)
            a.release(w3)
            return w3

        silu_c = act(cact[:, :], ccol[:, :], ACT.Silu, inputs)
        mod_ready = [None] * DEPTH

        def modulation(l):
            w = A["w_ada"][l]
            for half in range(2):
                bank = small_ps.take()
                pe.wait(bank.free)
                flat = bank.mem[:, 0, :]
                for b in range(12):
                    c = (half * 12 + b) * 256
                    slot, view, landed = load_weights(w[:, c:c + 256], DT, 256)
                    pe.wait(landed, silu_c)
                    for j in range(2):
                        for k in range(DT):
                            done = mm(flat[:, 2 * b + j:2 * b + j + 1], view[:, k, j * P:(j + 1) * P],
                                      cact[:, k:k + 1], k == 0, k == DT - 1, mark=k == DT - 1 and j == 1)
                    slot.release(done)
                    if b % 4 == 3 and b < 11:
                        yield
                o = mod[:, l, half * 24:half * 24 + 24]
                w1 = tt(ve, o, flat[:, 0:24], v2(l, "b_ada", half * 24, 24), ALU.add, done)
                bank.release(w1)
                scale = mod[:, l, half * 24 + 8:half * 24 + 16]
                w2 = stt(scale, scale, 1.0, v2(l, "norm2" if half else "norm1", 0, 8), ALU.add, ALU.mult, w1)
                yield
            mod_ready[l] = w2

        def softmax_rows(ps, done, nk, scale, mask, tag):
            st = stat.take()
            p = prob.take()
            mx, nm, sm, rs = (st.mem[:, 2 * j:2 * j + 2] for j in range(4))
            if mask is None:
                w = ve.do(lambda e: e.tensor_reduce(mx, ps.mem[:, :, :], AX.X, ALU.max), done, st.free)
                src = ps.mem
            else:
                src = p.mem
                for t in range(TT):
                    n = nk[t]
                    w = ve.do(lambda e, t=t, n=n: e.tensor_tensor_reduce(
                        out=p.mem[:, t, 0:n], in0=ps.mem[:, t, 0:n], in1=mask[:, t, 0:n], scale=1.0,
                        scalar=-3.0e38, op0=ALU.add, op1=ALU.max, accum_out=mx[:, t:t + 1]),
                        done, st.free, p.free)
                ps.release(w)
            w = ts(ve, nm, mx, -scale, None, ALU.mult, None, w)
            for t in range(TT):
                n = nk[t]
                w2 = act(p.mem[:, t, 0:n], src[:, t, 0:n], ACT.Exp, w, p.free, bias=nm[:, t:t + 1], scale=scale,
                         acc=sm[:, t:t + 1])
            if mask is None:
                ps.release(w2)
            w = recip(rs, sm, w2)
            for t in range(TT):
                n = nk[t]
                w3 = ts(po, p.mem[:, t, 0:n], p.mem[:, t, 0:n], rs[:, t:t + 1], None, ALU.mult, None, w, w2)
            st.release([w3, w2])
            return p, w3

        def attend(heads, scores, nk, scale, mask, v_of, out_of, out_free, result):
            live = {}
            pair = {}
            for i in range(heads + 2):
                if i < heads:
                    ps = small_ps.take()
                    pe.wait(ps.free)
                    done = scores(i, ps.mem)
                    live[i] = softmax_rows(ps, done, nk, scale, mask, i)
                    yield
                if 1 <= i <= heads:
                    p, normed = live.pop(i - 1)
                    ps = small_ps.take()
                    pe.wait(ps.free, normed)
                    for kt in range(TT):
                        for t in range(TT):
                            if kt * P >= nk[t]:
                                continue
                            turned = tr(ps.mem[:, kt, t * P:(t + 1) * P], p.mem[:, t, kt * P:(kt + 1) * P], ident,
                                        mark=kt == 1 and t == 1)
                    p.release(turned)
                    pt = probT.take()
                    if nk[0] == S:
                        w = act(pt.mem[:, :, :], ps.mem[:, :, :], ACT.Copy, turned, pt.free)
                    else:
                        act(pt.mem[:, 0, :], ps.mem[:, 0, :], ACT.Copy, turned, pt.free)
                        w = act(pt.mem[:, 1, P:S], ps.mem[:, 1, P:S], ACT.Copy)
                    ps.release(w)
                    live[("t", i - 1)] = (pt, w)
                if 2 <= i:
                    h = i - 2
                    pt, w = live.pop(("t", h))
                    r0 = 64 * (h % 2)
                    if h % 2 == 0:
                        pair["o"] = small_ps.take()
                        pe.wait(pair["o"].free)
                    o = pair["o"]
                    q0 = 0 if nk[0] == S else P
                    mm(o.mem[r0:r0 + 64, 0, :], v_of(h, 0), pt.mem[:, 0, :], True, False, w)
                    done = mm(o.mem[r0:r0 + 64, 0, q0:S], v_of(h, 1), pt.mem[:, 1, q0:S], False, True)
                    pt.release(done)
                    if h % 2:
                        w = act(out_of(h // 2), o.mem[:, 0, :], ACT.Copy, done, out_free)
                        o.release(w)
                        result.append(w)
                    yield

        x_ready = [inputs] * DT
        hid_free = None

        def add_normed(y, y_ready, gain, x_tok):
            r = tmp.take()
            ve.wait(r.free)
            ac.wait(r.free)
            rs = r.mem[:, 0, :]
            w = mean_square([y[:, t, :] for t in range(DT)], y_ready, D, ones, rs)
            out = []
            for t in range(DT):
                w2 = stt(y[:, t, :], y[:, t, :], gain(t), rs, ALU.mult, ALU.mult, w)
                out.append(tt(po, xres[:, t, :], xres[:, t, :], y[:, t, :], ALU.add, w2, x_tok))
            r.release(w2)
            return out

        for l in range(DEPTH):
            w_in = A["w_in"][l]
            gate = [region(0, DT, S), region(2048, DT, S)]
            merged = region(4096, DT, S)
            gbuf = region(6144, DT, S)
            vret = region(8192, TT, RET_H * RET_DV)
            rq, rk = region(10240, RET_H, S), region(11264, RET_H, S)
            conv_a, conv_y = region(12288, 4, S), region(13312, 4, S)
            cq, ckv = region(14336, 2, S), region(14848, S)
            vmla, omla = region(15104, TT, 512), region(16128, 4, S)
            qm, km = region(17152, HEADS, S), region(19200, HEADS, S)
            ymix = region(21248, 1, S)
            conv_g = region(21504, 4, S)

            normed = norm_residual(x_ready, lambda t: v1(l, "mix_pre", t), None, hid_free)

            def take_cq(i, ps, done):
                return act(cq[:, :, :], ps[:, :, :], ACT.Copy, done)
            run(linear(w_in, [C_Q], hid_k, normed, take_cq))
            cq_raw = (ac.sem, ac.count)

            slot, view, landed = load_weights(w_in[:, C_KV:C_CONV], DT, KV_RANK + ROPE)
            ps = small_ps.take()
            pe.wait(landed, ps.free)
            for k in range(DT):
                mm(ps.mem[:, 0, :], view[:, k, 0:P], hid_k(k), k == 0, k == DT - 1, normed[k])
            for k in range(DT):
                done = mm(ps.mem[64:96, 1, :], view[:, k, P:P + ROPE], hid_k(k), k == 0, k == DT - 1)
            slot.release(done)
            ckv_raw = act(ckv, ps.mem[:, 0, :], ACT.Copy, done)
            kpe = tmp.take()
            kpe_raw = act(kpe.mem[64:96, 0, :], ps.mem[64:96, 1, :], ACT.Copy, kpe.free)
            ps.release(kpe_raw)

            r = tmp.take()
            ac.wait(r.free)
            w = mean_square([cq[:, t, :] for t in range(2)], [cq_raw] * 2, Q_RANK, ones, r.mem[:, 0, :])
            for t in range(2):
                cq_n = stt(cq[:, t, :], cq[:, t, :], v1(l, "q_norm", t), r.mem[:, 0, :], ALU.mult, ALU.mult, w)
            w = mean_square([ckv], [ckv_raw], KV_RANK, ones, r.mem[:, 1, :])
            ckv_n = stt(ckv, ckv, v1(l, "kv_norm"), r.mem[:, 1, :], ALU.mult, ALU.mult, w)
            r.release(ckv_n)

            rot96 = cn("rot96", ROPE, 64)[:, 64:96]
            ps = small_ps.take()
            turned = mm(ps.mem[64:96, 0, :], rot96, kpe.mem[64:96, 0, :], True, True, ps.free, kpe_raw)
            cos, sin = rope_cs[64:96, 0, :], rope_cs[64:96, 1, :]
            t1 = tmp.take()
            w1 = tt(ve, t1.mem[64:96, 0, :], ps.mem[64:96, 0, :], sin, ALU.mult, turned, t1.free, tables)
            ps.release(w1)
            w2 = tt(ve, t1.mem[64:96, 1, :], kpe.mem[64:96, 0, :], cos, ALU.mult, kpe_raw)
            for h in range(HEADS):
                kpe_in = tt(po, km[64:96, h, :], t1.mem[64:96, 0, :], t1.mem[64:96, 1, :], ALU.add, w1, w2)
            kpe.release(kpe_in)
            t1.release(kpe_in)

            slot, view, landed = load_weights(A["w_uq"][l], 2, HEADS * QK)
            pe.wait(landed, cq_n)
            q_ready = [None] * 4
            for j in range(4):
                ps = small_ps.take()
                pe.wait(ps.free)
                for i in range(2):
                    h = 2 * j + i
                    for k in range(2):
                        done = mm(ps.mem[0:QK, i, :], view[:, k, h * QK:(h + 1) * QK], cq[:, k, :], k == 0, k == 1)
                w = act(qm[0:QK, 2 * j:2 * j + 2, :], ps.mem[0:QK, :, :], ACT.Copy, done)
                ps.release(w)
                q_ready[j] = w
            slot.release(done)
            for j in range(4):
                q_ready[j] = rotate(qm[64:96, 2 * j:2 * j + 2, :], ROPE, 64, rot96, 0, q_ready[j])

            slot, view, landed = load_weights(A["w_ukv"][l], 1, HEADS * (NOPE + VDIM))
            pe.wait(landed, ckv_n)
            k_ready = [None] * 4
            for j in range(4):
                ps = small_ps.take()
                pe.wait(ps.free)
                for i in range(2):
                    h = 2 * j + i
                    done = mm(ps.mem[0:NOPE, i, :], view[:, 0, h * P:h * P + NOPE], ckv, True, True)
                k_ready[j] = act(km[0:NOPE, 2 * j:2 * j + 2, :], ps.mem[0:NOPE, :, :], ACT.Copy, done)
                ps.release(k_ready[j])
            wv = view[:, 0, :].rearrange("p (h c) -> p h c", h=HEADS)[:, :, NOPE:]
            for t in range(TT):
                ps = small_ps.take()
                done = mm(ps.mem[:, :, :].rearrange("p a b -> p (a b)"), ckv[:, t * P:(t + 1) * P], wv, True, True,
                          ps.free)
                v_ready = act(vmla[:, t, :], ps.mem[:, :, :].rearrange("p a b -> p (a b)"), ACT.Copy, done)
                ps.release(v_ready)
            slot.release(done)

            def mla_scores(h, out):
                pe.wait(q_ready[h // 2], k_ready[h // 2], kpe_in, v_ready)
                for t in range(TT):
                    done = mm(out[:, t, :], qm[0:QK, h, t * P:(t + 1) * P], km[0:QK, h, :], True, True)
                return done

            o_ready = []
            mla = attend(HEADS, mla_scores, [S, S], QK ** -0.5, None,
                         lambda h, kt: vmla[:, kt, h * 64:(h + 1) * 64], lambda j: omla[:, j, :], None, o_ready)

            gate_ready = [[None] * 4 for _ in range(3)]

            def gate_sink(branch):
                def sink(i, ps, done):
                    g = gate[branch % 2]
                    gate_ready[branch][i] = act(g[:, 2 * i:2 * i + 2, :], ps[:, :, :], ACT.Sigmoid, done,
                                                gate_free[branch])
                    return gate_ready[branch][i]
                return sink

            gate_free = [None, None, None]
            conv_in = [None] * 4

            def conv_gate_sink(i, ps, done):
                conv_in[i] = act(conv_g[:, 2 * i:2 * i + 2, :], ps[:, :, :], ACT.Sigmoid, done)
                return conv_in[i]

            conv_ready = [None] * 4

            def conv_a_sink(i, ps, done):
                w = tt(ve, conv_a[:, 2 * i:2 * i + 2, :], ps[:, :, :], conv_g[:, 2 * i:2 * i + 2, :], ALU.mult,
                       done, conv_in[i])
                conv_ready[2 * i] = conv_ready[2 * i + 1] = w
                return w

            def to(dst, out, copy=ACT.Copy):
                def sink(i, ps, done):
                    w = act(dst[:, 2 * i:2 * i + 2, :], ps[:, :, :], copy, done)
                    out.append(w)
                    return w
                return sink

            rq_raw, rk_raw, rg_ready, vret_ready = [], [], [], []

            def vret_sink(i, ps, done):
                w = act(vret[:, :, i * 256:(i + 1) * 256], ps[:, :, :], ACT.Copy, done)
                vret_ready.append(w)
                return w

            def fill():
                yield from linear(w_in, [C_CONV + CONV_CH, C_CONV + CONV_CH + 256], hid_k, normed, conv_gate_sink)
                yield from linear(w_in, [C_CONV, C_CONV + 256], hid_k, normed, conv_a_sink)
                yield from linear(w_in, [C_RQ, C_RQ + 256], hid_k, normed, to(rq, rq_raw))
                yield from linear(w_in, [C_RK, C_RK + 256], hid_k, normed, to(rk, rk_raw))
                yield from linear_tokens(w_in, [C_RV + 256 * i for i in range(4)], hid_kt, normed, vret_sink)
                yield from linear(w_in, [C_RG + 256 * i for i in range(4)], hid_k, normed, to(gbuf, rg_ready, ACT.Silu))
                yield from linear(w_in, [C_GATE + 256 * i for i in range(4)], hid_k, normed, gate_sink(0))
                yield from linear(w_in, [C_GATE + D + 256 * i for i in range(4)], hid_k, normed, gate_sink(1))

            filler = fill()
            weave(mla, filler)

            def conv_steps():
                half = CONV_W // 2
                for t in range(4):
                    pe_free = conv_ready[t]
                    w = ts(ve, conv_y[:, t, :], conv_a[:, t, :], v1(l, "conv_w", half * 4 + t),
                           v1(l, "conv_b", t), ALU.mult, ALU.add, pe_free)
                    for j in range(CONV_W):
                        s = j - half
                        if s == 0:
                            continue
                        lo, hi = max(0, -s), min(S, S - s)
                        w = stt(conv_y[:, t, lo:hi], conv_a[:, t, lo + s:hi + s], v1(l, "conv_w", j * 4 + t),
                                conv_y[:, t, lo:hi], ALU.mult, ALU.add, w)
                        if j % 8 == 7:
                            yield
                    conv_done.append(w)
                    yield

            conv_done = []
            weave(conv_steps(), filler, every=2)
            run(filler)

            ps = small_ps.take()
            for t in range(4):
                w = mm(ps.mem[:, 0, :], ones, conv_y[:, t, :], t == 0, t == 3, ps.free, conv_done[t])
            mu = tmp.take()
            w = act(mu.mem[:, 0, :], ps.mem[:, 0, :], ACT.Copy, w, mu.free, scale=1.0 / CONV_CH)
            ps.release(w)
            centred = [tt(ve, conv_y[:, t, :], conv_y[:, t, :], mu.mem[:, 0, :], ALU.subtract, w) for t in range(4)]
            w = mean_square([conv_y[:, t, :] for t in range(4)], centred, CONV_CH, ones, mu.mem[:, 1, :])
            conv_out = []
            for t in range(4):
                w1 = stt(conv_y[:, t, :], conv_y[:, t, :], v1(l, "conv_g", t), mu.mem[:, 1, :], ALU.mult, ALU.mult, w)
                conv_out.append(act(conv_y[:, t, :], conv_y[:, t, :], ACT.Silu, w1, bias=v1(l, "conv_beta", t)))
            mu.release(w1)

            x = v1(l, "decay", 0, 8)
            lg = small[:, 0:8]
            e = small[:, 8:16]
            w = ve.do(lambda q, x=x: q.tensor_scalar(small[:, 16:24], x, -1.0, None, ALU.mult))
            w = tt(ve, small[:, 16:24], small[:, 16:24], x, ALU.min, w)
            w = act(e, small[:, 16:24], ACT.Exp, w)
            w = log1p(w, e, (P, 8))
            w = stt(lg, x, 0.0, e, ALU.min, ALU.subtract, w)
            lg_ready = w

            merged_ready = [None] * 4

            def first_branch(i, ps, done):
                w = tt(ve, merged[:, 2 * i:2 * i + 2, :], ps[:, :, :], gate[0][:, 2 * i:2 * i + 2, :], ALU.mult,
                       done, gate_ready[0][i])
                merged_ready[i] = w
                return w

            def next_branch(branch):
                def sink(i, ps, done):
                    t = tmp.take()
                    w = tt(ve, t.mem[:, :, :], ps[:, :, :], gate[branch % 2][:, 2 * i:2 * i + 2, :], ALU.mult,
                           done, gate_ready[branch][i], t.free)
                    m = merged[:, 2 * i:2 * i + 2, :]
                    merged_ready[i] = tt(po, m, m, t.mem[:, :, :], ALU.add, w, merged_ready[i])
                    t.release(merged_ready[i])
                    return w
                return sink

            branch_cols = [256 * i for i in range(4)]

            def fill2():
                yield from linear(A["w_o"][l], branch_cols, lambda k: omla[:, k, :], o_ready, first_branch, kts=4)
                gate_free[2] = merged_ready[3]
                yield from linear(w_in, [C_GATE + 2 * D + 256 * i for i in range(4)], hid_k, normed, gate_sink(2))
                yield from linear(A["w_pw"][l], branch_cols, lambda k: conv_y[:, k, :], conv_out, next_branch(1), kts=4)
                yield from modulation(l)

            filler = fill2()

            def retention():
                qr = [rotate(rq[:, 2 * j:2 * j + 2, :], P, 0, cn("rot128"), 1, rq_raw[j]) for j in range(2)]
                kr = [rotate(rk[:, 2 * j:2 * j + 2, :], P, 0, cn("rot128"), 1, rk_raw[j]) for j in range(2)]
                yield
                o_norm = {}
                for h in range(RET_H + 1):
                    if h < RET_H:
                        dec = prob.take()
                        flat = dec.mem[:, :, :].rearrange("p a b -> p (a b)")
                        w = ts(ve, flat, cn("ahead"), lg[:, h:h + 1], None, ALU.mult, None, lg_ready, dec.free)
                        w = stt(flat, cn("behind"), lg[:, 4 + h:5 + h], flat, ALU.mult, ALU.add, w)
                        w_dec = act(flat, flat, ACT.Exp, w)
                        ps = small_ps.take()
                        pe.wait(ps.free, qr[h // 2], kr[h // 2])
                        for mt in range(TT):
                            done = mm(ps.mem[:, mt, :], rk[:, h, mt * P:(mt + 1) * P], rq[:, h, :], True, True)
                        w_dec = stt(dec.mem[:, :, :], ps.mem[:, :, :], RET_DK ** -0.5, dec.mem[:, :, :], ALU.mult,
                                    ALU.mult, done, w_dec)
                        ps.release(w_dec)
                        yield
                        o = small_ps.take()
                        pe.wait(o.free, w_dec, vret_ready)
                        for t in range(TT):
                            for mt in range(TT):
                                done = mm(o.mem[:, t, :], dec.mem[:, mt, t * P:(t + 1) * P],
                                          vret[:, mt, h * 256:(h + 1) * 256], mt == 0, mt == 1)
                        dec.release(done)
                        on, st = tmp.take(), stat.take()
                        for t in range(TT):
                            b = st.mem[:, 8 * t:8 * t + 6]
                            w = ve.do(lambda q, b=b, t=t, o=o: q.bn_stats(b, o.mem[:, t, :]), done, st.free)
                            mv = st.mem[:, 8 * t + 6:8 * t + 8]
                            w = ve.do(lambda q, b=b, mv=mv: q.bn_aggr(mv, b), w)
                            var = mv[:, 1:2]
                            w = act(var, var, ACT.Sqrt, w, bias=eps)
                            w = recip(var, var, w)
                            w = ts(ve, on.mem[:, t, :], o.mem[:, t, :], mv[:, 0:1], var, ALU.subtract, ALU.mult, w,
                                   on.free)
                        o.release(w)
                        st.release(w)
                        o_norm[h] = (on, w)
                        yield
                    if h >= 1:
                        on, w = o_norm.pop(h - 1)
                        ps = small_ps.take()
                        pe.wait(ps.free, w)
                        for half in range(2):
                            for t in range(TT):
                                turned = tr(ps.mem[:, half, t * P:(t + 1) * P], on.mem[:, t, half * P:(half + 1) * P],
                                            ident)
                        on.release(turned)
                        for half in range(2):
                            j = 2 * (h - 1) + half
                            w = stt(gbuf[:, j, :], ps.mem[:, half, :], v1(l, "gn_g", j), gbuf[:, j, :], ALU.mult,
                                    ALU.mult, turned, rg_ready[j // 2])
                            ret_out[j] = w
                        ps.release(w)
                        yield

            ret_out = [None] * DT
            weave(retention(), filler)
            run(filler)

            def third(i, ps, done):
                return next_branch(2)(i, ps, done)
            run(linear(A["w_ro"][l], branch_cols, lambda k: gbuf[:, k, :], ret_out, third))

            y_ready = []
            y = gate[0]
            merged_in = [merged_ready[k // 2] for k in range(DT)]

            def y_sink(dst, out):
                def sink(i, ps, done):
                    w = act(dst[:, 2 * i:2 * i + 2, :], ps[:, :, :], ACT.Copy, done, merged_ready)
                    out.extend([w, w])
                    return w
                return sink
            run(linear(A["w_out"][l], branch_cols, lambda k: merged[:, k, :], merged_in, y_sink(y, y_ready)))
            x_ready = add_normed(y, y_ready, lambda t: v1(l, "mix_post", t), x_ready)

            hid_free = (pe.sem, pe.count)
            normed = norm_residual(x_ready, lambda t: v1(l, "ffn_pre", t), None, hid_free)
            f = region(0, FFN // P, S)
            f_ready = [None] * (FFN // P)
            held = {}

            def gate_half(i, ps, done):
                s = tmp.take()
                w = act(s.mem[:, :, :], ps[:, :, :], ACT.Silu, done, s.free)
                held[i] = (s, w)
                return w

            def up_half(i, ps, done):
                s, w = held.pop(i)
                w2 = tt(ve, f[:, 2 * i:2 * i + 2, :], ps[:, :, :], s.mem[:, :, :], ALU.mult, done, w, x_ready)
                s.release(w2)
                f_ready[2 * i] = f_ready[2 * i + 1] = w2
                return w2

            gs = linear(A["w_gate"][l], [256 * i for i in range(11)], hid_k, normed, gate_half)
            us = linear(A["w_up"][l], [256 * i for i in range(11)], hid_k, normed, up_half)
            for _ in range(11):
                next(gs)
                next(us)
            hid_free = (pe.sem, pe.count)
            y = region(6144, DT, S)
            y_ready = []
            run(linear(A["w_down"][l], branch_cols, lambda k: f[:, k, :], f_ready, y_sink(y, y_ready), kts=22))
            x_ready = add_normed(y, y_ready, lambda t: v1(l, "ffn_post", t), x_ready)

        for l in range(DEPTH):
            w_in = A["w_in2"][l]
            q2, k2 = region(0, DT, S), region(2048, DT, S)
            v2t = region(4096, TT, D)
            iq = region(6144, 4, S)
            ik = region(7168, S)
            keep = region(7424, TT, S)
            score = region(7936, TT, S)
            zbuf = region(8448, 16, S)
            xbc = region(12544, 24, S)
            cbm = region(18688, SG, 384)
            gbuf = region(20224, 2, S)
            dts = region(20736, 4, S)
            xtok = region(2048, TT, D_IN)
            ga, gm = region(0, DT, S), region(0, DT, S)

            def hshift(half):
                return lambda t: mod[:, l, half * 24 + t:half * 24 + t + 1]

            def hscale(half):
                return lambda t: mod[:, l, half * 24 + 8 + t:half * 24 + 9 + t]

            def hgate(half, t):
                return mod[:, l, half * 24 + 16 + t:half * 24 + 17 + t]

            ve.wait(mod_ready[l])
            hid_free = (pe.sem, pe.count)
            normed = norm_residual(x_ready, hscale(0), hshift(0), hid_free)
            arena_free = x_ready

            def qk_sink(dst, gain, out):
                def sink(i, ps, done):
                    x = dst[:, 2 * i:2 * i + 2, :]
                    raw = act(x, ps[:, :, :], ACT.Copy, done, arena_free)
                    sq = tmp.take()
                    w = tt(po, sq.mem[:, :, :], x, x, ALU.mult, raw, sq.free)
                    pending.append((x, raw, sq, w, gain, out))
                    return raw
                return sink

            pending = []
            q_ready, k_ready = [], []

            def finish_qk():
                x, raw, sq, w, gain, out = pending.pop(0)
                ps = small_ps.take()
                w = mm(ps.mem[:, :, :], cn("ones64"), sq.mem[:, :, :], True, True, ps.free, w)
                w = rstd(ps, ps.mem[:, :, :], sq.mem[:, :, :], HD, w)
                w = stt(x, x, gain, sq.mem[:, :, :], ALU.mult, ALU.mult, w)
                sq.release(w)
                late.append((x, w, out))

            late = []

            def finish_rotation():
                x, w, out = late.pop(0)
                out.append(rotate(x, P, 0, cn("rot64"), 2, w))

            steps = [linear(w_in, [C2_Q + 256 * i for i in range(4)], hid_k, normed, qk_sink(q2, v2(l, "qn"), q_ready)),
                     linear(w_in, [C2_K + 256 * i for i in range(4)], hid_k, normed, qk_sink(k2, v2(l, "kn"), k_ready))]
            for st in steps:
                for _ in st:
                    if late:
                        finish_rotation()
                    if len(pending) > 1:
                        finish_qk()
            iq_raw, iq_ready = [], []
            idx = linear(w_in, [C2_IQ, C2_IQ + 256], hid_k, normed, to(iq, iq_raw))
            for _ in idx:
                if late:
                    finish_rotation()
                finish_qk() if pending else None

            slot, view, landed = load_weights(w_in[:, C2_IK:C2_Z], DT, ID + IH)
            ps, psw = small_ps.take(), small_ps.take()
            pe.wait(landed, ps.free, psw.free)
            for k in range(DT):
                done = mm(ps.mem[0:ID, 0, :], view[:, k, 0:ID], hid_k(k), k == 0, k == DT - 1, normed[k])
            ikr = tmp.take()
            w = act(ikr.mem[0:ID, 0, :], ps.mem[0:ID, 0, :], ACT.Copy, done, ikr.free)
            ps.release(w)
            ik_raw = w
            for t in range(TT):
                for k in range(DT):
                    done = mm(psw.mem[:, 0, t * IH:(t + 1) * IH], hid_kt(k, t), view[:, k, ID:ID + IH], k == 0,
                              k == DT - 1)
            slot.release(done)
            iw = small[:, 32:32 + TT * IH]
            iw_ready = act(iw, psw.mem[:, 0, 0:TT * IH], ACT.Copy, done)
            psw.release(iw_ready)
            ps = small_ps.take()
            pe.wait(ps.free, ik_raw)
            mm(ps.mem[:, 0, :], cn("dup", ID), ikr.mem[0:ID, 0, :], True, True)
            done = mm(ps.mem[:, 1, :], cn("rotdup", ID), ikr.mem[0:ID, 0, :], True, True)
            ikr.release(done)
            t1 = tmp.take()
            w = tt(ve, t1.mem[:, :, :], ps.mem[:, :, :], rope_cs[:, 4:6, :], ALU.mult, done, t1.free)
            ps.release(w)
            ik_ready = tt(ve, ik, t1.mem[:, 0, :], t1.mem[:, 1, :], ALU.add, w)
            t1.release(ik_ready)
            while late or pending:
                if late:
                    finish_rotation()
                if pending:
                    finish_qk()
            for j in range(2):
                iq_ready.append(rotate(iq[:, 2 * j:2 * j + 2, :], P, 0, cn("rot64"), 2, iq_raw[j]))

            v_ready, z_ready = [], []
            xbc_ready = [None] * 24

            def v_sink(i, ps, done):
                w = act(v2t[:, :, i * 256:(i + 1) * 256], ps[:, :, :], ACT.Copy, done)
                v_ready.append(w)
                return w

            def xbc_sink(i, ps, done):
                raw = tmp.take()
                w0 = act(raw.mem[:, :, :], ps[:, :, :], ACT.Copy, done, raw.free)
                for j in range(2):
                    c = 2 * i + j
                    y = xbc[:, c, :]
                    w1 = act(y, ps[:, j, :], ACT.Identity, bias=v2(l, "conv_b", c), scale=v2(l, "conv_w", 3 * 24 + c))
                    w = [w0, w1]
                    for tap in (2, 1, 0):
                        s = 3 - tap
                        w = stt(y[:, s:S], raw.mem[:, j, 0:S - s], v2(l, "conv_w", tap * 24 + c), y[:, s:S],
                                ALU.mult, ALU.add, w)
                    last = w
                    xbc_ready[c] = act(y, y, ACT.Silu, last)
                raw.release(last)
                return w1

            def fill():
                yield from linear_tokens(w_in, [C2_V + 256 * i for i in range(4)], hid_kt, normed, v_sink)
                yield from linear(w_in, [C2_XBC + 256 * i for i in range(12)], hid_k, normed, xbc_sink)
                yield from linear(w_in, [C2_Z + 256 * i for i in range(8)], hid_k, normed, to(zbuf, z_ready, ACT.Silu))

            filler = fill()

            def select():
                for t in range(TT):
                    n = (t + 1) * P
                    acc = score[:, t, 0:n]
                    w = None
                    for j in range(4):
                        half, pair = j // 2, j % 2
                        r0 = 64 * half
                        ps = small_ps.take()
                        pe.wait(ps.free, iq_ready[pair], ik_ready)
                        for i in range(2):
                            done = mm(ps.mem[:, i, 0:n], iq[r0:r0 + 64, 2 * pair + i, t * P:(t + 1) * P],
                                      ik[r0:r0 + 64, 0:n], True, True)
                        r = tmp.take()
                        pos = act(r.mem[:, :, 0:n], ps.mem[:, :, 0:n], ACT.Relu, done, r.free)
                        ps.release(pos)
                        for i in range(2):
                            head = 4 * pair + 2 * i + half
                            weight = iw[:, t * IH + head:t * IH + head + 1]
                            if j == 0 and i == 0:
                                w = ts(ve, acc, r.mem[:, i, 0:n], weight, None, ALU.mult, None, pos, iw_ready)
                            else:
                                w = stt(acc, r.mem[:, i, 0:n], weight, acc, ALU.mult, ALU.add, pos, w)
                        r.release(w)
                        if j % 2:
                            yield
                    w = ts(ve, acc, acc, IDX_SCALE, 0.0, ALU.mult, ALU.add, w)

                    def causal(ap, w, t=t, n=n):
                        return po.do(lambda e: e.affine_select(
                            out=ap, in_=ap, pattern=[[-1, n]], compare_op=ALU.is_ge, fill=NOT_KEPT, base=t * P,
                            channel_multiplier=1), w)
                    w = causal(acc, w)
                    st = stat.take()
                    best = st.mem[:, 0:8]
                    for _ in range(KEEP // 8):
                        w = ve.do(lambda e, acc=acc, best=best: e.max(best, acc), w, st.free)
                        w = ve.do(lambda e, acc=acc, best=best: e.match_replace(acc, best, acc, TAKEN), w)
                    st.release(w)
                    kp = keep[:, t, 0:n]
                    w = ts(ve, kp, acc, TAKEN, -NOT_KEPT, ALU.is_equal, ALU.mult, w)
                    w = ts(ve, kp, kp, NOT_KEPT, None, ALU.add, None, w)
                    keep_ready.append(causal(kp, w))
                    yield

            keep_ready = []
            weave(select(), filler)

            def scores2(h, out):
                j, r0 = h // 2, 64 * (h % 2)
                pe.wait(q_ready[j // 2], k_ready[j // 2], v_ready)
                ve.wait(keep_ready)
                for t in range(TT):
                    n = (t + 1) * P
                    done = mm(out[:, t, 0:n], q2[r0:r0 + 64, j, t * P:(t + 1) * P], k2[r0:r0 + 64, j, 0:n], True, True)
                return done

            o_ready = []
            while len(v_ready) < 4:
                next(filler)
            weave(attend(AH, scores2, [P, S], HD ** -0.5, keep, lambda h, kt: v2t[:, kt, h * 64:(h + 1) * 64],
                         lambda j: q2[:, j, :], None, o_ready), filler, every=2)
            run(filler)
            attention_read = (pe.sem, pe.count)

            slot, view, landed = load_weights(w_in[:, C2_DT:C2_GA], DT, SH)
            ps = small_ps.take()
            pe.wait(landed, ps.free)
            for k in range(DT):
                done = mm(ps.mem[0:SH, 0, :], view[:, k, :], hid_k(k), k == 0, k == DT - 1)
            slot.release(done)
            u, dt_, cs, e_ = (dts[0:SH, j, :] for j in range(4))
            w = ts(ve, u, ps.mem[0:SH, 0, :], v2(l, "dt_bias", rows=SH), None, ALU.add, None, done)
            ps.release(w)
            w = ts(ve, e_, u, -1.0, None, ALU.mult, None, w)
            w = tt(ve, e_, e_, u, ALU.min, w)
            w = act(e_, e_, ACT.Exp, w)
            w = log1p(w, e_, (SH, S))
            dt_ready = stt(dt_, u, 0.0, e_, ALU.max, ALU.add, w)
            acol = small[0:SH, 64:65]
            wa = act(acol, v2(l, "a_log", rows=SH), ACT.Exp)
            w = ts(ve, u, dt_, acol, -1.0, ALU.mult, ALU.mult, dt_ready, wa)
            cs_ready = ve.do(lambda e: e.tensor_tensor_scan(cs, cn("ones_row", SH), u, 0.0, ALU.mult, ALU.add), w)
            ps = small_ps.take()
            pe.wait(ps.free, cs_ready)
            for t in range(TT):
                tr(ps.mem[:, 0, t * SH:(t + 1) * SH], cs[:, t * P:(t + 1) * P], ident[0:SH, 0:SH], mark=False)
                done = tr(ps.mem[:, 0, (2 + t) * SH:(3 + t) * SH], dt_[:, t * P:(t + 1) * P], ident[0:SH, 0:SH])
            ncs, dtT = small[:, 80:80 + 2 * SH], small[:, 80 + 2 * SH:80 + 4 * SH]
            ncs_ready = act(ncs, ps.mem[:, 0, 0:2 * SH], ACT.Copy, done, scale=-1.0)
            dtT_ready = act(dtT, ps.mem[:, 0, 2 * SH:4 * SH], ACT.Copy)
            ps.release(dtT_ready)

            cb_ready = []
            for g in range(SG):
                ps = small_ps.take()
                flat = ps.mem[:, :, :].rearrange("p a b -> p (a b)")
                b, c = xbc[:, 16 + g, :], xbc[:, 20 + g, :]
                pe.wait(ps.free, xbc_ready[16 + g], xbc_ready[20 + g])
                mm(flat[:, 0:S], b[:, 0:P], c, True, True)
                done = mm(flat[:, S:S + P], b[:, P:S], c[:, P:S], True, True)
                w = tt(ve, cbm[:, g, :], flat[:, 0:384], cn("tri"), ALU.mult, done)
                ps.release(w)
                cb_ready.append(w)

            xtok_ready = []
            for j in range(8):
                ps = small_ps.take()
                pe.wait(ps.free)
                for t in range(TT):
                    for i in range(2):
                        turned = tr(ps.mem[:, t, i * P:(i + 1) * P], xbc[:, 2 * j + i, t * P:(t + 1) * P], ident,
                                    xbc_ready[2 * j + i])
                for t in range(TT):
                    w = tt(ve, xtok[:, t, j * 256:(j + 1) * 256].rearrange("p (h c) -> p h c", h=4),
                           ps.mem[:, t, :].rearrange("p (h c) -> p h c", h=4),
                           dtT[:, t * SH + 4 * j:t * SH + 4 * j + 4].unsqueeze(2).to_broadcast([P, 4, 64]),
                           ALU.mult, turned, dtT_ready, attention_read)
                ps.release(w)
                xtok_ready.append(w)

            z_done = []

            def ssd():
                live = {}
                for h in range(SH + 1):
                    if h < SH:
                        ps = small_ps.take()
                        done = mm(ps.mem[:, 0, :], ident[0:SH, h:h + 1].to_broadcast([SH, P]), cs, True, True, ps.free)
                        g = prob.take()
                        flat = g.mem[:, :, :].rearrange("p a b -> p (a b)")
                        ts(ve, flat[:, 0:S], ps.mem[:, 0, :], ncs[:, h:h + 1], 0.0, ALU.add, ALU.min, done, g.free,
                           ncs_ready)
                        w = ts(ve, flat[:, S:S + P], ps.mem[:, 0, P:S], ncs[:, SH + h:SH + h + 1], 0.0, ALU.add,
                               ALU.min)
                        ps.release(w)
                        w = act(flat[:, 0:384], flat[:, 0:384], ACT.Exp, w)
                        w = tt(po, flat[:, 0:384], flat[:, 0:384], cbm[:, h // 8, :], ALU.mult, w, cb_ready[h // 8])
                        live[h] = (g, flat, w)
                    if h >= 1:
                        hh = h - 1
                        g, flat, w = live.pop(hh)
                        r0 = 64 * (hh % 2)
                        if hh % 2 == 0:
                            live["y"] = small_ps.take()
                            pe.wait(live["y"].free)
                        y = live["y"]
                        pe.wait(w, xtok_ready[hh // 4])
                        mm(y.mem[r0:r0 + 64, 0, :], xtok[:, 0, hh * 64:hh * 64 + 64], flat[:, 0:S], True, False)
                        done = mm(y.mem[r0:r0 + 64, 0, P:S], xtok[:, 1, hh * 64:hh * 64 + 64], flat[:, S:S + P], False,
                                  True)
                        g.release(done)
                        if hh % 2:
                            j = hh // 2
                            xs = xbc[:, j, :]
                            w = stt(xs, xs, v2(l, "d_skip", j), y.mem[:, 0, :], ALU.mult, ALU.add, done)
                            y.release(w)
                            z_done.append(tt(po, zbuf[:, j, :], zbuf[:, j, :], xs, ALU.mult, w, z_ready[j // 2]))
                    yield
                    if h % 8 == 0 and h:
                        g = h // 8 - 1
                        r = tmp.take()
                        ac.wait(r.free)
                        w = mean_square([zbuf[:, 4 * g + j, :] for j in range(4)], z_done[4 * g:4 * g + 4], 512, ones,
                                        r.mem[:, 0, :])
                        for j in range(4 * g, 4 * g + 4):
                            w2 = stt(zbuf[:, j, :], zbuf[:, j, :], v2(l, "ssm_norm", j), r.mem[:, 0, :], ALU.mult,
                                     ALU.mult, w)
                            y_ready2.append(w2)
                        r.release(w2)
                        yield

            y_ready2 = []
            mixed = region(12544 + 16 * S, DT, S)
            gate_a, gate_m = region(18688 + 4 * 384, 4, S), None

            ga_ready = [None] * 4

            def ga_sink(i, ps, done):
                ga_ready[i] = act(mixed[:, 2 * i:2 * i + 2, :], ps[:, :, :], ACT.Sigmoid, done, cb_ready)
                return ga_ready[i]

            def oa_sink(i, ps, done):
                m = mixed[:, 2 * i:2 * i + 2, :]
                mix_ready[i] = tt(ve, m, ps[:, :, :], m, ALU.mult, done, ga_ready[i])
                return mix_ready[i]

            mix_ready = [None] * 4
            gm_ready = [None] * 4
            gmb = region(0, DT, S)

            def gm_sink(i, ps, done):
                gm_ready[i] = act(gmb[:, 2 * i:2 * i + 2, :], ps[:, :, :], ACT.Sigmoid, done, oa_read[0])
                return gm_ready[i]

            oa_read = [None]

            def fill():
                yield from linear(w_in, [C2_GA + 256 * i for i in range(4)], hid_k, normed, ga_sink)
                yield from linear(A["w_ao"][l], branch_cols, lambda k: q2[:, k, :], o_ready, oa_sink)
                oa_read[0] = (pe.sem, pe.count)
                yield from linear(w_in, [C2_GM + 256 * i for i in range(4)], hid_k, normed, gm_sink)

            filler = fill()
            weave(ssd(), filler, every=2)
            run(filler)

            def os_sink(i, ps, done):
                t = tmp.take()
                w = tt(ve, t.mem[:, :, :], ps[:, :, :], gmb[:, 2 * i:2 * i + 2, :], ALU.mult, done, gm_ready[i], t.free)
                m = mixed[:, 2 * i:2 * i + 2, :]
                mix_ready[i] = tt(po, m, m, t.mem[:, :, :], ALU.add, w, mix_ready[i])
                t.release(mix_ready[i])
                return w
            run(linear(A["w_so"][l], branch_cols, lambda k: zbuf[:, k, :], y_ready2, os_sink, kts=16))

            def residual_sink(half, out):
                def sink(i, ps, done):
                    for j in range(2):
                        t = 2 * i + j
                        w = stt(xres[:, t, :], ps[:, j, :], hgate(half, t), xres[:, t, :], ALU.mult, ALU.add, done)
                        out.append(w)
                    return w
                return sink
            x_ready = []
            run(linear(A["w_out2"][l], branch_cols, lambda k: mixed[:, k, :], [mix_ready[k // 2] for k in range(DT)],
                       residual_sink(0, x_ready)))

            hid_free = (pe.sem, pe.count)
            normed = norm_residual(x_ready, hscale(1), hshift(1), hid_free)
            f = region(0, 22, S)
            f_ready = [None] * 22
            held = {}

            def conv3(i, ps, done, base, dst_ap, free):
                raw = tmp.take()
                w0 = act(raw.mem[:, :, :], ps[:, :, :], ACT.Copy, done, raw.free)
                for j in range(2):
                    c = base + 2 * i + j
                    y = dst_ap[:, j, :]
                    w1 = act(y, ps[:, j, :], ACT.Identity, free, bias=v2(l, "fconv_b", c),
                             scale=v2(l, "fconv_w", 2 * 44 + c))
                    w = [w0, w1]
                    for tap in (1, 0):
                        s = 2 - tap
                        w = stt(y[:, s:S], raw.mem[:, j, 0:S - s], v2(l, "fconv_w", tap * 44 + c), y[:, s:S],
                                ALU.mult, ALU.add, w)
                raw.release(w)
                return w1, w

            def gate_half(i, ps, done):
                s = prob.take()
                read, w = conv3(i, ps, done, 22, s.mem, s.free)
                held[i] = (s, act(s.mem[:, :, :], s.mem[:, :, :], ACT.Silu, w))
                return read

            def val_half(i, ps, done):
                s, gated = held.pop(i)
                o = f[:, 2 * i:2 * i + 2, :]
                read, w = conv3(i, ps, done, 0, o, x_ready)
                w = tt(ve, o, o, s.mem[:, :, :], ALU.mult, w, gated)
                s.release(w)
                f_ready[2 * i] = f_ready[2 * i + 1] = w
                return read

            gs = linear(A["w_up2"][l], [D_FF + 256 * i for i in range(11)], hid_k, normed, gate_half)
            us = linear(A["w_up2"][l], [256 * i for i in range(11)], hid_k, normed, val_half)
            for _ in range(11):
                next(gs)
                next(us)
            hid_free = (pe.sem, pe.count)
            out = []
            run(linear(A["w_down2"][l], branch_cols, lambda k: f[:, k, :], f_ready, residual_sink(1, out), kts=22))
            x_ready = out

        stored = sem("stored")
        sp.wait(x_ready)
        sp.ops.append(lambda e: e.dma_start(A["out"].rearrange("p (t s) -> p t s", t=DT),
                                            xres[:, :, :]).then_inc(stored, 16))
        sp.ops.append(lambda e: e.wait_ge(stored, 16))

        with nc.Block() as block:
            @block.sync
            def _(e):
                sp.play(e)

            @block.tensor
            def _(e):
                pe.play(e)

            @block.scalar
            def _(e):
                ac.play(e)

            @block.vector
            def _(e):
                ve.play(e)

            @block.gpsimd
            def _(e):
                po.play(e)


WEIGHTS = {"w_in": "w_in", "w_uq": "mla_w_uq", "w_ukv": "mla_w_ukv", "w_o": "mla_w_o", "w_pw": "conv_w_pw",
           "w_ro": "ret_w_o", "w_out": "w_out", "w_gate": "ffn_w_gate", "w_up": "ffn_w_up",
           "w_down": "ffn_w_down", "w_ada": "w_ada_2", "w_in2": "w_in_2", "w_ao": "w_attn_o_2",
           "w_so": "w_ssm_o_2", "w_out2": "w_out_2", "w_up2": "w_up_2", "w_down2": "w_down_2"}


def columns(v):
    return np.ascontiguousarray(v.reshape(-1, P).T)


def rows_padded(v):
    out = np.zeros((P, 1), v.dtype)
    out[:v.shape[0], 0] = v
    return out


def kernel(**inputs):
    import concourse.bacc as bacc
    from concourse.bass_utils import run_bass_kernel_spmd

    a = {k: np.asarray(v) for k, v in inputs.items()}
    parts = []
    for l in range(DEPTH):
        parts += [columns(a[n][l]) for n in ("ln_mix_pre", "ln_mix_post", "ln_ffn_pre", "ln_ffn_post", "mla_q_norm",
                                             "mla_kv_norm", "conv_w_dw", "conv_b_dw", "conv_ln_g", "conv_ln_b",
                                             "ret_gn_g")]
        parts.append(np.tile(a["ret_decay_logits"][l].reshape(1, 2 * RET_H), (P, 1)))
    for l in range(DEPTH):
        parts += [columns(a[n][l]) for n in ("b_ada_2", "norm1_g_2", "norm2_g_2")]
        parts += [columns(np.tile(a[n][l], 2)) for n in ("q_norm_g_2", "k_norm_g_2")]
        parts += [columns(a[n][l]) for n in ("ssm_conv_w_2", "ssm_conv_b_2")]
        parts += [rows_padded(a["dt_bias_2"][l]), rows_padded(a["a_log_2"][l])]
        parts += [columns(np.repeat(a["d_skip_2"][l], 64)), columns(a["ssm_norm_g_2"][l]),
                  columns(a["ffn_conv_w_2"][l]), columns(a["ffn_conv_b_2"][l])]
    host = {
        "consts": constants(),
        "vectors": np.ascontiguousarray(np.concatenate(parts, 1)),
        "x": np.ascontiguousarray(a["x"][0].T.reshape(DT, P, S).transpose(1, 0, 2).reshape(P, DT * S)),
        "positions": np.ascontiguousarray(
            np.tile(np.concatenate([a["positions"], a["positions_2"]], 1), (P, 1))),
        "c": columns(a["c_2"][0]),
    }
    for name, source in WEIGHTS.items():
        host[name] = np.ascontiguousarray(a[source])

    nc = bacc.Bacc("TRN2", target_bir_lowering=False, num_devices=1)
    A = {n: nc.dram_tensor(f"in_{n}", v.shape, mybir.dt.from_np(v.dtype), kind="ExternalInput").ap()
         for n, v in host.items()}
    A["out"] = nc.dram_tensor("out_x", (P, DT * S), F32, kind="ExternalOutput").ap()
    build(nc, A)
    r = run_bass_kernel_spmd(nc, [{f"in_{n}": v for n, v in host.items()}], core_ids=[0])
    y = r.results[0]["out_x"].reshape(P, DT, S).transpose(2, 1, 0).reshape(1, S, D)
    return np.ascontiguousarray(y)
```

```python
from contextlib import ExitStack

import numpy as np

import concourse.bass as bass
from concourse import mybir

F32 = mybir.dt.float32
I32 = mybir.dt.int32
F32R = mybir.dt.float32r
ALU = mybir.AluOpType
ACT = mybir.ActivationFunctionType
AX = mybir.AxisListType

P = 128
D = 1024
S = 256
DEPTH = 2
DT = D // P
TT = S // P
EPS = 1e-6

HEADS, NOPE, ROPE, VDIM = 8, 64, 32, 64
QK = NOPE + ROPE
Q_RANK, KV_RANK = 256, 128
CONV_CH, CONV_W = 512, 31
RET_H, RET_DK, RET_DV = 4, 128, 256
FFN = 2816
IN1 = [Q_RANK, KV_RANK, ROPE, 2 * CONV_CH, RET_H * RET_DK, RET_H * RET_DK, RET_H * RET_DV,
       RET_H * RET_DV, 3 * D]
(C_Q, C_KV, C_PE, C_CONV, C_RQ, C_RK, C_RV, C_RG, C_GATE, _E1) = [int(v) for v in np.cumsum([0] + IN1)]

AH, HD = 16, 64
IH, ID = 8, 64
IDX_SCALE = (IH ** -0.5) * (ID ** -0.5)
KEEP = 64
D_IN = 2 * D
SH = D_IN // 64
SG = 4
NST = 128
XBC = D_IN + 2 * SG * NST
D_FF = 2816
IN2 = [D, D, D, IH * ID, ID, IH, D_IN, XBC, SH, D, D]
(C2_Q, C2_K, C2_V, C2_IQ, C2_IK, C2_IW, C2_Z, C2_XBC, C2_DT, C2_GA, C2_GM, _E2) = [
    int(v) for v in np.cumsum([0] + IN2)]

NOT_KEPT = -1.0e30
TAKEN = -3.0e38
TWO_PI = 2 * np.pi
PI_1 = 6.28125
PI_2 = float(np.float32(round((TWO_PI - PI_1) * 2 ** 20) / 2 ** 20))
PI_3 = float(np.float32(TWO_PI - PI_1 - PI_2))
ROUND_MAGIC = 1.5 * 2 ** 23
PI_F = 3.1415925


def offsets(sizes):
    at, out = 0, {}
    for name, n in sizes:
        out[name] = (at, at + n)
        at += n
    return out, at


VEC1, NVEC1 = offsets([("mix_pre", 8), ("mix_post", 8), ("ffn_pre", 8), ("ffn_post", 8), ("q_norm", 2),
                       ("kv_norm", 1), ("conv_w", CONV_W * 4), ("conv_b", 4), ("conv_g", 4),
                       ("conv_beta", 4), ("gn_g", 8), ("decay", 2 * RET_H)])
VEC2, NVEC2 = offsets([("b_ada", 48), ("norm1", 8), ("norm2", 8), ("qn", 1), ("kn", 1), ("conv_w", 4 * 24),
                       ("conv_b", 24), ("dt_bias", 1), ("a_log", 1), ("d_skip", 16), ("ssm_norm", 16),
                       ("fconv_w", 3 * 44), ("fconv_b", 44)])
CON, NCON = offsets([("ident", P), ("ones", P), ("ones64", P), ("rot96", QK), ("rot128", P), ("rot64", P),
                     ("dup", P), ("rotdup", P), ("to_row", 64), ("ahead", TT * S), ("behind", TT * S), ("tri", 384),
                     ("freq", 3), ("eps", 1)])

KC = 4
UNIT = KC * 256
RAW, SPLIT = 5, 4
AHEAD = SPLIT - 1
POOL_EVERY = 4
ARENA = 24 * 1024


def rotation(n, dim):
    m = np.zeros((n, n), np.float32)
    half = dim // 2
    for g in range(0, n, dim):
        for i in range(half):
            m[g + half + i, g + i] = -1.0
            m[g + i, g + half + i] = 1.0
    return m


def constants():
    c = np.zeros((P, NCON), np.float32)

    def put(name, v, r0=0):
        a, _ = CON[name]
        c[r0:r0 + v.shape[0], a:a + v.shape[1]] = v

    put("ident", np.eye(P, dtype=np.float32))
    put("ones", np.ones((P, P), np.float32))
    put("ones64", np.kron(np.eye(2, dtype=np.float32), np.ones((64, 64), np.float32)))
    r96 = np.zeros((QK, QK), np.float32)
    r96[NOPE:, NOPE:] = rotation(ROPE, ROPE)
    put("rot96", r96)
    put("rot128", rotation(P, RET_DK))
    put("rot64", rotation(P, HD))
    put("dup", np.tile(np.eye(64, dtype=np.float32), (1, 2)))
    to_row = np.zeros((P, 64), np.float32)
    to_row[:64, 31] = to_row[64:, 32] = 1.0
    put("to_row", to_row)
    put("rotdup", np.tile(rotation(64, 64), (1, 2)))
    m = (np.arange(P)[:, None] + P * np.arange(TT)[None, :])[:, :, None]
    diff = np.arange(S)[None, None, :] - m
    put("ahead", np.maximum(diff, 0).reshape(P, -1).astype(np.float32))
    put("behind", np.maximum(-diff, 0).reshape(P, -1).astype(np.float32))
    tri = (np.arange(P)[:, None] <= np.arange(P)[None, :]).astype(np.float32)
    put("tri", np.concatenate([tri, np.ones((P, P), np.float32), tri], 1))
    freq = np.zeros((P, 3), np.float32)

    def inv_freq(dim):
        k = np.arange(0, dim, 2, dtype=np.float32) / np.float32(dim)
        return k.astype(np.float64)

    for row in range(P):
        freq[row, 0] = np.float32(10000.0 ** -inv_freq(ROPE)[row % 16])
        freq[row, 1] = np.float32(10000.0 ** -inv_freq(RET_DK)[row % 64])
        freq[row, 2] = np.float32(1) / np.float32(10000.0 ** inv_freq(HD)[row % 32])
    put("freq", freq)
    put("eps", np.full((P, 1), EPS, np.float32))
    return c


def spreader():
    s = np.zeros((32, 16, P), np.float32)
    for t in range(16):
        s[2 * t, t, :64] = s[2 * t + 1, t, 64:] = 1.0
    return s.reshape(32, 16 * P)


class Queue:

    def __init__(self, sem):
        self.sem, self.count, self.ops, self.seen = sem, 0, [], {}

    def wait(self, *tokens):
        for t in tokens:
            if t is None:
                continue
            if isinstance(t, list):
                self.wait(*t)
                continue
            sem, value = t
            if self.seen.get(sem.name, 0) < value:
                self.seen[sem.name] = value
                self.ops.append(lambda e, sem=sem, value=value: e.wait_ge(sem, value))

    def do(self, fn, *tokens, mark=True):
        self.wait(*tokens)
        if not mark:
            self.ops.append(fn)
            return None
        self.count += 1
        sem = self.sem
        self.ops.append(lambda e: fn(e).then_inc(sem, 1))
        return (sem, self.count)

    def hole(self):
        place = []
        self.ops.append(place)
        return place

    def play(self, eng):
        for op in self.ops:
            if isinstance(op, list):
                for inner in op:
                    inner(eng)
            else:
                op(eng)


class Slot:

    def __init__(self, mem, ring=None):
        self.mem, self.ring, self.free, self.sem, self.loads = mem, ring, None, None, 0

    def release(self, token):
        self.free = token
        self.ring.idle.append(self)


class Ring:

    def __init__(self, mems):
        self.slots = [Slot(m, self) for m in mems]
        self.idle = list(self.slots)

    def take(self):
        return self.idle.pop(0)


def weave(main, *others):
    due = [0.0] * len(others)
    for _ in main:
        for i, (steps, rate) in enumerate(others):
            due[i] += rate
            while due[i] >= 1:
                due[i] -= 1
                next(steps, None)


def run(steps):
    for _ in steps:
        pass


def build(nc, A):
    with ExitStack() as ctx:
        def sb(name, shape, dt=F32):
            return ctx.enter_context(nc.sbuf_tensor(name, shape, dt))

        def sem(name):
            return ctx.enter_context(nc.semaphore(name))

        pe, ve, ac, po, sp = (Queue(sem(n)) for n in ("pe_done", "ve_done", "ac_done", "po_done", "sp_done"))

        con = sb("con", [P, NCON])
        vec = sb("vec", [P, DEPTH * (NVEC1 + NVEC2)])
        xres = sb("xres", [P, DT, S])
        rope_cs = sb("rope_cs", [P, 4, S])
        pos_i = sb("pos_i", [P, 2, S], I32)
        small = sb("small", [P, 80 + 4 * SH])
        mod = sb("mod", [P, DEPTH, 48])
        ccol = sb("ccol", [P, DT])
        cact = sb("cact", [P, DT])

        raws = Ring([sb(f"raw{i}", [P, UNIT]) for i in range(RAW)])
        for i, s in enumerate(raws.slots):
            s.sem = sem(f"raw_landed{i}")
        w_hi = [sb(f"w_hi{i}", [P, UNIT], F32R) for i in range(SPLIT)]
        w_lo = [sb(f"w_lo{i}", [P, UNIT], F32R) for i in range(SPLIT)]
        hi_done, lo_done = sem("hi_done"), [sem("lo_done_ve"), sem("lo_done_po")]
        lo_count = [0, 0]
        used = [None] * SPLIT
        side = Ring([sb(f"side{i}", [P, UNIT]) for i in range(2)])
        for i, s in enumerate(side.slots):
            s.sem = sem(f"side_landed{i}")
        tmp = Ring([sb(f"tmp{i}", [P, 2, S]) for i in range(6)])
        prob = Ring([sb(f"prob{i}", [P, 2, S]) for i in range(3)])
        probT = Ring([sb(f"probT{i}", [P, 2, S]) for i in range(2)])
        stat = Ring([sb(f"stat{i}", [P, 16]) for i in range(4)])
        fence = sb("arena_fence", [P, ARENA])
        at = nc.sbuf_base - ARENA * 4
        arena = nc.alloc_sbuf_tensor_at("arena", [P, ARENA], F32, offset=at)
        arena_r = nc.alloc_sbuf_tensor_at("arena_r", [P, ARENA], F32R, offset=at)

        def region(at, *shape, mem=None):
            n = int(np.prod(shape))
            assert at + n <= ARENA, (at, shape)
            v = (arena if mem is None else mem)[:, at:at + n]
            if len(shape) == 1:
                return v
            return v.rearrange("p (a b) -> p a b", a=shape[0])

        def parts(hi_at, lo_at, tiles):
            return region(hi_at, tiles, S, mem=arena_r), region(lo_at, tiles, S, mem=arena_r)

        banks = [ctx.enter_context(nc.psum_tensor(f"bank{i}", [P, 2, S], F32)) for i in range(8)]
        big = Ring(banks[0:3])
        small_ps = Ring(banks[3:8])

        def cn(name, rows=P, r0=0):
            a, b = CON[name]
            return con[r0:r0 + rows, a:b]

        ident, ones, eps = cn("ident"), cn("ones"), cn("eps")

        def mm(out, lhsT, rhs, start, stop, *tokens, mark=None, skip=False):
            return pe.do(lambda e: e.matmul(out, lhsT, rhs, start=start, stop=stop, skip_group_check=skip),
                         *tokens, mark=stop if mark is None else mark)

        def tr(out, in_, idn, *tokens, mark=True):
            return pe.do(lambda e: e.transpose(out, in_, idn), *tokens, mark=mark)

        def act(out, in_, fn, *tokens, bias=0.0, scale=1.0, acc=None, mark=True):
            if fn == ACT.Copy:
                return ac.do(lambda e: e.activation(out, in_, fn, scale=scale), *tokens, mark=mark)
            if acc is None:
                return ac.do(lambda e: e.activation(out, in_, fn, bias=bias, scale=scale), *tokens, mark=mark)
            return ac.do(lambda e: e.activation(out, in_, fn, bias=bias, scale=scale, accum_out=acc),
                         *tokens, mark=mark)

        def ts(q, out, in0, s1, s2, op0, op1, *tokens, mark=True):
            if s2 is None:
                return q.do(lambda e: e.tensor_scalar(out, in0, s1, None, op0), *tokens, mark=mark)
            return q.do(lambda e: e.tensor_scalar(out, in0, s1, s2, op0, op1), *tokens, mark=mark)

        def tt(q, out, a, b, op, *tokens, mark=True):
            return q.do(lambda e: e.tensor_tensor(out, a, b, op), *tokens, mark=mark)

        def stt(out, in0, s, in1, op0, op1, *tokens, mark=True):
            return ve.do(lambda e: e.scalar_tensor_tensor(out, in0, s, in1, op0, op1), *tokens, mark=mark)

        def recip(out, in_, *tokens):
            return ve.do(lambda e: e.reciprocal(out, in_), *tokens)

        def load(dst, src, s, *tokens):
            sp.wait(*tokens)
            s.loads += 1
            landed = s.sem
            sp.ops.append(lambda e: e.dma_start(dst, src).then_inc(landed, 16))
            return (landed, 16 * s.loads)

        def load_side(src, kts, width, ring):
            s = ring.take()
            view = s.mem[:, 0:kts * width].rearrange("p (t n) -> p t n", t=kts)
            po.wait(s.free)
            s.loads += 1
            landed = s.sem
            po.ops.append(lambda e: e.dma_start(view, src.rearrange("(t p) n -> p t n", p=P)).then_inc(landed, 16))
            return s, view, (landed, 16 * s.loads)

        holes = []

        def split_unit(src, kts, width):
            n = len(holes)
            holes.append((ac.hole(), ve.hole(), po.hole()))
            raw, words, i = raws.take(), kts * width, n % SPLIT
            landed = load(raw.mem[:, 0:words].rearrange("p (t n) -> p t n", t=kts),
                          src.rearrange("(t p) n -> p t n", p=P), raw, raw.free)
            hi, lo, w = w_hi[i][:, 0:words], w_lo[i][:, 0:words], raw.mem[:, 0:words]
            free = used[i]
            by_pool = n % POOL_EVERY == POOL_EVERY - 1
            lo_sem, lo_count[by_pool] = lo_done[by_pool], lo_count[by_pool] + 1
            places = holes[max(n - AHEAD, 0)]
            in_act, in_lo = places[0], places[2 if by_pool else 1]
            for place in (in_act, in_lo):
                place.append(lambda e: e.wait_ge(*landed))
                if free is not None:
                    place.append(lambda e: e.wait_ge(*free))
            in_act.append(lambda e: e.activation(hi, w, ACT.Copy).then_inc(hi_done, 1))
            in_lo.append(lambda e: e.wait_ge(hi_done, n + 1))
            in_lo.append(lambda e: e.tensor_tensor(lo, w, hi.bitcast(F32), ALU.subtract).then_inc(lo_sem, 1))
            split_done = (lo_sem, lo_count[by_pool])
            raw.release([(hi_done, n + 1), split_done])
            pe.wait(split_done)

            def view(m):
                return m[i][:, 0:words].rearrange("p (t n) -> p t n", t=kts)
            return i, view(w_hi), view(w_lo)

        def linear(w, cols, rhs, ready, sink, kts=DT, blocks=(0, P), width=256):
            for i, c in enumerate(cols):
                bank = big.take()
                pe.wait(bank.free)
                for k0 in range(0, kts, KC):
                    n = min(KC, kts - k0)
                    slot, hi, lo = split_unit(w[k0 * P:(k0 + n) * P, c:c + width], n, width)
                    for half, b in enumerate(blocks):
                        for k in range(n):
                            pe.wait(ready[k0 + k])
                            x_hi, x_lo = rhs(k0 + k)
                            out = bank.mem[:, half, :]
                            last = k0 + k == kts - 1
                            mm(out, hi[:, k, b:b + P], x_hi, k0 + k == 0 and half == 0, False, skip=True)
                            mm(out, hi[:, k, b:b + P], x_lo, False, False, skip=True)
                            done = mm(out, lo[:, k, b:b + P], x_hi, False, last, skip=True,
                                      mark=k == n - 1 and half == len(blocks) - 1)
                    used[slot] = done
                bank.release(sink(i, bank.mem, done))
                yield

        def linear_tokens(w, cols, lhs, ready, sink):
            for i, c in enumerate(cols):
                bank = big.take()
                pe.wait(bank.free)
                for k0 in range(0, DT, KC):
                    slot, hi, lo = split_unit(w[k0 * P:(k0 + KC) * P, c:c + 256], KC, 256)
                    for t in range(TT):
                        for k in range(KC):
                            pe.wait(ready[k0 + k])
                            x_hi, x_lo = lhs(k0 + k, t)
                            out = bank.mem[:, t, :]
                            mm(out, x_hi, hi[:, k, :], k0 + k == 0 and t == 0, False, skip=True)
                            mm(out, x_lo, hi[:, k, :], False, False, skip=True)
                            done = mm(out, x_hi, lo[:, k, :], False, k0 + k == DT - 1, skip=True,
                                      mark=k == KC - 1 and t == 1)
                    used[slot] = done
                bank.release(sink(i, bank.mem, done))
                yield

        def split(q, src, hi, lo, *tokens):
            a = act(hi, src, ACT.Copy, *tokens)
            return [a, tt(q, lo, src, hi.bitcast(F32), ALU.subtract, a)]

        first_loads = Slot(None)
        first_loads.sem = sem("small_landed")
        load(con[:, :], A["consts"], first_loads)
        load(vec[:, :], A["vectors"], first_loads)
        load(xres[:, :, :], A["x"].rearrange("p (t s) -> p t s", t=DT), first_loads)
        load(pos_i[:, :, :], A["positions"].rearrange("p (t s) -> p t s", t=2), first_loads)
        inputs = load(ccol[:, :], A["c"], first_loads)
        for q in (pe, ve, ac, po):
            q.wait(inputs)

        def v1(l, name, j=0, n=1, rows=P, r0=0):
            a = l * NVEC1 + VEC1[name][0] + j
            return vec[r0:r0 + rows, a:a + n]

        def v2(l, name, j=0, n=1, rows=P, r0=0):
            a = DEPTH * NVEC1 + l * NVEC2 + VEC2[name][0] + j
            return vec[r0:r0 + rows, a:a + n]

        def rotary(k, which, j):
            cos, sin = rope_cs[:, 2 * j, :], rope_cs[:, 2 * j + 1, :]
            t1, t2, t3 = tmp.take(), tmp.take(), tmp.take()
            ang, n, r = t1.mem[:, 0, :], t2.mem[:, 0, :], t3.mem[:, 0, :]
            w = ve.do(lambda e, o=ang, i=pos_i[:, which, :]: e.tensor_copy(o, i), t1.free, t2.free, t3.free)
            f = cn("freq")[:, k:k + 1]
            w = ts(ve, ang, ang, f, None, ALU.mult, None, w)
            w = ts(ve, n, ang, float(1 / TWO_PI), ROUND_MAGIC, ALU.mult, ALU.add, w)
            w = ts(ve, n, n, ROUND_MAGIC, None, ALU.subtract, None, w)
            w = stt(r, n, -PI_1, ang, ALU.mult, ALU.add, w)
            w = stt(r, n, -PI_2, r, ALU.mult, ALU.add, w)
            w = stt(r, n, -PI_3, r, ALU.mult, ALU.add, w)
            w = ts(ve, r, r, PI_F, -PI_F, ALU.min, ALU.max, w)
            wa = act(sin, r, ACT.Sin, w)
            wb = act(cos, r, ACT.Sin, w, scale=0.5)
            w = tt(ve, cos, cos, cos, ALU.mult, wb)
            w = ts(ve, cos, cos, -2.0, 1.0, ALU.mult, ALU.add, w)
            for t in (t1, t2, t3):
                t.release([w, wa])
            return [w, wa]
        tables = [rotary(0, 0, 0), rotary(1, 0, 1)]

        def both(ap):
            return ap.unsqueeze(1).to_broadcast([ap.shape[0], 2, S])

        def mean_square(tiles, ready, width, ones_m, out):
            ps = small_ps.take()
            pe.wait(ps.free)
            n = len(tiles)
            for i, t in enumerate(tiles):
                sq = tmp.take()
                squared = act(sq.mem[:, 0, :], t, ACT.Square, sq.free, ready[i]) if i % 2 else \
                    tt(ve, sq.mem[:, 0, :], t, t, ALU.mult, sq.free, ready[i])
                summed = mm(ps.mem[:, 0, :], ones_m, sq.mem[:, 0, :], i == 0, i == n - 1, squared, mark=True)
                sq.release(summed)
            return rstd(ps, ps.mem[:, 0, :], out, width, summed)

        def rstd(ps, sums, out, width, summed, rows=P):
            root = act(out, sums, ACT.Sqrt, summed, scale=1.0 / width, bias=eps[0:rows, :])
            ps.release(root)
            return recip(out, out, root)

        def norm_residual(ready, gain, shift, done_reading):
            r = tmp.take()
            ve.wait(r.free)
            ac.wait(r.free)
            rs = r.mem[:, 0, :]
            w = mean_square([xres[:, t, :] for t in range(DT)], ready, D, ones, rs)
            out = []
            for j in range(DT // 2):
                h = tmp.take()
                for t in (2 * j, 2 * j + 1):
                    o = h.mem[:, t % 2, :]
                    last = stt(o, xres[:, t, :], gain(t), rs, ALU.mult, ALU.mult, w, h.free)
                    if shift is not None:
                        last = ts(ve, o, o, shift(t), None, ALU.add, None, last)
                pair = slice(2 * j, 2 * j + 2)
                parts_done = split(po if j % 2 else ve, h.mem[:, :, :], hid[0][:, pair, :], hid[1][:, pair, :], last,
                                   done_reading)
                h.release(parts_done)
                out.extend([parts_done, parts_done])
            r.release(last)
            return out

        hid = parts(0, 2048, DT)

        def of(pair):
            return lambda k: (pair[0][:, k, :], pair[1][:, k, :])

        hid_k = of(hid)

        def hid_kt(k, t):
            return tuple(part[:, k, t * P:(t + 1) * P] for part in hid)

        def log1p(e, u, shape):
            z, z2, acc = (tmp.take() for _ in range(3))
            zz, zz2, aa = (t.mem[0:shape[0], 0, 0:shape[1]] for t in (z, z2, acc))
            w = ts(ve, zz, u, 2.0, None, ALU.add, None, e, z.free, z2.free, acc.free)
            w = recip(zz, zz, w)
            w = tt(ve, zz, zz, u, ALU.mult, w)
            w = tt(ve, zz2, zz, zz, ALU.mult, w)
            w = ts(ve, aa, zz2, 2.0 / 17, 2.0 / 15, ALU.mult, ALU.add, w)
            for d in (13, 11, 9, 7, 5, 3, 1):
                w = tt(ve, aa, aa, zz2, ALU.mult, w)
                w = ts(ve, aa, aa, 2.0 / d, None, ALU.add, None, w)
            w = tt(ve, u, aa, zz, ALU.mult, w)
            for t in (z, z2, acc):
                t.release(w)
            return w

        def rotate(x, n_rows, r0, rot, table, ready, out=None, rows_out=None):
            cos = rope_cs[r0:r0 + n_rows, 2 * table, :]
            sin = rope_cs[r0:r0 + n_rows, 2 * table + 1, :]
            ps = small_ps.take()
            turned = mm(ps.mem[r0:r0 + n_rows, :, :], rot, x, True, True, ps.free, ready)
            a = tmp.take()
            am = a.mem[r0:r0 + n_rows, :, :]
            w1 = tt(ve, am, ps.mem[r0:r0 + n_rows, :, :], both(sin), ALU.mult, turned, a.free, tables)
            ps.release(w1)
            w2 = tt(po if n_rows == P else ve, x, x, both(cos), ALU.mult, turned, ready, tables)
            w3 = tt(ve, x, x, am, ALU.add, w1, w2)
            a.release(w3)
            return w3

        silu_c = act(cact[:, :], ccol[:, :], ACT.Silu, inputs)
        spread_loads = Slot(None)
        spread_loads.sem = sem("spread_landed")
        mod_ready = [None] * DEPTH
        mod_ring = Ring([region(17408 + UNIT * i, UNIT) for i in range(6)])
        for i, s in enumerate(mod_ring.slots):
            s.sem = sem(f"mod_landed{i}")

        def modulation(l, ring_free):
            w = A["w_ada"][l]
            po.wait(ring_free)

            def ask(b):
                return [load_side(w[k0 * P:(k0 + 2) * P, b * 512:b * 512 + 512], 2, 512, mod_ring)
                        for k0 in range(0, DT, 2)]

            asked = ask(0)
            late = []
            for b in range(12):
                if b % 6 == 0:
                    bank = small_ps.take()
                    flat = bank.mem[:, 0, :]
                sums = tmp.take()
                acc = sums.mem[:, :, :].rearrange("p a b -> p (a b)")
                done = None
                more = list(range(0, DT, 2)) if b < 11 else []
                for k0 in range(0, DT, 2):
                    slot, view, landed = asked.pop(0)
                    for k in range(2):
                        weight = cact[:, k0 + k:k0 + k + 1]
                        if done is None:
                            done = ts(ve, acc, view[:, k, :], weight, None, ALU.mult, None, landed, silu_c,
                                      sums.free)
                        else:
                            done = stt(acc, view[:, k, :], weight, acc, ALU.mult, ALU.add, landed, done)
                    slot.release(done)
                    if more:
                        asked.append(load_side(w[k0 * P:(k0 + 2) * P, (b + 1) * 512:(b + 2) * 512], 2, 512, mod_ring))
                    if late:
                        late.pop()()
                    yield

                def add_rows(b=b, bank=bank, flat=flat, sums=sums, acc=acc, done=done):
                    for j in range(4):
                        at = 4 * (b % 6) + j
                        turned = mm(flat[:, at:at + 1], acc[:, j * P:(j + 1) * P], ones[:, 0:1], True, True, done,
                                    bank.free)
                    sums.release(turned)
                    if b % 6 == 5:
                        half = b // 6
                        o = mod[:, l, half * 24:half * 24 + 24]
                        w1 = tt(ve, o, flat[:, 0:24], v2(l, "b_ada", half * 24, 24), ALU.add, turned)
                        bank.release(w1)
                        scale = mod[:, l, half * 24 + 8:half * 24 + 16]
                        mod_ready[l] = stt(scale, scale, 1.0, v2(l, "norm2" if half else "norm1", 0, 8), ALU.add,
                                           ALU.mult, w1)
                late.append(add_rows)
            yield
            late.pop()()

        def softmax_rows(ps, done, nk, scale, mask, tag):
            st = stat.take()
            p = prob.take()
            mx, nm, sm, rs = (st.mem[:, 2 * j:2 * j + 2] for j in range(4))
            if mask is None:
                w = ve.do(lambda e: e.tensor_reduce(mx, ps.mem[:, :, :], AX.X, ALU.max), done, st.free)
                src = ps.mem
            else:
                src = p.mem
                for t in range(TT):
                    n = nk[t]
                    w = ve.do(lambda e, t=t, n=n: e.tensor_tensor_reduce(
                        out=p.mem[:, t, 0:n], in0=ps.mem[:, t, 0:n], in1=mask[:, t, 0:n], scale=1.0,
                        scalar=-3.0e38, op0=ALU.add, op1=ALU.max, accum_out=mx[:, t:t + 1]),
                        done, st.free, p.free)
                ps.release(w)
            w = ts(ve, nm, mx, -scale, None, ALU.mult, None, w)
            for t in range(TT):
                n = nk[t]
                w2 = act(p.mem[:, t, 0:n], src[:, t, 0:n], ACT.Exp, w, p.free, bias=nm[:, t:t + 1], scale=scale,
                         acc=sm[:, t:t + 1])
            if mask is None:
                ps.release(w2)
            w = recip(rs, sm, w2)
            for t in range(TT):
                n = nk[t]
                w3 = ts(po, p.mem[:, t, 0:n], p.mem[:, t, 0:n], rs[:, t:t + 1], None, ALU.mult, None, w, w2)
            st.release([w3, w2])
            return p, w3

        def attend(heads, scores, nk, scale, mask, v_of, out_of, out_free, result):
            live = {}
            pair = {}
            for i in range(heads + 2):
                if i < heads:
                    ps = small_ps.take()
                    pe.wait(ps.free)
                    done = scores(i, ps.mem)
                    live[i] = softmax_rows(ps, done, nk, scale, mask, i)
                    yield
                if 1 <= i <= heads:
                    p, normed = live.pop(i - 1)
                    ps = small_ps.take()
                    pe.wait(ps.free, normed)
                    for kt in range(TT):
                        for t in range(TT):
                            if kt * P >= nk[t]:
                                continue
                            turned = tr(ps.mem[:, kt, t * P:(t + 1) * P], p.mem[:, t, kt * P:(kt + 1) * P], ident,
                                        mark=kt == 1 and t == 1)
                    p.release(turned)
                    pt = probT.take()
                    if nk[0] == S:
                        w = act(pt.mem[:, :, :], ps.mem[:, :, :], ACT.Copy, turned, pt.free)
                    else:
                        act(pt.mem[:, 0, :], ps.mem[:, 0, :], ACT.Copy, turned, pt.free)
                        w = act(pt.mem[:, 1, P:S], ps.mem[:, 1, P:S], ACT.Copy)
                    ps.release(w)
                    live[("t", i - 1)] = (pt, w)
                if 2 <= i:
                    h = i - 2
                    pt, w = live.pop(("t", h))
                    r0 = 64 * (h % 2)
                    if h % 2 == 0:
                        pair["o"] = small_ps.take()
                        pe.wait(pair["o"].free)
                    o = pair["o"]
                    q0 = 0 if nk[0] == S else P
                    mm(o.mem[r0:r0 + 64, 0, :], v_of(h, 0), pt.mem[:, 0, :], True, False, w)
                    done = mm(o.mem[r0:r0 + 64, 0, q0:S], v_of(h, 1), pt.mem[:, 1, q0:S], False, True)
                    pt.release(done)
                    if h % 2:
                        w = split(ve, o.mem[:, 0, :], *out_of(h // 2), done, out_free)
                        o.release(w)
                        result.append(w)
                    yield

        x_ready = [inputs] * DT
        hid_free = None

        def add_normed(y, y_ready, gain, x_tok):
            r = tmp.take()
            ve.wait(r.free)
            ac.wait(r.free)
            rs = r.mem[:, 0, :]
            w = mean_square([y[:, t, :] for t in range(DT)], y_ready, D, ones, rs)
            out = []
            for t in range(DT):
                w2 = stt(y[:, t, :], y[:, t, :], gain(t), rs, ALU.mult, ALU.mult, w)
                out.append(tt(po, xres[:, t, :], xres[:, t, :], y[:, t, :], ALU.add, w2, x_tok))
            r.release(w2)
            return out

        for l in range(DEPTH):
            w_in = A["w_in"][l]
            qm, km = region(4096, HEADS, S), region(6144, HEADS, S)
            gate = [region(4096, DT, S), region(6144, DT, S)]
            cq, ckv, vmla = region(8192, 2, S), region(8704, S), region(8960, TT, 512)
            gbuf = region(10240, DT, S)
            ret_p = parts(8192, 10240, DT)
            omla_p = parts(12288, 13312, 4)
            conv_a, conv_g, conv_y = region(14336, 4, S), region(15360, 4, S), region(16384, 4, S)
            conv_p = parts(14336, 15360, 4)
            rq, rk = region(17408, RET_H, S), region(18432, RET_H, S)
            vret = region(19456, TT, RET_H * RET_DV)
            merged = region(21504, DT, S)

            normed = norm_residual(x_ready, lambda t: v1(l, "mix_pre", t), None, hid_free)

            gate_ready = [[None] * 4 for _ in range(3)]

            def gate_sink(branch):
                def sink(i, ps, done):
                    g = gate[branch % 2]
                    gate_ready[branch][i] = act(g[:, 2 * i:2 * i + 2, :], ps[:, :, :], ACT.Sigmoid, done,
                                                gate_free[branch])
                    return gate_ready[branch][i]
                return sink

            gate_free = [None, None, None]
            conv_in = [None] * 4

            def conv_gate_sink(i, ps, done):
                conv_in[i] = act(conv_g[:, 2 * i:2 * i + 2, :], ps[:, :, :], ACT.Sigmoid, done)
                return conv_in[i]

            conv_ready = [None] * 4

            def conv_a_sink(i, ps, done):
                w = tt(ve, conv_a[:, 2 * i:2 * i + 2, :], ps[:, :, :], conv_g[:, 2 * i:2 * i + 2, :], ALU.mult,
                       done, conv_in[i])
                conv_ready[2 * i] = conv_ready[2 * i + 1] = w
                return w

            def to(dst, out, copy=ACT.Copy):
                def sink(i, ps, done):
                    w = act(dst[:, 2 * i:2 * i + 2, :], ps[:, :, :], copy, done)
                    out.append(w)
                    return w
                return sink

            rq_raw, rk_raw, rg_ready, vret_ready = [], [], [], []

            def vret_sink(i, ps, done):
                w = act(vret[:, :, i * 256:(i + 1) * 256], ps[:, :, :], ACT.Copy, done)
                vret_ready.append(w)
                return w

            def fill():
                yield from linear(w_in, [C_CONV + CONV_CH, C_CONV + CONV_CH + 256], hid_k, normed, conv_gate_sink)
                yield from linear(w_in, [C_CONV, C_CONV + 256], hid_k, normed, conv_a_sink)
                yield from linear(w_in, [C_RQ, C_RQ + 256], hid_k, normed, to(rq, rq_raw))
                yield from linear(w_in, [C_RK, C_RK + 256], hid_k, normed, to(rk, rk_raw))
                yield from linear_tokens(w_in, [C_RV + 256 * i for i in range(4)], hid_kt, normed, vret_sink)
                yield from linear(w_in, [C_RG + 256 * i for i in range(4)], hid_k, normed, to(gbuf, rg_ready, ACT.Silu))

            filler = fill()
            def take_cq(i, ps, done):
                return act(cq[:, :, :], ps[:, :, :], ACT.Copy, done)
            run(linear(w_in, [C_Q], hid_k, normed, take_cq))
            cq_raw = (ac.sem, ac.count)

            kpe = tmp.take()

            def take_ckv(i, ps, done):
                act(ckv, ps[:, 0, :], ACT.Copy, done)
                return act(kpe.mem[64:96, 0, :], ps[64:96, 1, :], ACT.Copy, kpe.free)
            run(linear(w_in, [C_KV], hid_k, normed, take_ckv, blocks=(0, 64), width=192))
            ckv_raw = kpe_raw = (ac.sem, ac.count)

            r = tmp.take()
            ac.wait(r.free)
            w = mean_square([cq[:, t, :] for t in range(2)], [cq_raw] * 2, Q_RANK, ones, r.mem[:, 0, :])
            for t in range(2):
                cq_n = stt(cq[:, t, :], cq[:, t, :], v1(l, "q_norm", t), r.mem[:, 0, :], ALU.mult, ALU.mult, w)
            w = mean_square([ckv], [ckv_raw], KV_RANK, ones, r.mem[:, 1, :])
            ckv_n = stt(ckv, ckv, v1(l, "kv_norm"), r.mem[:, 1, :], ALU.mult, ALU.mult, w)
            r.release(ckv_n)

            next(filler)
            next(filler)
            rot96 = cn("rot96", ROPE, 64)[:, 64:96]
            ps = small_ps.take()
            turned = mm(ps.mem[64:96, 0, :], rot96, kpe.mem[64:96, 0, :], True, True, ps.free, kpe_raw)
            cos, sin = rope_cs[64:96, 0, :], rope_cs[64:96, 1, :]
            t1 = tmp.take()
            w1 = tt(ve, t1.mem[64:96, 0, :], ps.mem[64:96, 0, :], sin, ALU.mult, turned, t1.free, tables)
            ps.release(w1)
            w2 = tt(ve, t1.mem[64:96, 1, :], kpe.mem[64:96, 0, :], cos, ALU.mult, kpe_raw)
            w = tt(ve, t1.mem[64:96, 0, :], t1.mem[64:96, 0, :], t1.mem[64:96, 1, :], ALU.add, w1, w2)
            kpe_in = act(km[64:96, :, :], t1.mem[64:96, 0:1, :].to_broadcast([ROPE, HEADS, S]), ACT.Copy, w)
            kpe.release(kpe_in)
            t1.release(kpe_in)

            uq = [load_side(A["w_uq"][l][k * P:(k + 1) * P, :], 1, HEADS * QK, side) for k in range(2)]
            pe.wait(cq_n, uq[0][2], uq[1][2])
            q_ready = [None] * 4
            for j in range(4):
                ps = small_ps.take()
                pe.wait(ps.free)
                for i in range(2):
                    h = 2 * j + i
                    for k in range(2):
                        done = mm(ps.mem[0:QK, i, :], uq[k][1][:, 0, h * QK:(h + 1) * QK], cq[:, k, :], k == 0, k == 1)
                w = act(qm[0:QK, 2 * j:2 * j + 2, :], ps.mem[0:QK, :, :], ACT.Copy, done)
                ps.release(w)
                q_ready[j] = w
            for s in uq:
                s[0].release(done)
            next(filler)
            for j in range(4):
                q_ready[j] = rotate(qm[64:96, 2 * j:2 * j + 2, :], ROPE, 64, rot96, 0, q_ready[j])

            slot, view, landed = load_side(A["w_ukv"][l], 1, HEADS * (NOPE + VDIM), side)
            pe.wait(landed, ckv_n)
            k_ready = [None] * 4
            for j in range(4):
                ps = small_ps.take()
                pe.wait(ps.free)
                for i in range(2):
                    h = 2 * j + i
                    done = mm(ps.mem[0:NOPE, i, :], view[:, 0, h * P:h * P + NOPE], ckv, True, True)
                k_ready[j] = act(km[0:NOPE, 2 * j:2 * j + 2, :], ps.mem[0:NOPE, :, :], ACT.Copy, done)
                ps.release(k_ready[j])
            wv = view[:, 0, :].rearrange("p (h c) -> p h c", h=HEADS)[:, :, NOPE:]
            for t in range(TT):
                ps = small_ps.take()
                done = mm(ps.mem[:, :, :].rearrange("p a b -> p (a b)"), ckv[:, t * P:(t + 1) * P], wv, True, True,
                          ps.free)
                v_ready = act(vmla[:, t, :], ps.mem[:, :, :].rearrange("p a b -> p (a b)"), ACT.Copy, done)
                ps.release(v_ready)
            slot.release(done)

            def mla_scores(h, out):
                pe.wait(q_ready[h // 2], k_ready[h // 2], kpe_in, v_ready)
                for t in range(TT):
                    done = mm(out[:, t, :], qm[0:QK, h, t * P:(t + 1) * P], km[0:QK, h, :], True, True)
                return done

            o_ready = []
            mla = attend(HEADS, mla_scores, [S, S], QK ** -0.5, None,
                         lambda h, kt: vmla[:, kt, h * 64:(h + 1) * 64], lambda j: (omla_p[0][:, j, :], omla_p[1][:, j, :]), None, o_ready)

            def conv_steps():
                half = CONV_W // 2
                for t in range(4):
                    pe_free = conv_ready[t]
                    w = ts(ve, conv_y[:, t, :], conv_a[:, t, :], v1(l, "conv_w", half * 4 + t),
                           v1(l, "conv_b", t), ALU.mult, ALU.add, pe_free)
                    for j in range(CONV_W):
                        s = j - half
                        if s == 0:
                            continue
                        lo, hi = max(0, -s), min(S, S - s)
                        w = stt(conv_y[:, t, lo:hi], conv_a[:, t, lo + s:hi + s], v1(l, "conv_w", j * 4 + t),
                                conv_y[:, t, lo:hi], ALU.mult, ALU.add, w)
                        if j % 8 == 7:
                            yield
                    conv_done.append(w)
                    yield

            conv_done = []
            conv = conv_steps()
            weave(mla, (filler, 0.55), (conv, 0.3))
            qk_read = (pe.sem, pe.count)
            gate_free = [qk_read, qk_read, None]

            x = v1(l, "decay", 0, 8)
            lg = small[:, 0:8]
            e = small[:, 8:16]
            w = ve.do(lambda q, x=x: q.tensor_scalar(small[:, 16:24], x, -1.0, None, ALU.mult))
            w = tt(ve, small[:, 16:24], small[:, 16:24], x, ALU.min, w)
            w = act(e, small[:, 16:24], ACT.Exp, w)
            w = log1p(w, e, (P, 8))
            w = stt(lg, x, 0.0, e, ALU.min, ALU.subtract, w)
            lg_ready = w

            merged_ready = [None] * 4

            def first_branch(i, ps, done):
                w = tt(ve, merged[:, 2 * i:2 * i + 2, :], ps[:, :, :], gate[0][:, 2 * i:2 * i + 2, :], ALU.mult,
                       done, gate_ready[0][i])
                merged_ready[i] = w
                return w

            def next_branch(branch):
                def sink(i, ps, done):
                    t = tmp.take()
                    w = tt(ve, t.mem[:, :, :], ps[:, :, :], gate[branch % 2][:, 2 * i:2 * i + 2, :], ALU.mult,
                           done, gate_ready[branch][i], t.free)
                    m = merged[:, 2 * i:2 * i + 2, :]
                    merged_ready[i] = tt(po, m, m, t.mem[:, :, :], ALU.add, w, merged_ready[i])
                    t.release(merged_ready[i])
                    return w
                return sink

            branch_cols = [256 * i for i in range(4)]

            def conv_norm():
                ps = small_ps.take()
                for t in range(4):
                    w = mm(ps.mem[:, 0, :], ones, conv_y[:, t, :], t == 0, t == 3, ps.free, conv_done[t])
                mu = tmp.take()
                w = act(mu.mem[:, 0, :], ps.mem[:, 0, :], ACT.Copy, w, mu.free, scale=1.0 / CONV_CH)
                ps.release(w)
                centred = [tt(ve, conv_y[:, t, :], conv_y[:, t, :], mu.mem[:, 0, :], ALU.subtract, w)
                           for t in range(4)]
                yield
                w = mean_square([conv_y[:, t, :] for t in range(4)], centred, CONV_CH, ones, mu.mem[:, 1, :])
                for t in range(4):
                    w1 = stt(conv_y[:, t, :], conv_y[:, t, :], v1(l, "conv_g", t), mu.mem[:, 1, :], ALU.mult, ALU.mult,
                             w)
                    w2 = act(conv_y[:, t, :], conv_y[:, t, :], ACT.Silu, w1, bias=v1(l, "conv_beta", t))
                    conv_out.append(split(po, conv_y[:, t, :], conv_p[0][:, t, :], conv_p[1][:, t, :], w2))
                mu.release(w1)
                yield

            conv_out = []

            def fill2():
                yield from linear(w_in, [C_GATE + 256 * i for i in range(4)], hid_k, normed, gate_sink(0))
                yield from linear(w_in, [C_GATE + D + 256 * i for i in range(4)], hid_k, normed, gate_sink(1))
                yield from linear(A["w_o"][l], branch_cols, of(omla_p), o_ready, first_branch, kts=4)
                gate_free[2] = merged_ready[3]
                yield from linear(w_in, [C_GATE + 2 * D + 256 * i for i in range(4)], hid_k, normed, gate_sink(2))

            def both_fills(first, then):
                yield from first
                yield from then

            filler = both_fills(filler, fill2())

            def retention():
                qr = [rotate(rq[:, 2 * j:2 * j + 2, :], P, 0, cn("rot128"), 1, rq_raw[j]) for j in range(2)]
                kr = [rotate(rk[:, 2 * j:2 * j + 2, :], P, 0, cn("rot128"), 1, rk_raw[j]) for j in range(2)]
                yield
                o_norm = {}
                for h in range(RET_H + 1):
                    if h < RET_H:
                        dec = prob.take()
                        flat = dec.mem[:, :, :].rearrange("p a b -> p (a b)")
                        w = ts(ve, flat, cn("ahead"), lg[:, h:h + 1], None, ALU.mult, None, lg_ready, dec.free)
                        w = stt(flat, cn("behind"), lg[:, 4 + h:5 + h], flat, ALU.mult, ALU.add, w)
                        w_dec = act(flat, flat, ACT.Exp, w)
                        ps = small_ps.take()
                        pe.wait(ps.free, qr[h // 2], kr[h // 2])
                        for mt in range(TT):
                            done = mm(ps.mem[:, mt, :], rk[:, h, mt * P:(mt + 1) * P], rq[:, h, :], True, True)
                        w_dec = stt(dec.mem[:, :, :], ps.mem[:, :, :], RET_DK ** -0.5, dec.mem[:, :, :], ALU.mult,
                                    ALU.mult, done, w_dec)
                        ps.release(w_dec)
                        yield
                        o = small_ps.take()
                        pe.wait(o.free, w_dec, vret_ready)
                        for t in range(TT):
                            for mt in range(TT):
                                done = mm(o.mem[:, t, :], dec.mem[:, mt, t * P:(t + 1) * P],
                                          vret[:, mt, h * 256:(h + 1) * 256], mt == 0, mt == 1)
                        dec.release(done)
                        on, st = tmp.take(), stat.take()
                        for t in range(TT):
                            b = st.mem[:, 8 * t:8 * t + 6]
                            w = ve.do(lambda q, b=b, t=t, o=o: q.bn_stats(b, o.mem[:, t, :]), done, st.free)
                            mv = st.mem[:, 8 * t + 6:8 * t + 8]
                            w = ve.do(lambda q, b=b, mv=mv: q.bn_aggr(mv, b), w)
                            var = mv[:, 1:2]
                            w = act(var, var, ACT.Sqrt, w, bias=eps)
                            w = recip(var, var, w)
                            w = ts(ve, on.mem[:, t, :], o.mem[:, t, :], mv[:, 0:1], var, ALU.subtract, ALU.mult, w,
                                   on.free)
                        o.release(w)
                        st.release(w)
                        o_norm[h] = (on, w)
                        yield
                    if h >= 1:
                        on, w = o_norm.pop(h - 1)
                        ps = small_ps.take()
                        pe.wait(ps.free, w)
                        for half in range(2):
                            for t in range(TT):
                                turned = tr(ps.mem[:, half, t * P:(t + 1) * P], on.mem[:, t, half * P:(half + 1) * P],
                                            ident)
                        on.release(turned)
                        gated = tmp.take()
                        for half in range(2):
                            j = 2 * (h - 1) + half
                            w = stt(gated.mem[:, half, :], ps.mem[:, half, :], v1(l, "gn_g", j), gbuf[:, j, :], ALU.mult,
                                    ALU.mult, turned, rg_ready[j // 2], gated.free)
                        ps.release(w)
                        pair = slice(2 * (h - 1), 2 * h)
                        w = split(po, gated.mem[:, :, :], ret_p[0][:, pair, :], ret_p[1][:, pair, :], w)
                        gated.release(w)
                        ret_out[2 * (h - 1)] = ret_out[2 * h - 1] = w
                        yield

            ret_out = [None] * DT
            weave(retention(), (filler, 1.4), (conv, 1.2))
            weave(filler, (conv, 1.0))
            run(conv)
            weave(linear(A["w_ro"][l], branch_cols, of(ret_p), ret_out, next_branch(2)), (conv_norm(), 1.0))

            merged_in = []
            hid_read = (pe.sem, pe.count)

            def last_branch(i, ps, done):
                w = next_branch(1)(i, ps, done)
                pair = slice(2 * i, 2 * i + 2)
                m = split(ve, merged[:, pair, :], hid[0][:, pair, :], hid[1][:, pair, :], merged_ready[i], hid_read)
                merged_in.extend([m, m])
                return w
            run(linear(A["w_pw"][l], branch_cols, of(conv_p), conv_out, last_branch, kts=4))

            y_ready = []
            y = gate[0]
            def y_sink(dst, out):
                def sink(i, ps, done):
                    w = act(dst[:, 2 * i:2 * i + 2, :], ps[:, :, :], ACT.Copy, done, merged_ready)
                    out.extend([w, w])
                    return w
                return sink
            run(linear(A["w_out"][l], branch_cols, hid_k, merged_in, y_sink(y, y_ready)))
            x_ready = add_normed(y, y_ready, lambda t: v1(l, "mix_post", t), x_ready)

            hid_free = (pe.sem, pe.count)
            normed = norm_residual(x_ready, lambda t: v1(l, "ffn_pre", t), None, hid_free)
            f_p = parts(4096, 4096 + 22 * S, 22)
            f_ready = [None] * (FFN // P)
            held = {}

            def gate_half(i, ps, done):
                s = tmp.take()
                w = act(s.mem[:, :, :], ps[:, :, :], ACT.Silu, done, s.free)
                held[i] = (s, w)
                return w

            def up_half(i, ps, done):
                s, w = held.pop(i)
                w2 = tt(ve, s.mem[:, :, :], ps[:, :, :], s.mem[:, :, :], ALU.mult, done, w)
                pair = slice(2 * i, 2 * i + 2)
                w3 = split(po, s.mem[:, :, :], f_p[0][:, pair, :], f_p[1][:, pair, :], w2, x_ready)
                s.release(w3)
                f_ready[2 * i] = f_ready[2 * i + 1] = w3
                return w2

            gs = linear(A["w_gate"][l], [256 * i for i in range(11)], hid_k, normed, gate_half)
            us = linear(A["w_up"][l], [256 * i for i in range(11)], hid_k, normed, up_half)
            mod_steps = modulation(l, x_ready)

            def gate_and_up():
                for _ in range(11):
                    next(gs)
                    yield
                    next(us)
                    yield
            weave(gate_and_up(), (mod_steps, 1.7))
            hid_free = (pe.sem, pe.count)
            y = region(15360, DT, S)
            y_ready = []
            weave(linear(A["w_down"][l], branch_cols, of(f_p), f_ready, y_sink(y, y_ready), kts=22),
                  (mod_steps, 3.0))
            run(mod_steps)
            x_ready = add_normed(y, y_ready, lambda t: v1(l, "ffn_post", t), x_ready)

        for l in range(DEPTH):
            w_in = A["w_in2"][l]
            q2, k2, v2t = region(4096, DT, S), region(6144, DT, S), region(8192, TT, D)
            iq, ik = region(10240, 4, S), region(11264, S)
            score = region(11520, TT, S)
            keep = region(12288, TT, S)
            xbc = region(12800, 24, S)
            zbuf = region(18944, 16, S)
            cbm = region(23040, SG, 384)
            o_p = parts(4096, 10240, DT)
            xtok = region(6144, TT, D_IN)
            dts = region(12288, 2, S)
            y_p = parts(18944, 12800, 16)
            mixed = region(16896, DT, S)
            gmb = region(4096, DT, S)

            def hshift(half):
                return lambda t: mod[:, l, half * 24 + t:half * 24 + t + 1]

            def hscale(half):
                return lambda t: mod[:, l, half * 24 + 8 + t:half * 24 + 9 + t]

            def hgate(half, t):
                return mod[:, l, half * 24 + 16 + t:half * 24 + 17 + t]

            ve.wait(mod_ready[l])
            if l == 0:
                ac.wait(x_ready)
                ve.wait(x_ready)
                tables = [rotary(2, 1, 0)]
            hid_free = (pe.sem, pe.count)
            normed = norm_residual(x_ready, hscale(0), hshift(0), hid_free)
            arena_free = x_ready

            spread = region(18944, 16, P)
            po.wait(x_ready)
            spread_loads.loads += 1
            po.ops.append(lambda e, o=spread: e.dma_start(
                o[0:32, :, :], A["spread"].rearrange("k (t m) -> k t m", t=16)).then_inc(spread_loads.sem, 16))
            spread_landed = (spread_loads.sem, 16 * spread_loads.loads)

            heads_ps = small_ps.take()
            pe.wait(heads_ps.free)
            squares, qk_raw = [], []

            def qk_sink(dst):
                def sink(i, ps, done):
                    x = dst[:, 2 * i:2 * i + 2, :]
                    raw = act(x, ps[:, :, :], ACT.Copy, done, arena_free)
                    sq = tmp.take()
                    squares.append((sq, tt(po, sq.mem[:, :, :], x, x, ALU.mult, raw, sq.free)))
                    qk_raw.append(raw)
                    return raw
                return sink

            def sum_squares():
                n = summed[0]
                sq, w = squares.pop(0)
                for i in range(2):
                    a = 31 - 2 * (2 * n + i)
                    done = mm(heads_ps.mem[0:32, 0, :], cn("to_row")[:, a:a + 32], sq.mem[:, i, :], n == 0 and i == 0,
                              n == 7 and i == 1, w, mark=i == 1)
                sq.release(done)
                summed[0] += 1
                return done

            summed = [0]
            for st in (linear(w_in, [C2_Q + 256 * i for i in range(4)], hid_k, normed, qk_sink(q2)),
                       linear(w_in, [C2_K + 256 * i for i in range(4)], hid_k, normed, qk_sink(k2))):
                for _ in st:
                    if len(squares) > 1:
                        sum_squares()
            iq_raw, iq_ready = [], []
            idx = linear(w_in, [C2_IQ, C2_IQ + 256], hid_k, normed, to(iq, iq_raw))
            next(idx)
            all_summed = sum_squares()
            hr = tmp.take()
            head_rstd = rstd(heads_ps, heads_ps.mem[0:32, 0, :], hr.mem[0:32, 0, :], HD, [all_summed, hr.free],
                             rows=32)
            run(idx)
            q_ready, k_ready = [None] * 4, [None] * 4

            def norm_heads():
                for n in (0, 4, 1, 5, 2, 6, 3, 7):
                    dst, gain, out = (q2, v2(l, "qn"), q_ready) if n < 4 else (k2, v2(l, "kn"), k_ready)
                    i = n % 4
                    x = dst[:, 2 * i:2 * i + 2, :]
                    ps = small_ps.take()
                    for j in range(2):
                        t = 2 * n + j
                        done = mm(ps.mem[:, j, :], spread[0:32, t, :], hr.mem[0:32, 0, :], True, True, ps.free,
                                  head_rstd, spread_landed)
                    w = stt(x, x, gain, ps.mem[:, :, :], ALU.mult, ALU.mult, done, qk_raw[n])
                    ps.release(w)
                    yield
                    out[i] = rotate(x, P, 0, cn("rot64"), 0, w)
                hr.release(done)

            ikr = tmp.take()

            def take_ik(i, ps, done):
                return act(ikr.mem[0:ID + IH, 0, :], ps[0:ID + IH, 0, :], ACT.Copy, done, ikr.free)
            run(linear(w_in, [C2_IK], hid_k, normed, take_ik, blocks=(0,), width=P))
            ik_raw = (ac.sem, ac.count)
            ps = small_ps.take()
            pe.wait(ps.free, ik_raw)
            for t in range(TT):
                done = tr(ps.mem[:, 0, t * IH:(t + 1) * IH], ikr.mem[ID:ID + IH, 0, t * P:(t + 1) * P],
                          ident[ID:ID + IH, ID:ID + IH])
            iw = small[:, 32:32 + TT * IH]
            iw_ready = act(iw, ps.mem[:, 0, 0:TT * IH], ACT.Copy, done)
            ps.release(iw_ready)
            ps = small_ps.take()
            pe.wait(ps.free, ik_raw)
            mm(ps.mem[:, 0, :], cn("dup", ID), ikr.mem[0:ID, 0, :], True, True)
            done = mm(ps.mem[:, 1, :], cn("rotdup", ID), ikr.mem[0:ID, 0, :], True, True)
            ikr.release(done)
            t1 = tmp.take()
            w = tt(ve, t1.mem[:, :, :], ps.mem[:, :, :], rope_cs[:, 0:2, :], ALU.mult, done, t1.free)
            ps.release(w)
            ik_ready = tt(ve, ik, t1.mem[:, 0, :], t1.mem[:, 1, :], ALU.add, w)
            t1.release(ik_ready)
            for j in range(2):
                iq_ready.append(rotate(iq[:, 2 * j:2 * j + 2, :], P, 0, cn("rot64"), 0, iq_raw[j]))

            v_ready, z_ready = [], []
            xbc_raw, xbc_ready = [None] * 24, [None] * 24

            def v_sink(i, ps, done):
                w = act(v2t[:, :, i * 256:(i + 1) * 256], ps[:, :, :], ACT.Copy, done)
                v_ready.append(w)
                return w

            def xbc_sink(i, ps, done):
                raw = tmp.take()
                w0 = act(raw.mem[:, :, :], ps[:, :, :], ACT.Copy, done, raw.free)
                for j in range(2):
                    c = 2 * i + j
                    y = xbc[:, c, :]
                    w1 = act(y, ps[:, j, :], ACT.Identity, bias=v2(l, "conv_b", c), scale=v2(l, "conv_w", 3 * 24 + c))
                    w = [w0, w1]
                    for tap in (2, 1, 0):
                        s = 3 - tap
                        w = stt(y[:, s:S], raw.mem[:, j, 0:S - s], v2(l, "conv_w", tap * 24 + c), y[:, s:S],
                                ALU.mult, ALU.add, w)
                    last = w
                    xbc_raw[c] = last
                raw.release(last)
                return w1

            def fill():
                yield from linear_tokens(w_in, [C2_V + 256 * i for i in range(4)], hid_kt, normed, v_sink)
                yield from linear(w_in, [C2_XBC + 256 * i for i in range(12)], hid_k, normed, xbc_sink)

            filler = fill()
            norm_heads_steps = norm_heads()

            def select():
                for t in range(TT):
                    n = (t + 1) * P
                    acc = score[:, t, 0:n]
                    w = None
                    for j in range(4):
                        half, pair = j // 2, j % 2
                        r0 = 64 * half
                        ps = small_ps.take()
                        pe.wait(ps.free, iq_ready[pair], ik_ready)
                        for i in range(2):
                            done = mm(ps.mem[:, i, 0:n], iq[r0:r0 + 64, 2 * pair + i, t * P:(t + 1) * P],
                                      ik[r0:r0 + 64, 0:n], True, True)
                        r = tmp.take()
                        pos = act(r.mem[:, :, 0:n], ps.mem[:, :, 0:n], ACT.Relu, done, r.free)
                        ps.release(pos)
                        for i in range(2):
                            head = 4 * pair + 2 * i + half
                            weight = iw[:, t * IH + head:t * IH + head + 1]
                            if j == 0 and i == 0:
                                w = ts(ve, acc, r.mem[:, i, 0:n], weight, None, ALU.mult, None, pos, iw_ready)
                            else:
                                w = stt(acc, r.mem[:, i, 0:n], weight, acc, ALU.mult, ALU.add, pos, w)
                        r.release(w)
                        if j % 2:
                            yield
                    w = ts(ve, acc, acc, IDX_SCALE, 0.0, ALU.mult, ALU.add, w)

                    def causal(ap, w, t=t, n=n):
                        return po.do(lambda e: e.affine_select(
                            out=ap, in_=ap, pattern=[[-1, n]], compare_op=ALU.is_ge, fill=NOT_KEPT, base=t * P,
                            channel_multiplier=1), w)
                    w = causal(acc, w)
                    st = stat.take()
                    best = st.mem[:, 0:8]
                    for _ in range(KEEP // 8):
                        w = ve.do(lambda e, acc=acc, best=best: e.max(best, acc), w, st.free)
                        w = ve.do(lambda e, acc=acc, best=best: e.match_replace(acc, best, acc, TAKEN), w)
                    st.release(w)
                    kp = keep[:, t, 0:n]
                    w = ts(ve, kp, acc, TAKEN, -NOT_KEPT, ALU.is_equal, ALU.mult, w)
                    w = ts(ve, kp, kp, NOT_KEPT, None, ALU.add, None, w)
                    keep_ready.append(causal(kp, w))
                    yield

            keep_ready = []
            weave(select(), (norm_heads_steps, 1.0), (filler, 1.0))
            run(norm_heads_steps)

            def scores2(h, out):
                j, r0 = h // 2, 64 * (h % 2)
                pe.wait(q_ready[j // 2], k_ready[j // 2], v_ready)
                ve.wait(keep_ready)
                for t in range(TT):
                    n = (t + 1) * P
                    done = mm(out[:, t, 0:n], q2[r0:r0 + 64, j, t * P:(t + 1) * P], k2[r0:r0 + 64, j, 0:n], True, True)
                return done

            o_ready = []
            while len(v_ready) < 4:
                next(filler)
            weave(attend(AH, scores2, [P, S], HD ** -0.5, keep, lambda h, kt: v2t[:, kt, h * 64:(h + 1) * 64],
                         lambda j: (o_p[0][:, j, :], o_p[1][:, j, :]), None, o_ready), (filler, 0.34))
            run(filler)
            attention_read = (pe.sem, pe.count)
            for c in (16, 20, 18, 22, 0, 2, 4, 6, 8, 10, 12, 14):
                y = xbc[:, c:c + 2, :]
                xbc_ready[c] = xbc_ready[c + 1] = act(y, y, ACT.Silu, xbc_raw[c], xbc_raw[c + 1])

            dtmp = tmp.take()
            u, e_ = dtmp.mem[0:SH, 0, :], dtmp.mem[0:SH, 1, :]
            dt_, cs = dts[0:SH, 0, :], dts[0:SH, 1, :]

            def take_dt(i, ps, done):
                return ts(ve, u, ps[0:SH, 0, :], v2(l, "dt_bias", rows=SH), None, ALU.add, None, done, dtmp.free)
            run(linear(w_in, [C2_DT], hid_k, normed, take_dt, blocks=(0,), width=P))
            w = (ve.sem, ve.count)
            w = ts(ve, e_, u, -1.0, None, ALU.mult, None, w)
            w = tt(ve, e_, e_, u, ALU.min, w)
            w = act(e_, e_, ACT.Exp, w)
            w = log1p(w, e_, (SH, S))
            dt_ready = stt(dt_, u, 0.0, e_, ALU.max, ALU.add, w, attention_read)
            acol = small[0:SH, 64:65]
            wa = act(acol, v2(l, "a_log", rows=SH), ACT.Exp)
            w = ts(ve, u, dt_, acol, -1.0, ALU.mult, ALU.mult, dt_ready, wa)
            cs_ready = ve.do(lambda e, cs=cs, u=u: e.tensor_tensor_scan(
                cs, ones[0:SH, 0:1].to_broadcast([SH, S]), u, 0.0, ALU.mult, ALU.add), w)
            dtmp.release(cs_ready)
            ps = small_ps.take()
            pe.wait(ps.free, cs_ready)
            for t in range(TT):
                tr(ps.mem[:, 0, t * SH:(t + 1) * SH], cs[:, t * P:(t + 1) * P], ident[0:SH, 0:SH], mark=False)
                done = tr(ps.mem[:, 0, (2 + t) * SH:(3 + t) * SH], dt_[:, t * P:(t + 1) * P], ident[0:SH, 0:SH])
            ncs, dtT = small[:, 80:80 + 2 * SH], small[:, 80 + 2 * SH:80 + 4 * SH]
            ncs_ready = act(ncs, ps.mem[:, 0, 0:2 * SH], ACT.Copy, done, scale=-1.0)
            dtT_ready = act(dtT, ps.mem[:, 0, 2 * SH:4 * SH], ACT.Copy)
            ps.release(dtT_ready)

            cb_ready = []
            for g in range(SG):
                ps = small_ps.take()
                flat = ps.mem[:, :, :].rearrange("p a b -> p (a b)")
                b, c = xbc[:, 16 + g, :], xbc[:, 20 + g, :]
                pe.wait(ps.free, xbc_ready[16 + g], xbc_ready[20 + g])
                mm(flat[:, 0:S], b[:, 0:P], c, True, True)
                done = mm(flat[:, S:S + P], b[:, P:S], c[:, P:S], True, True)
                w = tt(ve, cbm[:, g, :], flat[:, 0:384], cn("tri"), ALU.mult, done)
                ps.release(w)
                cb_ready.append(w)

            xtok_ready = []
            for j in range(8):
                ps = small_ps.take()
                pe.wait(ps.free)
                for t in range(TT):
                    for i in range(2):
                        turned = tr(ps.mem[:, t, i * P:(i + 1) * P], xbc[:, 2 * j + i, t * P:(t + 1) * P], ident,
                                    xbc_ready[2 * j + i])
                for t in range(TT):
                    w = tt(ve, xtok[:, t, j * 256:(j + 1) * 256].rearrange("p (h c) -> p h c", h=4),
                           ps.mem[:, t, :].rearrange("p (h c) -> p h c", h=4),
                           dtT[:, t * SH + 4 * j:t * SH + 4 * j + 4].unsqueeze(2).to_broadcast([P, 4, 64]),
                           ALU.mult, turned, dtT_ready, attention_read)
                ps.release(w)
                xtok_ready.append(w)

            z_done = []

            def ssd():
                live = {}
                for h in range(SH + 1):
                    if h < SH:
                        ps = small_ps.take()
                        done = mm(ps.mem[:, 0, :], ident[0:SH, h:h + 1].to_broadcast([SH, P]), cs, True, True, ps.free)
                        g = prob.take()
                        flat = g.mem[:, :, :].rearrange("p a b -> p (a b)")
                        ts(ve, flat[:, 0:S], ps.mem[:, 0, :], ncs[:, h:h + 1], 0.0, ALU.add, ALU.min, done, g.free,
                           ncs_ready)
                        w = ts(ve, flat[:, S:S + P], ps.mem[:, 0, P:S], ncs[:, SH + h:SH + h + 1], 0.0, ALU.add,
                               ALU.min)
                        ps.release(w)
                        w = act(flat[:, 0:384], flat[:, 0:384], ACT.Exp, w)
                        w = tt(po, flat[:, 0:384], flat[:, 0:384], cbm[:, h // 8, :], ALU.mult, w, cb_ready[h // 8])
                        live[h] = (g, flat, w)
                    if h >= 1:
                        hh = h - 1
                        g, flat, w = live.pop(hh)
                        r0 = 64 * (hh % 2)
                        if hh % 2 == 0:
                            live["y"] = small_ps.take()
                            pe.wait(live["y"].free)
                        y = live["y"]
                        pe.wait(w, xtok_ready[hh // 4])
                        mm(y.mem[r0:r0 + 64, 0, :], xtok[:, 0, hh * 64:hh * 64 + 64], flat[:, 0:S], True, False)
                        done = mm(y.mem[r0:r0 + 64, 0, P:S], xtok[:, 1, hh * 64:hh * 64 + 64], flat[:, S:S + P], False,
                                  True)
                        g.release(done)
                        if hh % 2:
                            j = hh // 2
                            xs = xbc[:, j, :]
                            w = stt(xs, xs, v2(l, "d_skip", j), y.mem[:, 0, :], ALU.mult, ALU.add, done)
                            y.release(w)
                            x_done.append(w)
                    yield

            x_done = []

            def gate_and_norm():
                for i in range(8):
                    pair = slice(2 * i, 2 * i + 2)
                    z = zbuf[:, pair, :]
                    w = act(z, z, ACT.Silu, z_raw[i])
                    z_done.extend([tt(po if i % 2 else ve, z, z, xbc[:, pair, :], ALU.mult, w, x_done)] * 2)
                yield
                for g in range(SG):
                    r = tmp.take()
                    ac.wait(r.free)
                    w = mean_square([zbuf[:, 4 * g + j, :] for j in range(4)], z_done[4 * g:4 * g + 4], 512, ones,
                                    r.mem[:, 0, :])
                    yield
                    for i in (2 * g, 2 * g + 1):
                        t = tmp.take()
                        for j in range(2):
                            w2 = stt(t.mem[:, j, :], zbuf[:, 2 * i + j, :], v2(l, "ssm_norm", 2 * i + j),
                                     r.mem[:, 0, :], ALU.mult, ALU.mult, w, t.free)
                        pair = slice(2 * i, 2 * i + 2)
                        w3 = split(po, t.mem[:, :, :], y_p[0][:, pair, :], y_p[1][:, pair, :], w2, z_done[2 * i])
                        t.release(w3)
                        y_ready2.extend([w3, w3])
                    r.release(w2)
                    yield

            y_ready2 = []
            ga_ready = [None] * 4

            def ga_sink(i, ps, done):
                ga_raw.append(act(mixed[:, 2 * i:2 * i + 2, :], ps[:, :, :], ACT.Copy, done, cb_ready))
                return ga_raw[i]

            ga_raw, z_raw = [], []

            def oa_sink(i, ps, done):
                m = mixed[:, 2 * i:2 * i + 2, :]
                mix_ready[i] = tt(ve, m, ps[:, :, :], m, ALU.mult, done, ga_ready[i])
                return mix_ready[i]

            mix_ready = [None] * 4
            gm_ready = [None] * 4

            def gm_sink(i, ps, done):
                gm_ready[i] = act(gmb[:, 2 * i:2 * i + 2, :], ps[:, :, :], ACT.Sigmoid, done, oa_read[0])
                return gm_ready[i]

            oa_read = [None]

            def fill():
                yield from linear(w_in, [C2_GA + 256 * i for i in range(4)], hid_k, normed, ga_sink)
                yield from linear(w_in, [C2_Z + 256 * i for i in range(8)], hid_k, normed, to(zbuf, z_raw))

            filler = fill()
            weave(ssd(), (filler, 0.4))
            run(filler)
            for i in range(4):
                m = mixed[:, 2 * i:2 * i + 2, :]
                ga_ready[i] = act(m, m, ACT.Sigmoid, ga_raw[i])
            finish = gate_and_norm()
            weave(linear(A["w_ao"][l], branch_cols, of(o_p), o_ready, oa_sink), (finish, 1.0))
            oa_read[0] = (pe.sem, pe.count)
            weave(linear(w_in, [C2_GM + 256 * i for i in range(4)], hid_k, normed, gm_sink), (finish, 1.0))
            run(finish)

            def os_sink(i, ps, done):
                t = tmp.take()
                w = tt(ve, t.mem[:, :, :], ps[:, :, :], gmb[:, 2 * i:2 * i + 2, :], ALU.mult, done, gm_ready[i], t.free)
                m = mixed[:, 2 * i:2 * i + 2, :]
                mix_ready[i] = tt(po, m, m, t.mem[:, :, :], ALU.add, w, mix_ready[i])
                t.release(mix_ready[i])
                pair = slice(2 * i, 2 * i + 2)
                x = split(ve, m, hid[0][:, pair, :], hid[1][:, pair, :], mix_ready[i], hid_read)
                mixed_in.extend([x, x])
                return w

            mixed_in = []
            hid_read = (pe.sem, pe.count)
            run(linear(A["w_so"][l], branch_cols, of(y_p), y_ready2, os_sink, kts=16))

            def residual_sink(half, out):
                def sink(i, ps, done):
                    for j in range(2):
                        t = 2 * i + j
                        w = stt(xres[:, t, :], ps[:, j, :], hgate(half, t), xres[:, t, :], ALU.mult, ALU.add, done)
                        out.append(w)
                    return w
                return sink
            x_ready = []
            run(linear(A["w_out2"][l], branch_cols, hid_k, mixed_in, residual_sink(0, x_ready)))

            hid_free = (pe.sem, pe.count)
            normed = norm_residual(x_ready, hscale(1), hshift(1), hid_free)
            f_p = parts(4096, 4096 + 22 * S, 22)
            f_ready = [None] * 22
            held = {}

            def conv3(i, ps, done, base, dst_ap, free):
                raw = tmp.take()
                w0 = act(raw.mem[:, :, :], ps[:, :, :], ACT.Copy, done, raw.free)
                for j in range(2):
                    c = base + 2 * i + j
                    y = dst_ap[:, j, :]
                    w1 = act(y, ps[:, j, :], ACT.Identity, free, bias=v2(l, "fconv_b", c),
                             scale=v2(l, "fconv_w", 2 * 44 + c))
                    w = [w0, w1]
                    for tap in (1, 0):
                        s = 2 - tap
                        w = stt(y[:, s:S], raw.mem[:, j, 0:S - s], v2(l, "fconv_w", tap * 44 + c), y[:, s:S],
                                ALU.mult, ALU.add, w)
                raw.release(w)
                return w1, w

            def gate_half(i, ps, done):
                s = prob.take()
                read, w = conv3(i, ps, done, 22, s.mem, s.free)
                held[i] = (s, act(s.mem[:, :, :], s.mem[:, :, :], ACT.Silu, w))
                return read

            def val_half(i, ps, done):
                s, gated = held.pop(i)
                v = tmp.take()
                read, w = conv3(i, ps, done, 0, v.mem, v.free)
                w = tt(ve, v.mem[:, :, :], v.mem[:, :, :], s.mem[:, :, :], ALU.mult, w, gated)
                s.release(w)
                pair = slice(2 * i, 2 * i + 2)
                w = split(po, v.mem[:, :, :], f_p[0][:, pair, :], f_p[1][:, pair, :], w, x_ready)
                v.release(w)
                f_ready[2 * i] = f_ready[2 * i + 1] = w
                return read

            gs = linear(A["w_up2"][l], [D_FF + 256 * i for i in range(11)], hid_k, normed, gate_half)
            us = linear(A["w_up2"][l], [256 * i for i in range(11)], hid_k, normed, val_half)
            for _ in range(11):
                next(gs)
                next(us)
            hid_free = (pe.sem, pe.count)
            out = []
            run(linear(A["w_down2"][l], branch_cols, of(f_p), f_ready, residual_sink(1, out), kts=22))
            x_ready = out

        stored = sem("stored")
        sp.wait(x_ready)
        sp.ops.append(lambda e: e.dma_start(A["out"].rearrange("p (t s) -> p t s", t=DT),
                                            xres[:, :, :]).then_inc(stored, 16))
        sp.ops.append(lambda e: e.wait_ge(stored, 16))

        with nc.Block() as block:
            @block.sync
            def _(e):
                sp.play(e)

            @block.tensor
            def _(e):
                pe.play(e)

            @block.scalar
            def _(e):
                ac.play(e)

            @block.vector
            def _(e):
                ve.play(e)

            @block.gpsimd
            def _(e):
                po.play(e)


WEIGHTS = {"w_in": "w_in", "w_uq": "mla_w_uq", "w_ukv": "mla_w_ukv", "w_o": "mla_w_o", "w_pw": "conv_w_pw",
           "w_ro": "ret_w_o", "w_out": "w_out", "w_gate": "ffn_w_gate", "w_up": "ffn_w_up",
           "w_down": "ffn_w_down", "w_ada": "w_ada_2", "w_in2": "w_in_2", "w_ao": "w_attn_o_2",
           "w_so": "w_ssm_o_2", "w_out2": "w_out_2", "w_up2": "w_up_2", "w_down2": "w_down_2"}


def columns(v):
    return np.ascontiguousarray(v.reshape(-1, P).T)


def rows_padded(v):
    out = np.zeros((P, 1), v.dtype)
    out[:v.shape[0], 0] = v
    return out


def kernel(**inputs):
    import concourse.bacc as bacc
    from concourse.bass_utils import run_bass_kernel_spmd

    a = {k: np.asarray(v) for k, v in inputs.items()}
    parts = []
    for l in range(DEPTH):
        parts += [columns(a[n][l]) for n in ("ln_mix_pre", "ln_mix_post", "ln_ffn_pre", "ln_ffn_post", "mla_q_norm",
                                             "mla_kv_norm", "conv_w_dw", "conv_b_dw", "conv_ln_g", "conv_ln_b",
                                             "ret_gn_g")]
        parts.append(np.tile(a["ret_decay_logits"][l].reshape(1, 2 * RET_H), (P, 1)))
    for l in range(DEPTH):
        parts += [columns(a[n][l]) for n in ("b_ada_2", "norm1_g_2", "norm2_g_2")]
        parts += [columns(np.tile(a[n][l], 2)) for n in ("q_norm_g_2", "k_norm_g_2")]
        parts += [columns(a[n][l]) for n in ("ssm_conv_w_2", "ssm_conv_b_2")]
        parts += [rows_padded(a["dt_bias_2"][l]), rows_padded(a["a_log_2"][l])]
        parts += [columns(np.repeat(a["d_skip_2"][l], 64)), columns(a["ssm_norm_g_2"][l]),
                  columns(a["ffn_conv_w_2"][l]), columns(a["ffn_conv_b_2"][l])]
    host = {
        "consts": constants(),
        "spread": spreader(),
        "vectors": np.ascontiguousarray(np.concatenate(parts, 1)),
        "x": np.ascontiguousarray(a["x"][0].T.reshape(DT, P, S).transpose(1, 0, 2).reshape(P, DT * S)),
        "positions": np.ascontiguousarray(
            np.tile(np.concatenate([a["positions"], a["positions_2"]], 1), (P, 1))),
        "c": columns(a["c_2"][0]),
    }
    for name, source in WEIGHTS.items():
        host[name] = np.ascontiguousarray(a[source])

    nc = bacc.Bacc("TRN2", target_bir_lowering=False, num_devices=1)
    A = {n: nc.dram_tensor(f"in_{n}", v.shape, mybir.dt.from_np(v.dtype), kind="ExternalInput").ap()
         for n, v in host.items()}
    A["out"] = nc.dram_tensor("out_x", (P, DT * S), F32, kind="ExternalOutput").ap()
    build(nc, A)
    r = run_bass_kernel_spmd(nc, [{f"in_{n}": v for n, v in host.items()}], core_ids=[0])
    y = r.results[0]["out_x"].reshape(P, DT, S).transpose(2, 1, 0).reshape(1, S, D)
    return np.ascontiguousarray(y)
```

```python
from contextlib import ExitStack
from itertools import chain

import numpy as np

import concourse.bass as bass
from concourse import mybir

F32 = mybir.dt.float32
I32 = mybir.dt.int32
F32R = mybir.dt.float32r
ALU = mybir.AluOpType
ACT = mybir.ActivationFunctionType
AX = mybir.AxisListType

P = 128
D = 1024
S = 256
DEPTH = 2
DT = D // P
TT = S // P
EPS = 1e-6

HEADS, NOPE, ROPE, VDIM = 8, 64, 32, 64
QK = NOPE + ROPE
Q_RANK, KV_RANK = 256, 128
CONV_CH, CONV_W = 512, 31
RET_H, RET_DK, RET_DV = 4, 128, 256
FFN = 2816
IN1 = [Q_RANK, KV_RANK, ROPE, 2 * CONV_CH, RET_H * RET_DK, RET_H * RET_DK, RET_H * RET_DV,
       RET_H * RET_DV, 3 * D]
(C_Q, C_KV, C_PE, C_CONV, C_RQ, C_RK, C_RV, C_RG, C_GATE, _E1) = [int(v) for v in np.cumsum([0] + IN1)]

AH, HD = 16, 64
IH, ID = 8, 64
IDX_SCALE = (IH ** -0.5) * (ID ** -0.5)
KEEP = 64
D_IN = 2 * D
SH = D_IN // 64
SG = 4
NST = 128
XBC = D_IN + 2 * SG * NST
D_FF = 2816
IN2 = [D, D, D, IH * ID, ID, IH, D_IN, XBC, SH, D, D]
(C2_Q, C2_K, C2_V, C2_IQ, C2_IK, C2_IW, C2_Z, C2_XBC, C2_DT, C2_GA, C2_GM, _E2) = [
    int(v) for v in np.cumsum([0] + IN2)]

NOT_KEPT = -1.0e30
TAKEN = -3.0e38
TWO_PI = 2 * np.pi
PI_1 = 6.28125
PI_2 = float(np.float32(round((TWO_PI - PI_1) * 2 ** 20) / 2 ** 20))
PI_3 = float(np.float32(TWO_PI - PI_1 - PI_2))
ROUND_MAGIC = 1.5 * 2 ** 23
PI_F = 3.1415925


def offsets(sizes):
    at, out = 0, {}
    for name, n in sizes:
        out[name] = (at, at + n)
        at += n
    return out, at


VEC1, NVEC1 = offsets([("mix_pre", 8), ("mix_post", 8), ("ffn_pre", 8), ("ffn_post", 8), ("q_norm", 2),
                       ("kv_norm", 1), ("conv_w", CONV_W * 4), ("conv_b", 4), ("conv_g", 4),
                       ("conv_beta", 4), ("gn_g", 8), ("decay", 2 * RET_H)])
VEC2, NVEC2 = offsets([("b_ada", 48), ("norm1", 8), ("norm2", 8), ("qn", 1), ("kn", 1), ("conv_w", 4 * 24),
                       ("conv_b", 24), ("dt_bias", 1), ("a_log", 1), ("d_skip", 16), ("ssm_norm", 16),
                       ("fconv_w", 3 * 44), ("fconv_b", 44)])
CON, NCON = offsets([("ident", P), ("ones", P), ("freq", 3), ("eps", 1), ("ones64", P), ("rot96", QK), ("rot128", P), ("rot64", P),
                     ("dup", P), ("rotdup", P), ("to_row", 64), ("ahead", TT * S), ("behind", TT * S), ("tri", 384)])

KC = 4
UNIT = KC * 256
RAW, SPLIT = 5, 4
AHEAD = SPLIT - 1
POOL_EVERY = 3
ARENA = 24 * 1024


def rotation(n, dim):
    m = np.zeros((n, n), np.float32)
    half = dim // 2
    for g in range(0, n, dim):
        for i in range(half):
            m[g + half + i, g + i] = -1.0
            m[g + i, g + half + i] = 1.0
    return m


def constants():
    c = np.zeros((P, NCON), np.float32)

    def put(name, v, r0=0):
        a, _ = CON[name]
        c[r0:r0 + v.shape[0], a:a + v.shape[1]] = v

    put("ident", np.eye(P, dtype=np.float32))
    put("ones", np.ones((P, P), np.float32))
    put("ones64", np.kron(np.eye(2, dtype=np.float32), np.ones((64, 64), np.float32)))
    r96 = np.zeros((QK, QK), np.float32)
    r96[NOPE:, NOPE:] = rotation(ROPE, ROPE)
    put("rot96", r96)
    put("rot128", rotation(P, RET_DK))
    put("rot64", rotation(P, HD))
    put("dup", np.tile(np.eye(64, dtype=np.float32), (1, 2)))
    to_row = np.zeros((P, 64), np.float32)
    to_row[:64, 31] = to_row[64:, 32] = 1.0
    put("to_row", to_row)
    put("rotdup", np.tile(rotation(64, 64), (1, 2)))
    m = (np.arange(P)[:, None] + P * np.arange(TT)[None, :])[:, :, None]
    diff = np.arange(S)[None, None, :] - m
    put("ahead", np.maximum(diff, 0).reshape(P, -1).astype(np.float32))
    put("behind", np.maximum(-diff, 0).reshape(P, -1).astype(np.float32))
    tri = (np.arange(P)[:, None] <= np.arange(P)[None, :]).astype(np.float32)
    put("tri", np.concatenate([tri, np.ones((P, P), np.float32), tri], 1))
    freq = np.zeros((P, 3), np.float32)

    def inv_freq(dim):
        k = np.arange(0, dim, 2, dtype=np.float32) / np.float32(dim)
        return k.astype(np.float64)

    for row in range(P):
        freq[row, 0] = np.float32(10000.0 ** -inv_freq(ROPE)[row % 16])
        freq[row, 1] = np.float32(10000.0 ** -inv_freq(RET_DK)[row % 64])
        freq[row, 2] = np.float32(1) / np.float32(10000.0 ** inv_freq(HD)[row % 32])
    put("freq", freq)
    put("eps", np.full((P, 1), EPS, np.float32))
    return c


def spreader():
    s = np.zeros((32, 16, P), np.float32)
    for t in range(16):
        s[2 * t, t, :64] = s[2 * t + 1, t, 64:] = 1.0
    return s.reshape(32, 16 * P)


class Queue:

    def __init__(self, sem):
        self.sem, self.count, self.ops, self.seen = sem, 0, [], {}

    def wait(self, *tokens):
        for t in tokens:
            if t is None:
                continue
            if isinstance(t, list):
                self.wait(*t)
                continue
            sem, value = t
            if self.seen.get(sem.name, 0) < value:
                self.seen[sem.name] = value
                self.ops.append(lambda e, sem=sem, value=value: e.wait_ge(sem, value))

    def do(self, fn, *tokens, mark=True):
        self.wait(*tokens)
        if not mark:
            self.ops.append(fn)
            return None
        self.count += 1
        sem = self.sem
        self.ops.append(lambda e: fn(e).then_inc(sem, 1))
        return (sem, self.count)

    def hole(self):
        place = []
        self.ops.append(place)
        return place

    def play(self, eng):
        for op in self.ops:
            if isinstance(op, list):
                for inner in op:
                    inner(eng)
            else:
                op(eng)


class Slot:

    def __init__(self, mem, ring=None):
        self.mem, self.ring, self.free, self.sem, self.loads = mem, ring, None, None, 0

    def release(self, token):
        self.free = token
        self.ring.idle.append(self)


class Ring:

    def __init__(self, mems):
        self.slots = [Slot(m, self) for m in mems]
        self.idle = list(self.slots)

    def take(self):
        return self.idle.pop(0)


def weave(main, *others):
    due = [0.99] * len(others)
    for _ in main:
        for i, (steps, rate) in enumerate(others):
            due[i] += rate
            while due[i] >= 1:
                due[i] -= 1
                next(steps, None)


def run(steps):
    for _ in steps:
        pass


def build(nc, A):
    with ExitStack() as ctx:
        def sb(name, shape, dt=F32):
            return ctx.enter_context(nc.sbuf_tensor(name, shape, dt))

        def sem(name):
            return ctx.enter_context(nc.semaphore(name))

        pe, ve, ac, po, sp = (Queue(sem(n)) for n in ("pe_done", "ve_done", "ac_done", "po_done", "sp_done"))

        con = sb("con", [P, NCON])
        vec = sb("vec", [P, DEPTH * (NVEC1 + NVEC2)])
        xres = sb("xres", [P, DT, S])
        rope_cs = sb("rope_cs", [P, 4, S])
        pos_i = sb("pos_i", [P, 2, S], I32)
        eps_col, table_in = sb("eps_col", [P, 1])[:, :], sb("table_in", [P, 1])[:, :]
        ac.wait(ve.do(lambda e: e.memset(eps_col, EPS)))
        small = sb("small", [P, 80 + 4 * SH])
        mod = sb("mod", [P, DEPTH, 48])
        ccol = sb("ccol", [P, DT])
        cact = sb("cact", [P, DT])

        raws = Ring([sb(f"raw{i}", [P, UNIT]) for i in range(RAW)])
        for i, s in enumerate(raws.slots):
            s.sem = sem(f"raw_landed{i}")
        w_hi = [sb(f"w_hi{i}", [P, UNIT], F32R) for i in range(SPLIT)]
        w_lo = [sb(f"w_lo{i}", [P, UNIT], F32R) for i in range(SPLIT)]
        hi_done, lo_done = sem("hi_done"), [sem("lo_done_ve"), sem("lo_done_po")]
        lo_count = [0, 0]
        used = [None] * SPLIT
        side = Ring([sb(f"side{i}", [P, UNIT]) for i in range(2)])
        for i, s in enumerate(side.slots):
            s.sem = sem(f"side_landed{i}")
        tmp = Ring([sb(f"tmp{i}", [P, 2, S]) for i in range(6)])
        prob = Ring([sb(f"prob{i}", [P, 2, S]) for i in range(3)])
        probT = Ring([sb(f"probT{i}", [P, 2, S]) for i in range(2)])
        stat = Ring([sb(f"stat{i}", [P, 16]) for i in range(4)])
        fence = sb("arena_fence", [P, ARENA])
        at = nc.sbuf_base - ARENA * 4
        arena = nc.alloc_sbuf_tensor_at("arena", [P, ARENA], F32, offset=at)
        arena_r = nc.alloc_sbuf_tensor_at("arena_r", [P, ARENA], F32R, offset=at)

        def region(at, *shape, mem=None):
            n = int(np.prod(shape))
            assert at + n <= ARENA, (at, shape)
            v = (arena if mem is None else mem)[:, at:at + n]
            if len(shape) == 1:
                return v
            return v.rearrange("p (a b) -> p a b", a=shape[0])

        def parts(hi_at, lo_at, tiles):
            return region(hi_at, tiles, S, mem=arena_r), region(lo_at, tiles, S, mem=arena_r)

        banks = [ctx.enter_context(nc.psum_tensor(f"bank{i}", [P, 2, S], F32)) for i in range(8)]
        big = Ring(banks[0:3])
        small_ps = Ring(banks[3:8])

        def cn(name, rows=P, r0=0):
            a, b = CON[name]
            return con[r0:r0 + rows, a:b]

        ident, ones, eps = cn("ident"), cn("ones"), cn("eps")

        def mm(out, lhsT, rhs, start, stop, *tokens, mark=None, skip=False):
            return pe.do(lambda e: e.matmul(out, lhsT, rhs, start=start, stop=stop, skip_group_check=skip),
                         *tokens, mark=stop if mark is None else mark)

        def tr(out, in_, idn, *tokens, mark=True):
            return pe.do(lambda e: e.transpose(out, in_, idn), *tokens, mark=mark)

        def act(out, in_, fn, *tokens, bias=0.0, scale=1.0, acc=None, mark=True):
            if fn == ACT.Copy:
                return ac.do(lambda e: e.activation(out, in_, fn, scale=scale), *tokens, mark=mark)
            if acc is None:
                return ac.do(lambda e: e.activation(out, in_, fn, bias=bias, scale=scale), *tokens, mark=mark)
            return ac.do(lambda e: e.activation(out, in_, fn, bias=bias, scale=scale, accum_out=acc),
                         *tokens, mark=mark)

        def ts(q, out, in0, s1, s2, op0, op1, *tokens, mark=True):
            if s2 is None:
                return q.do(lambda e: e.tensor_scalar(out, in0, s1, None, op0), *tokens, mark=mark)
            return q.do(lambda e: e.tensor_scalar(out, in0, s1, s2, op0, op1), *tokens, mark=mark)

        def tt(q, out, a, b, op, *tokens, mark=True):
            return q.do(lambda e: e.tensor_tensor(out, a, b, op), *tokens, mark=mark)

        def stt(out, in0, s, in1, op0, op1, *tokens, mark=True):
            return ve.do(lambda e: e.scalar_tensor_tensor(out, in0, s, in1, op0, op1), *tokens, mark=mark)

        def recip(out, in_, *tokens):
            return ve.do(lambda e: e.reciprocal(out, in_), *tokens)

        def load(dst, src, s, *tokens):
            sp.wait(*tokens)
            s.loads += 1
            landed = s.sem
            sp.ops.append(lambda e: e.dma_start(dst, src).then_inc(landed, 16))
            return (landed, 16 * s.loads)

        def load_side(src, kts, width, ring):
            s = ring.take()
            view = s.mem[:, 0:kts * width].rearrange("p (t n) -> p t n", t=kts)
            po.wait(s.free)
            s.loads += 1
            landed = s.sem
            po.ops.append(lambda e: e.dma_start(view, src.rearrange("(t p) n -> p t n", p=P)).then_inc(landed, 16))
            return s, view, (landed, 16 * s.loads)

        holes, first_places = [], []

        def split_unit(src, kts, width):
            n = len(holes)
            holes.append((ac.hole(), ve.hole(), po.hole()))
            raw, words, i = raws.take(), kts * width, n % SPLIT
            landed = load(raw.mem[:, 0:words].rearrange("p (t n) -> p t n", t=kts),
                          src.rearrange("(t p) n -> p t n", p=P), raw, raw.free)
            hi, lo, w = w_hi[i][:, 0:words], w_lo[i][:, 0:words], raw.mem[:, 0:words]
            free = used[i]
            by_pool = n % POOL_EVERY == POOL_EVERY - 1
            lo_sem, lo_count[by_pool] = lo_done[by_pool], lo_count[by_pool] + 1
            places = holes[max(n - AHEAD, 0)] if n else first_places
            in_act, in_lo = places[0], places[2 if by_pool else 1]
            for place in (in_act, in_lo):
                place.append(lambda e: e.wait_ge(*landed))
                if free is not None:
                    place.append(lambda e: e.wait_ge(*free))
            in_act.append(lambda e: e.activation(hi, w, ACT.Copy).then_inc(hi_done, 1))
            in_lo.append(lambda e: e.wait_ge(hi_done, n + 1))
            in_lo.append(lambda e: e.tensor_tensor(lo, w, hi.bitcast(F32), ALU.subtract).then_inc(lo_sem, 1))
            split_done = (lo_sem, lo_count[by_pool])
            raw.release([(hi_done, n + 1), split_done])
            pe.wait(split_done)

            def view(m):
                return m[i][:, 0:words].rearrange("p (t n) -> p t n", t=kts)
            return i, view(w_hi), view(w_lo)

        def linear(w, cols, rhs, ready, sink, kts=DT, blocks=(0, P), width=256):
            for i, c in enumerate(cols):
                bank = big.take()
                pe.wait(bank.free)
                for k0 in range(0, kts, KC):
                    n = min(KC, kts - k0)
                    slot, hi, lo = split_unit(w[k0 * P:(k0 + n) * P, c:c + width], n, width)
                    for half, b in enumerate(blocks):
                        for k in range(n):
                            pe.wait(ready[k0 + k])
                            x_hi, x_lo = rhs(k0 + k)
                            out = bank.mem[:, half, :]
                            last = k0 + k == kts - 1
                            mm(out, hi[:, k, b:b + P], x_hi, k0 + k == 0 and half == 0, False, skip=True)
                            mm(out, hi[:, k, b:b + P], x_lo, False, False, skip=True)
                            done = mm(out, lo[:, k, b:b + P], x_hi, False, last, skip=True,
                                      mark=k == n - 1 and half == len(blocks) - 1)
                    used[slot] = done
                bank.release(sink(i, bank.mem, done))
                yield

        def linear_tokens(w, cols, lhs, ready, sink):
            for i, c in enumerate(cols):
                bank = big.take()
                pe.wait(bank.free)
                for k0 in range(0, DT, KC):
                    slot, hi, lo = split_unit(w[k0 * P:(k0 + KC) * P, c:c + 256], KC, 256)
                    for t in range(TT):
                        for k in range(KC):
                            pe.wait(ready[k0 + k])
                            x_hi, x_lo = lhs(k0 + k, t)
                            out = bank.mem[:, t, :]
                            mm(out, x_hi, hi[:, k, :], k0 + k == 0 and t == 0, False, skip=True)
                            mm(out, x_lo, hi[:, k, :], False, False, skip=True)
                            done = mm(out, x_hi, lo[:, k, :], False, k0 + k == DT - 1, skip=True,
                                      mark=k == KC - 1 and t == 1)
                    used[slot] = done
                bank.release(sink(i, bank.mem, done))
                yield

        def split(q, src, hi, lo, *tokens):
            a = act(hi, src, ACT.Copy, *tokens)
            return [a, tt(q, lo, src, hi.bitcast(F32), ALU.subtract, a)]

        first_loads = Slot(None)
        first_loads.sem = sem("small_landed")
        table_loads = Slot(None)
        table_loads.sem = sem("tables_landed")
        hot_loads = Slot(None)
        hot_loads.sem = sem("hot_landed")
        hot = CON["eps"][1]
        load(con[:, 0:hot], A["consts"][:, 0:hot], hot_loads)
        pos_in = load(pos_i[:, :, :], A["positions"].rearrange("p (t s) -> p t s", t=2), hot_loads)
        for q in (pe, ve, ac):
            q.wait(pos_in)
        x_loads = Slot(None)
        x_loads.sem = sem("x_landed")
        x_in = load(xres[:, :, :], A["x"].rearrange("p (t s) -> p t s", t=DT), x_loads)
        inputs = load(vec[:, :], A["vectors"], first_loads)

        def load_tables():
            load(ccol[:, :], A["c"], table_loads)
            landed = load(con[:, hot:NCON], A["consts"][:, hot:NCON], table_loads)
            for q in (pe, ve, ac, po):
                q.wait(landed)

        def v1(l, name, j=0, n=1, rows=P, r0=0):
            a = l * NVEC1 + VEC1[name][0] + j
            return vec[r0:r0 + rows, a:a + n]

        def v2(l, name, j=0, n=1, rows=P, r0=0):
            a = DEPTH * NVEC1 + l * NVEC2 + VEC2[name][0] + j
            return vec[r0:r0 + rows, a:a + n]

        def rotary(columns_, which, out):
            n_t = len(columns_)
            table = rope_cs[:, 0:2 * n_t, :].rearrange("p (j c) s -> p j c s", c=2)
            cos, sin = table[:, :, 0, :], table[:, :, 1, :]
            t1, t2, t3 = tmp.take(), tmp.take(), tmp.take()
            ang, n, r = (t.mem[:, 0:n_t, :] for t in (t1, t2, t3))
            w0 = ve.do(lambda e: e.tensor_copy(n[:, 0, :], pos_i[:, which, :]), t1.free, t2.free, t3.free)
            for i, k in enumerate(columns_):
                w = ts(ve, ang[:, i, :], n[:, 0, :], cn("freq")[:, k:k + 1], None, ALU.mult, None, w0)
            w = ts(ve, n, ang, float(1 / TWO_PI), ROUND_MAGIC, ALU.mult, ALU.add, w)
            w = ts(ve, n, n, ROUND_MAGIC, None, ALU.subtract, None, w)
            w = stt(r, n, -PI_1, ang, ALU.mult, ALU.add, w)
            w = stt(r, n, -PI_2, r, ALU.mult, ALU.add, w)
            w = stt(r, n, -PI_3, r, ALU.mult, ALU.add, w)
            w = ts(ve, r, r, PI_F, -PI_F, ALU.min, ALU.max, w)
            yield
            wa = act(sin, r, ACT.Sin, w)
            wb = act(cos, r, ACT.Sin, w, scale=0.5)
            yield
            w = tt(ve, cos, cos, cos, ALU.mult, wb)
            w = ts(ve, cos, cos, -2.0, 1.0, ALU.mult, ALU.add, w)
            for t in (t1, t2, t3):
                t.release([w, wa])
            out += [w, wa]
        tables = []

        def both(ap):
            return ap.unsqueeze(1).to_broadcast([ap.shape[0], 2, S])

        last_table = [None]

        class SquareSum:

            def __init__(self, tiles):
                self.ps, self.tiles, self.seen, self.late = small_ps.take(), tiles, 0, []
                pe.wait(self.ps.free)
                last_table[0] = act(table_in, eps_col, ACT.Sqrt, last_table[0])

            def add(self, x, q, *ready):
                sq = tmp.take()
                n = x.shape[1]
                o = sq.mem[:, 0:n, :]
                w = act(o, x, ACT.Square, sq.free, *ready) if q is ac else tt(q, o, x, x, ALU.mult, sq.free, *ready)
                self.sum_up()
                self.late.append((sq, n, w))
                return w

            def sum_up(self):
                while self.late:
                    sq, n, w = self.late.pop()
                    for i in range(n):
                        self.done = mm(self.ps.mem[:, 0, :], ones, sq.mem[:, i, :], self.seen == 0,
                                       self.seen == self.tiles - 1, w, mark=i == n - 1)
                        self.seen += 1
                    sq.release(self.done)

            def close(self, width):
                self.sum_up()
                self.slot = tmp.take()
                rs = self.slot.mem[:, 0, :]
                root = act(rs, self.ps.mem[:, 0, :], ACT.Sqrt, self.done, self.slot.free, scale=1.0 / width, bias=eps_col)
                self.ps.release(root)
                return rs, recip(rs, rs, root)

            def release(self, token):
                self.slot.release(token)

        def mean_square(pieces, width):
            total = SquareSum(sum(x.shape[1] for x, _ in pieces))
            for i, (x, ready) in enumerate(pieces):
                total.add(x, ac if i % 2 == 0 else ve, ready)
            rs, w = total.close(width)
            return total, rs, w

        def norm_residual(total, gain, shift, done_reading, meanwhile=None):
            rs, w = total.close(D)
            if meanwhile is not None:
                next(meanwhile)
                first_places.extend([ac.hole(), ve.hole(), po.hole()])
            out = []
            for j in range(DT // 2):
                h = tmp.take()
                pair = slice(2 * j, 2 * j + 2)
                if shift is None:
                    for t in (2 * j, 2 * j + 1):
                        last = stt(h.mem[:, t % 2, :], xres[:, t, :], gain(t), rs, ALU.mult, ALU.mult, w, h.free)
                    done = last
                else:
                    last = tt(ve, h.mem[:, :, :], xres[:, pair, :], both(rs), ALU.mult, w, h.free)
                    for t in (2 * j, 2 * j + 1):
                        o = h.mem[:, t % 2, :]
                        done = act(o, o, ACT.Identity, last, scale=gain(t), bias=shift(t))
                parts_done = split(po if j % 2 else ve, h.mem[:, :, :], hid[0][:, pair, :], hid[1][:, pair, :], done,
                                   done_reading)
                h.release(parts_done)
                out.extend([parts_done, parts_done])
            total.release(last)
            return out

        hid = parts(0, 2048, DT)

        def of(pair):
            return lambda k: (pair[0][:, k, :], pair[1][:, k, :])

        hid_k = of(hid)

        def hid_kt(k, t):
            return tuple(part[:, k, t * P:(t + 1) * P] for part in hid)

        def log1p(e, u, shape, out):
            z, z2, acc = (tmp.take() for _ in range(3))
            zz, zz2, aa = (t.mem[0:shape[0], 0, 0:shape[1]] for t in (z, z2, acc))
            w = ts(ve, zz, u, 2.0, None, ALU.add, None, e, z.free, z2.free, acc.free)
            w = recip(zz, zz, w)
            w = tt(ve, zz, zz, u, ALU.mult, w)
            w = tt(ve, zz2, zz, zz, ALU.mult, w)
            w = ts(ve, aa, zz2, 2.0 / 17, 2.0 / 15, ALU.mult, ALU.add, w)
            for d in (13, 11, 9, 7, 5, 3, 1):
                w = tt(ve, aa, aa, zz2, ALU.mult, w)
                w = ts(ve, aa, aa, 2.0 / d, None, ALU.add, None, w)
                yield
            w = tt(ve, u, aa, zz, ALU.mult, w)
            for t in (z, z2, acc):
                t.release(w)
            out.append(w)

        def rotate(x, n_rows, r0, rot, table, ready):
            cos = rope_cs[r0:r0 + n_rows, 2 * table, :]
            sin = rope_cs[r0:r0 + n_rows, 2 * table + 1, :]
            ps = small_ps.take()
            turned = mm(ps.mem[r0:r0 + n_rows, :, :], rot, x, True, True, ps.free, ready)
            a = tmp.take()
            am = a.mem[r0:r0 + n_rows, :, :]
            w1 = tt(ve, am, ps.mem[r0:r0 + n_rows, :, :], both(sin), ALU.mult, turned, a.free, tables)
            ps.release(w1)
            w2 = tt(po if n_rows == P else ve, x, x, both(cos), ALU.mult, turned, ready, tables)
            w3 = tt(ve, x, x, am, ALU.add, w1, w2)
            a.release(w3)
            return w3

        spread_loads = Slot(None)
        spread_loads.sem = sem("spread_landed")
        mod_ready = [None] * DEPTH
        mod_ring = Ring([region(17408 + UNIT * i, UNIT) for i in range(6)])
        for i, s in enumerate(mod_ring.slots):
            s.sem = sem(f"mod_landed{i}")

        def modulation(l, ring_free, silu_c):
            w = A["w_ada"][l]
            po.wait(ring_free)

            def ask(b):
                return [load_side(w[k0 * P:(k0 + 2) * P, b * 512:b * 512 + 512], 2, 512, mod_ring)
                        for k0 in range(0, DT, 2)]

            asked = ask(0)
            late = []
            for b in range(12):
                if b % 6 == 0:
                    bank = small_ps.take()
                    flat = bank.mem[:, 0, :]
                sums = tmp.take()
                acc = sums.mem[:, :, :].rearrange("p a b -> p (a b)")
                done = None
                more = list(range(0, DT, 2)) if b < 11 else []
                for k0 in range(0, DT, 2):
                    slot, view, landed = asked.pop(0)
                    for k in range(2):
                        weight = cact[:, k0 + k:k0 + k + 1]
                        if done is None:
                            done = ts(ve, acc, view[:, k, :], weight, None, ALU.mult, None, landed, silu_c,
                                      sums.free)
                        else:
                            done = stt(acc, view[:, k, :], weight, acc, ALU.mult, ALU.add, landed, done)
                    slot.release(done)
                    if more:
                        asked.append(load_side(w[k0 * P:(k0 + 2) * P, (b + 1) * 512:(b + 2) * 512], 2, 512, mod_ring))
                    if late:
                        late.pop()()
                    yield

                def add_rows(b=b, bank=bank, flat=flat, sums=sums, acc=acc, done=done):
                    for j in range(4):
                        at = 4 * (b % 6) + j
                        turned = mm(flat[:, at:at + 1], acc[:, j * P:(j + 1) * P], ones[:, 0:1], True, True, done,
                                    bank.free)
                    sums.release(turned)
                    if b % 6 == 5:
                        half = b // 6
                        o = mod[:, l, half * 24:half * 24 + 24]
                        w1 = tt(ve, o, flat[:, 0:24], v2(l, "b_ada", half * 24, 24), ALU.add, turned)
                        bank.release(w1)
                        scale = mod[:, l, half * 24 + 8:half * 24 + 16]
                        mod_ready[l] = stt(scale, scale, 1.0, v2(l, "norm2" if half else "norm1", 0, 8), ALU.add,
                                           ALU.mult, w1)
                late.append(add_rows)
            yield
            late.pop()()

        def softmax_rows(ps, done, nk, scale, mask, tag):
            st = stat.take()
            p = prob.take()
            mx, nm, sm, rs = (st.mem[:, 2 * j:2 * j + 2] for j in range(4))
            if mask is None:
                w = ve.do(lambda e: e.tensor_reduce(mx, ps.mem[:, :, :], AX.X, ALU.max), done, st.free)
                src = ps.mem
            else:
                src = p.mem
                for t in range(TT):
                    n = nk[t]
                    w = ve.do(lambda e, t=t, n=n: e.tensor_tensor_reduce(
                        out=p.mem[:, t, 0:n], in0=ps.mem[:, t, 0:n], in1=mask[:, t, 0:n], scale=1.0,
                        scalar=-3.0e38, op0=ALU.add, op1=ALU.max, accum_out=mx[:, t:t + 1]),
                        done, st.free, p.free)
                ps.release(w)
            w = ts(ve, nm, mx, -scale, None, ALU.mult, None, w)
            for t in range(TT):
                n = nk[t]
                w2 = act(p.mem[:, t, 0:n], src[:, t, 0:n], ACT.Exp, w, p.free, bias=nm[:, t:t + 1], scale=scale,
                         acc=sm[:, t:t + 1])
            if mask is None:
                ps.release(w2)
            w = recip(rs, sm, w2)
            for t in range(TT):
                n = nk[t]
                w3 = ts(po, p.mem[:, t, 0:n], p.mem[:, t, 0:n], rs[:, t:t + 1], None, ALU.mult, None, w, w2)
            st.release([w3, w2])
            return p, w3

        def attend(heads, scores, nk, scale, mask, v_of, out_of, out_free, result):
            live = {}
            pair = {}
            for i in range(heads + 2):
                if i < heads:
                    ps = small_ps.take()
                    pe.wait(ps.free)
                    done = scores(i, ps.mem)
                    live[i] = softmax_rows(ps, done, nk, scale, mask, i)
                    yield
                if 1 <= i <= heads:
                    p, normed = live.pop(i - 1)
                    ps = small_ps.take()
                    pe.wait(ps.free, normed)
                    for kt in range(TT):
                        for t in range(TT):
                            if kt * P >= nk[t]:
                                continue
                            turned = tr(ps.mem[:, kt, t * P:(t + 1) * P], p.mem[:, t, kt * P:(kt + 1) * P], ident,
                                        mark=kt == 1 and t == 1)
                    p.release(turned)
                    pt = probT.take()
                    if nk[0] == S:
                        w = act(pt.mem[:, :, :], ps.mem[:, :, :], ACT.Copy, turned, pt.free)
                    else:
                        act(pt.mem[:, 0, :], ps.mem[:, 0, :], ACT.Copy, turned, pt.free)
                        w = act(pt.mem[:, 1, P:S], ps.mem[:, 1, P:S], ACT.Copy)
                    ps.release(w)
                    live[("t", i - 1)] = (pt, w)
                if 2 <= i:
                    h = i - 2
                    pt, w = live.pop(("t", h))
                    r0 = 64 * (h % 2)
                    if h % 2 == 0:
                        pair["o"] = small_ps.take()
                        pe.wait(pair["o"].free)
                    o = pair["o"]
                    q0 = 0 if nk[0] == S else P
                    mm(o.mem[r0:r0 + 64, 0, :], v_of(h, 0), pt.mem[:, 0, :], True, False, w)
                    done = mm(o.mem[r0:r0 + 64, 0, q0:S], v_of(h, 1), pt.mem[:, 1, q0:S], False, True)
                    pt.release(done)
                    if h % 2:
                        w = split(ve, o.mem[:, 0, :], *out_of(h // 2), done, out_free)
                        o.release(w)
                        result.append(w)
                    yield

        hid_free = None

        def scaled_sink(y, total, gain, *free):
            def sink(i, ps, done):
                w = total.add(ps[:, :, :], ac, done)
                for j in range(2):
                    t = 2 * i + j
                    last = ts(ve, y[:, t, :], ps[:, j, :], gain(t), None, ALU.mult, None, w, *free)
                return last
            return sink

        def add_normed(y, total, x_tok):
            rs, w = total.close(D)
            out = []
            squares = SquareSum(DT)
            for i in range(DT // 2):
                pair = slice(2 * i, 2 * i + 2)
                w2 = tt(ve, y[:, pair, :], y[:, pair, :], both(rs), ALU.mult, w)
                w3 = tt(po if i == 1 else ve, xres[:, pair, :], xres[:, pair, :], y[:, pair, :], ALU.add, w2, x_tok)
                out += [w3, w3]
            for i in range(DT // 2):
                squares.add(xres[:, 2 * i:2 * i + 2, :], ac, out[2 * i])
            total.release(w2)
            return out, squares

        x_ready = [x_in] * DT
        ac.wait(x_in)
        pe.wait(x_in)
        tables_steps = rotary([0, 1], 0, tables)
        next(tables_steps)
        x_squares = SquareSum(DT)
        for i in range(DT // 2):
            x_squares.add(xres[:, 2 * i:2 * i + 2, :], ac, x_in)
        for q in (pe, ve, ac, po):
            q.wait(inputs)

        for l in range(DEPTH):
            w_in = A["w_in"][l]
            qm, km = region(4096, HEADS, S), region(6144, HEADS, S)
            gate = [region(4096, DT, S), region(6144, DT, S)]
            cq, ckv, vmla = region(8192, 2, S), region(8704, S), region(8960, TT, 512)
            gbuf = region(10240, DT, S)
            ret_p = parts(8192, 10240, DT)
            omla_p = parts(12288, 13312, 4)
            conv_a, conv_g, conv_y = region(14336, 4, S), region(15360, 4, S), region(16384, 4, S)
            conv_p = parts(14336, 15360, 4)
            rq, rk = region(17408, RET_H, S), region(18432, RET_H, S)
            vret = region(19456, TT, RET_H * RET_DV)
            merged = region(21504, DT, S)

            normed = norm_residual(x_squares, lambda t: v1(l, "mix_pre", t), None, hid_free,
                                   None if l else tables_steps)

            gate_ready = [[None] * 4 for _ in range(3)]

            def gate_sink(branch):
                def sink(i, ps, done):
                    g = gate[branch % 2]
                    gate_ready[branch][i] = act(g[:, 2 * i:2 * i + 2, :], ps[:, :, :], ACT.Sigmoid, done,
                                                gate_free[branch])
                    return gate_ready[branch][i]
                return sink

            gate_free = [None, None, None]
            conv_in = [None] * 4

            def conv_gate_sink(i, ps, done):
                conv_in[i] = act(conv_g[:, 2 * i:2 * i + 2, :], ps[:, :, :], ACT.Sigmoid, done)
                return conv_in[i]

            conv_ready = [None] * 4

            def conv_a_sink(i, ps, done):
                w = tt(ve, conv_a[:, 2 * i:2 * i + 2, :], ps[:, :, :], conv_g[:, 2 * i:2 * i + 2, :], ALU.mult,
                       done, conv_in[i])
                conv_ready[2 * i] = conv_ready[2 * i + 1] = w
                return w

            def to(dst, out, copy=ACT.Copy):
                def sink(i, ps, done):
                    w = act(dst[:, 2 * i:2 * i + 2, :], ps[:, :, :], copy, done)
                    out.append(w)
                    return w
                return sink

            rq_raw, rk_raw, rg_ready, vret_ready = [], [], [], []

            def vret_sink(i, ps, done):
                w = act(vret[:, :, i * 256:(i + 1) * 256], ps[:, :, :], ACT.Copy, done)
                vret_ready.append(w)
                return w

            def fill():
                yield from linear(w_in, [C_CONV + CONV_CH, C_CONV + CONV_CH + 256], hid_k, normed, conv_gate_sink)
                yield from linear(w_in, [C_CONV, C_CONV + 256], hid_k, normed, conv_a_sink)
                yield from linear(w_in, [C_RQ, C_RQ + 256], hid_k, normed, to(rq, rq_raw))
                yield from linear(w_in, [C_RK, C_RK + 256], hid_k, normed, to(rk, rk_raw))
                yield from linear_tokens(w_in, [C_RV + 256 * i for i in range(4)], hid_kt, normed, vret_sink)
                yield from linear(w_in, [C_RG + 256 * i for i in range(4)], hid_k, normed, to(gbuf, rg_ready, ACT.Silu))

            filler = fill()
            def take_cq(i, ps, done):
                return act(cq[:, :, :], ps[:, :, :], ACT.Copy, done)
            run(linear(w_in, [C_Q], hid_k, normed, take_cq))
            cq_raw = (ac.sem, ac.count)
            if l == 0:
                load_tables()
                run(tables_steps)
                silu_c = act(cact[:, :], ccol[:, :], ACT.Silu)

            kpe = tmp.take()

            def take_ckv(i, ps, done):
                act(ckv, ps[:, 0, :], ACT.Copy, done)
                return act(kpe.mem[64:96, 0, :], ps[64:96, 1, :], ACT.Copy, kpe.free)
            run(linear(w_in, [C_KV], hid_k, normed, take_ckv, blocks=(0, 64), width=192))
            ckv_raw = kpe_raw = (ac.sem, ac.count)

            q_total, kv_total = SquareSum(2), SquareSum(1)
            q_total.add(cq, ac, cq_raw)
            kv_total.add(ckv.unsqueeze(1), ac, ckv_raw)
            next(filler)
            total = q_total
            rs, w = total.close(Q_RANK)
            for t in range(2):
                cq_n = stt(cq[:, t, :], cq[:, t, :], v1(l, "q_norm", t), rs, ALU.mult, ALU.mult, w)
            total.release(cq_n)
            total = kv_total
            rs, w = total.close(KV_RANK)
            ckv_n = stt(ckv, ckv, v1(l, "kv_norm"), rs, ALU.mult, ALU.mult, w)
            total.release(ckv_n)

            next(filler)
            rot96 = cn("rot96", ROPE, 64)[:, 64:96]
            ps = small_ps.take()
            turned = mm(ps.mem[64:96, 0, :], rot96, kpe.mem[64:96, 0, :], True, True, ps.free, kpe_raw)
            cos, sin = rope_cs[64:96, 0, :], rope_cs[64:96, 1, :]
            t1 = tmp.take()
            w1 = tt(ve, t1.mem[64:96, 0, :], ps.mem[64:96, 0, :], sin, ALU.mult, turned, t1.free, tables)
            ps.release(w1)
            w2 = tt(ve, t1.mem[64:96, 1, :], kpe.mem[64:96, 0, :], cos, ALU.mult, kpe_raw)
            w = tt(ve, t1.mem[64:96, 0, :], t1.mem[64:96, 0, :], t1.mem[64:96, 1, :], ALU.add, w1, w2)
            kpe_in = act(km[64:96, :, :], t1.mem[64:96, 0:1, :].to_broadcast([ROPE, HEADS, S]), ACT.Copy, w)
            kpe.release(kpe_in)
            t1.release(kpe_in)

            uq = [load_side(A["w_uq"][l][k * P:(k + 1) * P, :], 1, HEADS * QK, side) for k in range(2)]
            pe.wait(cq_n, uq[0][2], uq[1][2])
            q_ready = [None] * 4
            for j in range(4):
                ps = small_ps.take()
                pe.wait(ps.free)
                for i in range(2):
                    h = 2 * j + i
                    for k in range(2):
                        done = mm(ps.mem[0:QK, i, :], uq[k][1][:, 0, h * QK:(h + 1) * QK], cq[:, k, :], k == 0, k == 1)
                w = act(qm[0:QK, 2 * j:2 * j + 2, :], ps.mem[0:QK, :, :], ACT.Copy, done)
                ps.release(w)
                q_ready[j] = w
            for s in uq:
                s[0].release(done)
            next(filler)
            for j in range(4):
                q_ready[j] = rotate(qm[64:96, 2 * j:2 * j + 2, :], ROPE, 64, rot96, 0, q_ready[j])

            slot, view, landed = load_side(A["w_ukv"][l], 1, HEADS * (NOPE + VDIM), side)
            pe.wait(landed, ckv_n)
            k_ready = [None] * 4
            for j in range(4):
                ps = small_ps.take()
                pe.wait(ps.free)
                for i in range(2):
                    h = 2 * j + i
                    done = mm(ps.mem[0:NOPE, i, :], view[:, 0, h * P:h * P + NOPE], ckv, True, True)
                k_ready[j] = act(km[0:NOPE, 2 * j:2 * j + 2, :], ps.mem[0:NOPE, :, :], ACT.Copy, done)
                ps.release(k_ready[j])
            wv = view[:, 0, :].rearrange("p (h c) -> p h c", h=HEADS)[:, :, NOPE:]
            for t in range(TT):
                ps = small_ps.take()
                done = mm(ps.mem[:, :, :].rearrange("p a b -> p (a b)"), ckv[:, t * P:(t + 1) * P], wv, True, True,
                          ps.free)
                v_ready = act(vmla[:, t, :], ps.mem[:, :, :].rearrange("p a b -> p (a b)"), ACT.Copy, done)
                ps.release(v_ready)
            slot.release(done)

            def mla_scores(h, out):
                pe.wait(q_ready[h // 2], k_ready[h // 2], kpe_in, v_ready)
                for t in range(TT):
                    done = mm(out[:, t, :], qm[0:QK, h, t * P:(t + 1) * P], km[0:QK, h, :], True, True)
                return done

            o_ready = []
            mla = attend(HEADS, mla_scores, [S, S], QK ** -0.5, None,
                         lambda h, kt: vmla[:, kt, h * 64:(h + 1) * 64], lambda j: (omla_p[0][:, j, :], omla_p[1][:, j, :]), None, o_ready)

            def conv_steps():
                half = CONV_W // 2
                for pair in ((0, 1), (2, 3)):
                    w = {t: ts(ve, conv_y[:, t, :], conv_a[:, t, :], v1(l, "conv_w", half * 4 + t),
                               v1(l, "conv_b", t), ALU.mult, ALU.add, conv_ready[t]) for t in pair}
                    for j in range(CONV_W):
                        s = j - half
                        if s == 0:
                            continue
                        lo, hi = max(0, -s), min(S, S - s)
                        for t in pair:
                            w[t] = stt(conv_y[:, t, lo:hi], conv_a[:, t, lo + s:hi + s], v1(l, "conv_w", j * 4 + t),
                                       conv_y[:, t, lo:hi], ALU.mult, ALU.add, w[t])
                        if j % 2:
                            yield
                    conv_done.extend([w[pair[0]], w[pair[1]]])
                    yield

            conv_done = []
            conv = conv_steps()
            lg, lg_ready = small[:, 0:8], []

            def decay_steps():
                x, e, neg = v1(l, "decay", 0, 8), small[:, 8:16], small[:, 16:24]
                w = ts(ve, neg, x, -1.0, None, ALU.mult, None)
                w = tt(ve, neg, neg, x, ALU.min, w)
                w = act(e, neg, ACT.Exp, w)
                yield
                done = []
                yield from log1p(w, e, (P, 8), done)
                lg_ready.append(stt(lg, x, 0.0, e, ALU.min, ALU.subtract, done))

            decay = decay_steps()
            weave(mla, (filler, 0.55), (conv, 0.9), (decay, 0.6))
            run(decay)
            qk_read = (pe.sem, pe.count)
            gate_free = [qk_read, qk_read, None]

            merged_ready = [None] * 4

            def first_branch(i, ps, done):
                w = tt(ve, merged[:, 2 * i:2 * i + 2, :], ps[:, :, :], gate[0][:, 2 * i:2 * i + 2, :], ALU.mult,
                       done, gate_ready[0][i])
                merged_ready[i] = w
                return w

            def next_branch(branch):
                def sink(i, ps, done):
                    t = tmp.take()
                    w = tt(ve, t.mem[:, :, :], ps[:, :, :], gate[branch % 2][:, 2 * i:2 * i + 2, :], ALU.mult,
                           done, gate_ready[branch][i], t.free)
                    m = merged[:, 2 * i:2 * i + 2, :]
                    merged_ready[i] = tt(po, m, m, t.mem[:, :, :], ALU.add, w, merged_ready[i])
                    t.release(merged_ready[i])
                    return w
                return sink

            branch_cols = [256 * i for i in range(4)]

            def conv_norm():
                ps = small_ps.take()
                for t in range(4):
                    w = mm(ps.mem[:, 0, :], ones, conv_y[:, t, :], t == 0, t == 3, ps.free, conv_done[t])
                mu = tmp.take()
                w = act(mu.mem[:, 0, :], ps.mem[:, 0, :], ACT.Copy, w, mu.free, scale=1.0 / CONV_CH)
                ps.release(w)
                centred = [tt(ve, conv_y[:, t, :], conv_y[:, t, :], mu.mem[:, 0, :], ALU.subtract, w)
                           for t in range(4)]
                yield
                mu.release(centred)
                total, rs, w = mean_square([(conv_y[:, 0:2, :], centred), (conv_y[:, 2:4, :], centred)], CONV_CH)
                for t in range(4):
                    w1 = stt(conv_y[:, t, :], conv_y[:, t, :], v1(l, "conv_g", t), rs, ALU.mult, ALU.mult, w)
                    w2 = act(conv_y[:, t, :], conv_y[:, t, :], ACT.Silu, w1, bias=v1(l, "conv_beta", t))
                    conv_out.append(split(po, conv_y[:, t, :], conv_p[0][:, t, :], conv_p[1][:, t, :], w2))
                total.release(w1)
                yield

            conv_out = []

            def fill2():
                yield from linear(w_in, [C_GATE + 256 * i for i in range(4)], hid_k, normed, gate_sink(0))
                yield from linear(w_in, [C_GATE + D + 256 * i for i in range(4)], hid_k, normed, gate_sink(1))
                yield from linear(A["w_o"][l], branch_cols, of(omla_p), o_ready, first_branch, kts=4)
                gate_free[2] = merged_ready[3]
                yield from linear(w_in, [C_GATE + 2 * D + 256 * i for i in range(4)], hid_k, normed, gate_sink(2))

            filler = chain(filler, fill2())

            def retention():
                qr = [rotate(rq[:, 2 * j:2 * j + 2, :], P, 0, cn("rot128"), 1, rq_raw[j]) for j in range(2)]
                kr = [rotate(rk[:, 2 * j:2 * j + 2, :], P, 0, cn("rot128"), 1, rk_raw[j]) for j in range(2)]
                yield
                o_norm = {}
                for h in range(RET_H + 1):
                    if h < RET_H:
                        dec = prob.take()
                        flat = dec.mem[:, :, :].rearrange("p a b -> p (a b)")
                        w = ts(ve, flat, cn("ahead"), lg[:, h:h + 1], None, ALU.mult, None, lg_ready, dec.free)
                        w = stt(flat, cn("behind"), lg[:, 4 + h:5 + h], flat, ALU.mult, ALU.add, w)
                        w_dec = act(flat, flat, ACT.Exp, w)
                        ps = small_ps.take()
                        pe.wait(ps.free, qr[h // 2], kr[h // 2])
                        for mt in range(TT):
                            done = mm(ps.mem[:, mt, :], rk[:, h, mt * P:(mt + 1) * P], rq[:, h, :], True, True)
                        w_dec = stt(dec.mem[:, :, :], ps.mem[:, :, :], RET_DK ** -0.5, dec.mem[:, :, :], ALU.mult,
                                    ALU.mult, done, w_dec)
                        ps.release(w_dec)
                        yield
                        o = small_ps.take()
                        pe.wait(o.free, w_dec, vret_ready)
                        for t in range(TT):
                            for mt in range(TT):
                                done = mm(o.mem[:, t, :], dec.mem[:, mt, t * P:(t + 1) * P],
                                          vret[:, mt, h * 256:(h + 1) * 256], mt == 0, mt == 1)
                        dec.release(done)
                        on, st = tmp.take(), stat.take()
                        for t in range(TT):
                            b = st.mem[:, 8 * t:8 * t + 6]
                            w = ve.do(lambda q, b=b, t=t, o=o: q.bn_stats(b, o.mem[:, t, :]), done, st.free)
                            mv = st.mem[:, 8 * t + 6:8 * t + 8]
                            w = ve.do(lambda q, b=b, mv=mv: q.bn_aggr(mv, b), w)
                            var = mv[:, 1:2]
                            w = act(var, var, ACT.Sqrt, w, bias=eps)
                            w = recip(var, var, w)
                            w = ts(ve, on.mem[:, t, :], o.mem[:, t, :], mv[:, 0:1], var, ALU.subtract, ALU.mult, w,
                                   on.free)
                        o.release(w)
                        st.release(w)
                        o_norm[h] = (on, w)
                        yield
                    if h >= 1:
                        on, w = o_norm.pop(h - 1)
                        ps = small_ps.take()
                        pe.wait(ps.free, w)
                        for half in range(2):
                            for t in range(TT):
                                turned = tr(ps.mem[:, half, t * P:(t + 1) * P], on.mem[:, t, half * P:(half + 1) * P],
                                            ident)
                        on.release(turned)
                        gated = tmp.take()
                        for half in range(2):
                            j = 2 * (h - 1) + half
                            w = stt(gated.mem[:, half, :], ps.mem[:, half, :], v1(l, "gn_g", j), gbuf[:, j, :], ALU.mult,
                                    ALU.mult, turned, rg_ready[j // 2], gated.free)
                        ps.release(w)
                        pair = slice(2 * (h - 1), 2 * h)
                        w = split(po, gated.mem[:, :, :], ret_p[0][:, pair, :], ret_p[1][:, pair, :], w)
                        gated.release(w)
                        ret_out[2 * (h - 1)] = ret_out[2 * h - 1] = w
                        yield

            ret_out = [None] * DT
            weave(retention(), (filler, 1.4), (conv, 0.9))
            weave(filler, (conv, 2.0))
            run(conv)
            weave(linear(A["w_ro"][l], branch_cols, of(ret_p), ret_out, next_branch(2)), (conv_norm(), 1.0))

            merged_in = []
            hid_read = (pe.sem, pe.count)

            def last_branch(i, ps, done):
                w = next_branch(1)(i, ps, done)
                pair = slice(2 * i, 2 * i + 2)
                m = split(ve, merged[:, pair, :], hid[0][:, pair, :], hid[1][:, pair, :], merged_ready[i], hid_read)
                merged_in.extend([m, m])
                return w
            run(linear(A["w_pw"][l], branch_cols, of(conv_p), conv_out, last_branch, kts=4))

            y = gate[0]
            total = SquareSum(DT)
            run(linear(A["w_out"][l], branch_cols, hid_k, merged_in,
                       scaled_sink(y, total, lambda t: v1(l, "mix_post", t), merged_ready)))
            x_ready, x_squares = add_normed(y, total, x_ready)

            hid_free = (pe.sem, pe.count)
            normed = norm_residual(x_squares, lambda t: v1(l, "ffn_pre", t), None, hid_free)
            f_p = parts(4096, 4096 + 22 * S, 22)
            f_ready = [None] * (FFN // P)
            held = {}

            def gate_half(i, ps, done):
                s = tmp.take()
                w = act(s.mem[:, :, :], ps[:, :, :], ACT.Silu, done, s.free)
                held[i] = (s, w)
                return w

            def up_half(i, ps, done):
                s, w = held.pop(i)
                w2 = tt(ve, s.mem[:, :, :], ps[:, :, :], s.mem[:, :, :], ALU.mult, done, w)
                pair = slice(2 * i, 2 * i + 2)
                w3 = split(po, s.mem[:, :, :], f_p[0][:, pair, :], f_p[1][:, pair, :], w2, x_ready)
                s.release(w3)
                f_ready[2 * i] = f_ready[2 * i + 1] = w3
                return w2

            gs = linear(A["w_gate"][l], [256 * i for i in range(11)], hid_k, normed, gate_half)
            us = linear(A["w_up"][l], [256 * i for i in range(11)], hid_k, normed, up_half)
            mod_steps = modulation(l, x_ready, silu_c)

            def gate_and_up():
                for _ in range(11):
                    next(gs)
                    yield
                    next(us)
                    yield
            weave(gate_and_up(), (mod_steps, 1.7))
            hid_free = (pe.sem, pe.count)
            y = region(15360, DT, S)
            if l == DEPTH - 1:
                tables = []
                run(rotary([2], 1, tables))
            total = SquareSum(DT)
            weave(linear(A["w_down"][l], branch_cols, of(f_p), f_ready,
                         scaled_sink(y, total, lambda t: v1(l, "ffn_post", t)), kts=22), (mod_steps, 3.0))
            run(mod_steps)
            x_ready, x_squares = add_normed(y, total, x_ready)

        for l in range(DEPTH):
            w_in = A["w_in2"][l]
            q2, k2, v2t = region(4096, DT, S), region(6144, DT, S), region(8192, TT, D)
            iq, ik = region(10240, 4, S), region(11264, S)
            score = region(11520, TT, S)
            keep = region(12288, TT, S)
            xbc = region(12800, 24, S)
            zbuf = region(18944, 16, S)
            cbm = region(23040, SG, 384)
            o_p = parts(4096, 10240, DT)
            xtok = region(6144, TT, D_IN)
            dts = side.slots[0].mem[:, 0:2 * S].rearrange("p (a b) -> p a b", a=2)
            y_p = parts(18944, 12800, 16)
            mixed = region(16896, DT, S)
            gmb = region(4096, DT, S)

            def hshift(half):
                return lambda t: mod[:, l, half * 24 + t:half * 24 + t + 1]

            def hscale(half):
                return lambda t: mod[:, l, half * 24 + 8 + t:half * 24 + 9 + t]

            def hgate(half, t):
                return mod[:, l, half * 24 + 16 + t:half * 24 + 17 + t]

            ve.wait(mod_ready[l])
            hid_free = (pe.sem, pe.count)
            ac.wait(mod_ready[l])
            normed = norm_residual(x_squares, hscale(0), hshift(0), hid_free)
            spread = region(18944, 16, P)
            po.wait(x_ready)
            spread_loads.loads += 1
            po.ops.append(lambda e, o=spread: e.dma_start(
                o[0:32, :, :], A["spread"].rearrange("k (t m) -> k t m", t=16)).then_inc(spread_loads.sem, 16))
            spread_landed = (spread_loads.sem, 16 * spread_loads.loads)

            heads_ps = small_ps.take()
            pe.wait(heads_ps.free)
            squares, qk_raw = [], []

            def qk_sink(dst):
                def sink(i, ps, done):
                    x = dst[:, 2 * i:2 * i + 2, :]
                    raw = act(x, ps[:, :, :], ACT.Copy, done, x_ready)
                    sq = tmp.take()
                    squares.append((sq, tt(po, sq.mem[:, :, :], x, x, ALU.mult, raw, sq.free)))
                    qk_raw.append(raw)
                    return raw
                return sink

            def sum_squares():
                n = summed[0]
                sq, w = squares.pop(0)
                for i in range(2):
                    a = 31 - 2 * (2 * n + i)
                    done = mm(heads_ps.mem[0:32, 0, :], cn("to_row")[:, a:a + 32], sq.mem[:, i, :], n == 0 and i == 0,
                              n == 7 and i == 1, w, mark=i == 1)
                sq.release(done)
                summed[0] += 1
                return done

            summed = [0]
            for st in (linear(w_in, [C2_Q + 256 * i for i in range(4)], hid_k, normed, qk_sink(q2)),
                       linear(w_in, [C2_K + 256 * i for i in range(4)], hid_k, normed, qk_sink(k2))):
                for _ in st:
                    if len(squares) > 1:
                        sum_squares()
            iq_raw, iq_ready = [], []
            idx = linear(w_in, [C2_IQ, C2_IQ + 256], hid_k, normed, to(iq, iq_raw))
            next(idx)
            all_summed = sum_squares()
            hr = tmp.take()
            root = act(hr.mem[0:32, 0, :], heads_ps.mem[0:32, 0, :], ACT.Sqrt, all_summed, hr.free, scale=1.0 / HD,
                       bias=eps[0:32, :])
            heads_ps.release(root)
            head_rstd = recip(hr.mem[0:32, 0, :], hr.mem[0:32, 0, :], root)
            run(idx)
            q_ready, k_ready = [None] * 4, [None] * 4

            def norm_heads():
                for n in (0, 4, 1, 5, 2, 6, 3, 7):
                    dst, gain, out = (q2, v2(l, "qn"), q_ready) if n < 4 else (k2, v2(l, "kn"), k_ready)
                    i = n % 4
                    x = dst[:, 2 * i:2 * i + 2, :]
                    ps = small_ps.take()
                    for j in range(2):
                        t = 2 * n + j
                        done = mm(ps.mem[:, j, :], spread[0:32, t, :], hr.mem[0:32, 0, :], True, True, ps.free,
                                  head_rstd, spread_landed)
                    w = stt(x, x, gain, ps.mem[:, :, :], ALU.mult, ALU.mult, done, qk_raw[n])
                    ps.release(w)
                    yield
                    out[i] = rotate(x, P, 0, cn("rot64"), 0, w)
                hr.release(done)

            v_ready, z_ready = [], []
            xbc_raw, xbc_ready = [None] * 24, [None] * 24

            def v_sink(i, ps, done):
                w = act(v2t[:, :, i * 256:(i + 1) * 256], ps[:, :, :], ACT.Copy, done)
                v_ready.append(w)
                return w

            def xbc_sink(i, ps, done):
                raw = tmp.take()
                w0 = act(raw.mem[:, :, :], ps[:, :, :], ACT.Copy, done, raw.free)
                for j in range(2):
                    c = 2 * i + j
                    y = xbc[:, c, :]
                    w1 = act(y, ps[:, j, :], ACT.Identity, bias=v2(l, "conv_b", c), scale=v2(l, "conv_w", 3 * 24 + c))
                    w = [w0, w1]
                    for tap in (2, 1, 0):
                        s = 3 - tap
                        w = stt(y[:, s:S], raw.mem[:, j, 0:S - s], v2(l, "conv_w", tap * 24 + c), y[:, s:S],
                                ALU.mult, ALU.add, w)
                    last = w
                    xbc_raw[c] = last
                raw.release(last)
                return w1

            def fill():
                yield from linear_tokens(w_in, [C2_V + 256 * i for i in range(4)], hid_kt, normed, v_sink)
                yield from linear(w_in, [C2_XBC + 256 * i for i in range(12)], hid_k, normed, xbc_sink)

            filler = fill()
            ikr = tmp.take()

            def take_ik(i, ps, done):
                return act(ikr.mem[0:ID + IH, 0, :], ps[0:ID + IH, 0, :], ACT.Copy, done, ikr.free)
            run(linear(w_in, [C2_IK], hid_k, normed, take_ik, blocks=(0,), width=P))
            ik_raw = (ac.sem, ac.count)
            next(filler)
            ps = small_ps.take()
            pe.wait(ps.free, ik_raw)
            for t in range(TT):
                done = tr(ps.mem[:, 0, t * IH:(t + 1) * IH], ikr.mem[ID:ID + IH, 0, t * P:(t + 1) * P],
                          ident[ID:ID + IH, ID:ID + IH])
            iw = small[:, 32:32 + TT * IH]
            iw_ready = act(iw, ps.mem[:, 0, 0:TT * IH], ACT.Copy, done)
            ps.release(iw_ready)
            ps = small_ps.take()
            pe.wait(ps.free, ik_raw)
            mm(ps.mem[:, 0, :], cn("dup", ID), ikr.mem[0:ID, 0, :], True, True)
            done = mm(ps.mem[:, 1, :], cn("rotdup", ID), ikr.mem[0:ID, 0, :], True, True)
            ikr.release(done)
            t1 = tmp.take()
            w = tt(ve, t1.mem[:, :, :], ps.mem[:, :, :], rope_cs[:, 0:2, :], ALU.mult, done, t1.free)
            ps.release(w)
            ik_ready = tt(ve, ik, t1.mem[:, 0, :], t1.mem[:, 1, :], ALU.add, w)
            t1.release(ik_ready)
            next(filler)
            for j in range(2):
                iq_ready.append(rotate(iq[:, 2 * j:2 * j + 2, :], P, 0, cn("rot64"), 0, iq_raw[j]))

            norm_heads_steps = norm_heads()

            def select():
                for t in range(TT):
                    n = (t + 1) * P
                    acc = score[:, t, 0:n]
                    w = None
                    for j in range(4):
                        half, pair = j // 2, j % 2
                        r0 = 64 * half
                        ps = small_ps.take()
                        pe.wait(ps.free, iq_ready[pair], ik_ready)
                        for i in range(2):
                            done = mm(ps.mem[:, i, 0:n], iq[r0:r0 + 64, 2 * pair + i, t * P:(t + 1) * P],
                                      ik[r0:r0 + 64, 0:n], True, True)
                        r = tmp.take()
                        pos = act(r.mem[:, :, 0:n], ps.mem[:, :, 0:n], ACT.Relu, done, r.free)
                        ps.release(pos)
                        for i in range(2):
                            head = 4 * pair + 2 * i + half
                            weight = iw[:, t * IH + head:t * IH + head + 1]
                            if j == 0 and i == 0:
                                w = ts(ve, acc, r.mem[:, i, 0:n], weight, None, ALU.mult, None, pos, iw_ready)
                            else:
                                w = stt(acc, r.mem[:, i, 0:n], weight, acc, ALU.mult, ALU.add, pos, w)
                        r.release(w)
                        if j % 2:
                            yield
                    w = ts(ve, acc, acc, IDX_SCALE, 0.0, ALU.mult, ALU.add, w)

                    def causal(ap, w, t=t, n=n):
                        return po.do(lambda e: e.affine_select(
                            out=ap, in_=ap, pattern=[[-1, n]], compare_op=ALU.is_ge, fill=NOT_KEPT, base=t * P,
                            channel_multiplier=1), w)
                    w = causal(acc, w)
                    st = stat.take()
                    best = st.mem[:, 0:8]
                    for _ in range(KEEP // 8):
                        w = ve.do(lambda e, acc=acc, best=best: e.max(best, acc), w, st.free)
                        w = ve.do(lambda e, acc=acc, best=best: e.match_replace(acc, best, acc, TAKEN), w)
                    st.release(w)
                    kp = keep[:, t, 0:n]
                    w = ts(ve, kp, acc, TAKEN, -NOT_KEPT, ALU.is_equal, ALU.mult, w)
                    w = ts(ve, kp, kp, NOT_KEPT, None, ALU.add, None, w)
                    keep_ready.append(causal(kp, w))
                    yield

            keep_ready = []
            weave(select(), (norm_heads_steps, 1.0), (filler, 1.0))
            run(norm_heads_steps)

            def scores2(h, out):
                j, r0 = h // 2, 64 * (h % 2)
                pe.wait(q_ready[j // 2], k_ready[j // 2], v_ready)
                ve.wait(keep_ready)
                for t in range(TT):
                    n = (t + 1) * P
                    done = mm(out[:, t, 0:n], q2[r0:r0 + 64, j, t * P:(t + 1) * P], k2[r0:r0 + 64, j, 0:n], True, True)
                return done

            dtmp = tmp.take()
            u, e_ = dtmp.mem[0:SH, 0, :], dtmp.mem[0:SH, 1, :]
            dt_, cs = dts[0:SH, 0, :], dts[0:SH, 1, :]
            ncs, dtT = small[:, 80:80 + 2 * SH], small[:, 80 + 2 * SH:80 + 4 * SH]
            ncs_ready, dtT_ready = [], []

            def take_dt(i, ps, done):
                return ts(ve, u, ps[0:SH, 0, :], v2(l, "dt_bias", rows=SH), None, ALU.add, None, done, dtmp.free)

            def dt_steps():
                w = (ve.sem, ve.count)
                w = ts(ve, e_, u, -1.0, None, ALU.mult, None, w)
                w = tt(ve, e_, e_, u, ALU.min, w)
                w = act(e_, e_, ACT.Exp, w)
                acol = small[0:SH, 64:65]
                wa = act(acol, v2(l, "a_log", rows=SH), ACT.Exp)
                yield
                done = []
                yield from log1p(w, e_, (SH, S), done)
                dt_ready = stt(dt_, u, 0.0, e_, ALU.max, ALU.add, done)
                w = ts(ve, u, dt_, acol, -1.0, ALU.mult, ALU.mult, dt_ready, wa)
                cs_ready = ve.do(lambda e, cs=cs, u=u: e.tensor_tensor_scan(
                    cs, ones[0:SH, 0:1].to_broadcast([SH, S]), u, 0.0, ALU.mult, ALU.add), w)
                dtmp.release(cs_ready)
                yield
                ps = small_ps.take()
                pe.wait(ps.free, cs_ready)
                for t in range(TT):
                    tr(ps.mem[:, 0, t * SH:(t + 1) * SH], cs[:, t * P:(t + 1) * P], ident[0:SH, 0:SH], mark=False)
                    done = tr(ps.mem[:, 0, (2 + t) * SH:(3 + t) * SH], dt_[:, t * P:(t + 1) * P], ident[0:SH, 0:SH])
                ncs_ready.append(act(ncs, ps.mem[:, 0, 0:2 * SH], ACT.Copy, done, scale=-1.0))
                dtT_ready.append(act(dtT, ps.mem[:, 0, 2 * SH:4 * SH], ACT.Copy))
                ps.release(dtT_ready)

            o_ready = []
            while len(v_ready) < 4:
                next(filler)
            run(linear(w_in, [C2_DT], hid_k, normed, take_dt, blocks=(0,), width=P))
            dt_chain = dt_steps()
            weave(attend(AH, scores2, [P, S], HD ** -0.5, keep, lambda h, kt: v2t[:, kt, h * 64:(h + 1) * 64],
                         lambda j: (o_p[0][:, j, :], o_p[1][:, j, :]), None, o_ready), (filler, 0.34), (dt_chain, 0.4))
            run(dt_chain)
            run(filler)
            attention_read = (pe.sem, pe.count)
            z_raw = []
            z_steps = linear(w_in, [C2_Z + 256 * i for i in range(8)], hid_k, normed, to(zbuf, z_raw))
            for n, c in enumerate((16, 20, 18, 22, 0, 2, 4, 6, 8, 10, 12, 14)):
                y = xbc[:, c:c + 2, :]
                xbc_ready[c] = xbc_ready[c + 1] = act(y, y, ACT.Silu, xbc_raw[c], xbc_raw[c + 1])
                if n % 4 == 3:
                    next(z_steps)

            cb_ready = []
            for g in range(SG):
                ps = small_ps.take()
                flat = ps.mem[:, :, :].rearrange("p a b -> p (a b)")
                b, c = xbc[:, 16 + g, :], xbc[:, 20 + g, :]
                pe.wait(ps.free, xbc_ready[16 + g], xbc_ready[20 + g])
                mm(flat[:, 0:S], b[:, 0:P], c, True, True)
                done = mm(flat[:, S:S + P], b[:, P:S], c[:, P:S], True, True)
                w = tt(ve, cbm[:, g, :], flat[:, 0:384], cn("tri"), ALU.mult, done)
                ps.release(w)
                cb_ready.append(w)

            xtok_ready = []
            for j in range(8):
                ps = small_ps.take()
                pe.wait(ps.free)
                for t in range(TT):
                    for i in range(2):
                        turned = tr(ps.mem[:, t, i * P:(i + 1) * P], xbc[:, 2 * j + i, t * P:(t + 1) * P], ident,
                                    xbc_ready[2 * j + i])
                for t in range(TT):
                    w = tt(ve, xtok[:, t, j * 256:(j + 1) * 256].rearrange("p (h c) -> p h c", h=4),
                           ps.mem[:, t, :].rearrange("p (h c) -> p h c", h=4),
                           dtT[:, t * SH + 4 * j:t * SH + 4 * j + 4].unsqueeze(2).to_broadcast([P, 4, 64]),
                           ALU.mult, turned, dtT_ready, attention_read)
                ps.release(w)
                xtok_ready.append(w)

            z_done = []

            def ssd():
                live = {}
                for h in range(SH + 2):
                    if h < SH:
                        ps = small_ps.take()
                        done = mm(ps.mem[:, 0, :], ident[0:SH, h:h + 1].to_broadcast([SH, P]), cs, True, True, ps.free)
                        g = prob.take()
                        flat = g.mem[:, :, :].rearrange("p a b -> p (a b)")
                        ts(ve, flat[:, 0:S], ps.mem[:, 0, :], ncs[:, h:h + 1], 0.0, ALU.add, ALU.min, done, g.free,
                           ncs_ready)
                        w = ts(ve, flat[:, S:S + P], ps.mem[:, 0, P:S], ncs[:, SH + h:SH + h + 1], 0.0, ALU.add,
                               ALU.min)
                        ps.release(w)
                        w = act(flat[:, 0:384], flat[:, 0:384], ACT.Exp, w)
                        w = tt(po, flat[:, 0:384], flat[:, 0:384], cbm[:, h // 8, :], ALU.mult, w, cb_ready[h // 8])
                        live[h] = (g, flat, w)
                    if h >= 2:
                        hh = h - 2
                        g, flat, w = live.pop(hh)
                        r0 = 64 * (hh % 2)
                        if hh % 2 == 0:
                            live["y"] = small_ps.take()
                            pe.wait(live["y"].free)
                        y = live["y"]
                        pe.wait(w, xtok_ready[hh // 4])
                        mm(y.mem[r0:r0 + 64, 0, :], xtok[:, 0, hh * 64:hh * 64 + 64], flat[:, 0:S], True, False)
                        done = mm(y.mem[r0:r0 + 64, 0, P:S], xtok[:, 1, hh * 64:hh * 64 + 64], flat[:, S:S + P], False,
                                  True)
                        g.release(done)
                        if hh % 2:
                            j = hh // 2
                            xs = xbc[:, j, :]
                            w = stt(xs, xs, v2(l, "d_skip", j), y.mem[:, 0, :], ALU.mult, ALU.add, done)
                            y.release(w)
                            x_done.append(w)
                    yield

            x_done = []

            def gate_and_norm():
                for i in range(8):
                    pair = slice(2 * i, 2 * i + 2)
                    z = zbuf[:, pair, :]
                    w = act(z, z, ACT.Silu, z_raw[i])
                    z_done.extend([tt(po if i % 2 else ve, z, z, xbc[:, pair, :], ALU.mult, w, x_done)] * 2)
                yield
                for g in range(SG):
                    total, rs, w = mean_square([(zbuf[:, c:c + 2, :], z_done[c]) for c in (4 * g, 4 * g + 2)], 512)
                    yield
                    for i in (2 * g, 2 * g + 1):
                        t = tmp.take()
                        for j in range(2):
                            w2 = stt(t.mem[:, j, :], zbuf[:, 2 * i + j, :], v2(l, "ssm_norm", 2 * i + j),
                                     rs, ALU.mult, ALU.mult, w, t.free)
                        pair = slice(2 * i, 2 * i + 2)
                        w3 = split(po, t.mem[:, :, :], y_p[0][:, pair, :], y_p[1][:, pair, :], w2, z_done[2 * i])
                        t.release(w3)
                        y_ready2.extend([w3, w3])
                    total.release(w2)
                    yield

            y_ready2 = []
            ga_ready = [None] * 4

            def ga_sink(i, ps, done):
                ga_raw.append(act(mixed[:, 2 * i:2 * i + 2, :], ps[:, :, :], ACT.Copy, done, cb_ready))
                return ga_raw[i]

            ga_raw = []

            def oa_sink(i, ps, done):
                m = mixed[:, 2 * i:2 * i + 2, :]
                mix_ready[i] = tt(ve, m, ps[:, :, :], m, ALU.mult, done, ga_ready[i])
                return mix_ready[i]

            mix_ready = [None] * 4
            gm_ready = [None] * 4

            def gm_sink(i, ps, done):
                gm_ready[i] = act(gmb[:, 2 * i:2 * i + 2, :], ps[:, :, :], ACT.Sigmoid, done, oa_read[0])
                return gm_ready[i]

            oa_read = [None]

            def fill():
                yield from linear(w_in, [C2_GA + 256 * i for i in range(4)], hid_k, normed, ga_sink)
                yield from z_steps

            filler = fill()
            weave(ssd(), (filler, 0.4))
            run(filler)
            for i in range(4):
                m = mixed[:, 2 * i:2 * i + 2, :]
                ga_ready[i] = act(m, m, ACT.Sigmoid, ga_raw[i])
            finish = gate_and_norm()
            weave(linear(A["w_ao"][l], branch_cols, of(o_p), o_ready, oa_sink), (finish, 1.0))
            oa_read[0] = (pe.sem, pe.count)
            weave(linear(w_in, [C2_GM + 256 * i for i in range(4)], hid_k, normed, gm_sink), (finish, 1.0))
            run(finish)

            def os_sink(i, ps, done):
                t = tmp.take()
                w = tt(ve, t.mem[:, :, :], ps[:, :, :], gmb[:, 2 * i:2 * i + 2, :], ALU.mult, done, gm_ready[i], t.free)
                m = mixed[:, 2 * i:2 * i + 2, :]
                mix_ready[i] = tt(ve, m, m, t.mem[:, :, :], ALU.add, w, mix_ready[i])
                t.release(mix_ready[i])
                pair = slice(2 * i, 2 * i + 2)
                x = split(ve, m, hid[0][:, pair, :], hid[1][:, pair, :], mix_ready[i], hid_read)
                mixed_in.extend([x, x])
                return w

            mixed_in = []
            hid_read = (pe.sem, pe.count)
            run(linear(A["w_so"][l], branch_cols, of(y_p), y_ready2, os_sink, kts=16))

            def residual_sink(half, out, total):
                def sink(i, ps, done):
                    for j in range(2):
                        t = 2 * i + j
                        w = stt(xres[:, t, :], ps[:, j, :], hgate(half, t), xres[:, t, :], ALU.mult, ALU.add, done)
                        out.append(w)
                    if total is not None:
                        total.add(xres[:, 2 * i:2 * i + 2, :], ac, w)
                    return w
                return sink
            x_ready = []
            x_squares = SquareSum(DT)
            run(linear(A["w_out2"][l], branch_cols, hid_k, mixed_in, residual_sink(0, x_ready, x_squares)))

            hid_free = (pe.sem, pe.count)
            normed = norm_residual(x_squares, hscale(1), hshift(1), hid_free)
            f_p = parts(4096, 4096 + 22 * S, 22)
            f_ready = [None] * 22
            held = {}

            def conv3(i, ps, done, base, dst_ap, free):
                raw = tmp.take()
                w0 = act(raw.mem[:, :, :], ps[:, :, :], ACT.Copy, done, raw.free)
                for j in range(2):
                    c = base + 2 * i + j
                    y = dst_ap[:, j, :]
                    w1 = act(y, ps[:, j, :], ACT.Identity, free, bias=v2(l, "fconv_b", c),
                             scale=v2(l, "fconv_w", 2 * 44 + c))
                    w = [w0, w1]
                    for tap in (1, 0):
                        s = 2 - tap
                        w = stt(y[:, s:S], raw.mem[:, j, 0:S - s], v2(l, "fconv_w", tap * 44 + c), y[:, s:S],
                                ALU.mult, ALU.add, w)
                raw.release(w)
                return w1, w

            def gate_half(i, ps, done):
                s = prob.take()
                read, w = conv3(i, ps, done, 22, s.mem, s.free)
                held[i] = (s, w)
                while late:
                    late.pop()()
                return read

            late = []

            def val_half(i, ps, done):
                s, gate_done = held.pop(i)
                v = tmp.take()
                read, w = conv3(i, ps, done, 0, v.mem, v.free)
                gated = act(s.mem[:, :, :], s.mem[:, :, :], ACT.Silu, gate_done)

                def finish():
                    both_done = tt(ve, v.mem[:, :, :], v.mem[:, :, :], s.mem[:, :, :], ALU.mult, w, gated)
                    s.release(both_done)
                    pair = slice(2 * i, 2 * i + 2)
                    done = split(po, v.mem[:, :, :], f_p[0][:, pair, :], f_p[1][:, pair, :], both_done, x_ready)
                    v.release(done)
                    f_ready[2 * i] = f_ready[2 * i + 1] = done
                late.append(finish)
                return read

            gs = linear(A["w_up2"][l], [D_FF + 256 * i for i in range(11)], hid_k, normed, gate_half)
            us = linear(A["w_up2"][l], [256 * i for i in range(11)], hid_k, normed, val_half)
            for _ in range(11):
                next(gs)
                next(us)
            late.pop()()
            hid_free = (pe.sem, pe.count)
            out = []
            x_squares = SquareSum(DT) if l < DEPTH - 1 else None
            run(linear(A["w_down2"][l], branch_cols, of(f_p), f_ready, residual_sink(1, out, x_squares), kts=22))
            x_ready = out

        stored = sem("stored")
        sp.wait(x_ready)
        sp.ops.append(lambda e: e.dma_start(A["out"].rearrange("p (t s) -> p t s", t=DT),
                                            xres[:, :, :]).then_inc(stored, 16))
        sp.ops.append(lambda e: e.wait_ge(stored, 16))

        with nc.Block() as block:
            @block.sync
            def _(e):
                sp.play(e)

            @block.tensor
            def _(e):
                pe.play(e)

            @block.scalar
            def _(e):
                ac.play(e)

            @block.vector
            def _(e):
                ve.play(e)

            @block.gpsimd
            def _(e):
                po.play(e)


WEIGHTS = {"w_in": "w_in", "w_uq": "mla_w_uq", "w_ukv": "mla_w_ukv", "w_o": "mla_w_o", "w_pw": "conv_w_pw",
           "w_ro": "ret_w_o", "w_out": "w_out", "w_gate": "ffn_w_gate", "w_up": "ffn_w_up",
           "w_down": "ffn_w_down", "w_ada": "w_ada_2", "w_in2": "w_in_2", "w_ao": "w_attn_o_2",
           "w_so": "w_ssm_o_2", "w_out2": "w_out_2", "w_up2": "w_up_2", "w_down2": "w_down_2"}


def columns(v):
    return np.ascontiguousarray(v.reshape(-1, P).T)


def rows_padded(v):
    out = np.zeros((P, 1), v.dtype)
    out[:v.shape[0], 0] = v
    return out


def kernel(**inputs):
    import concourse.bacc as bacc
    from concourse.bass_utils import run_bass_kernel_spmd

    a = {k: np.asarray(v) for k, v in inputs.items()}
    parts = []
    for l in range(DEPTH):
        parts += [columns(a[n][l]) for n in ("ln_mix_pre", "ln_mix_post", "ln_ffn_pre", "ln_ffn_post", "mla_q_norm",
                                             "mla_kv_norm", "conv_w_dw", "conv_b_dw", "conv_ln_g", "conv_ln_b",
                                             "ret_gn_g")]
        parts.append(np.tile(a["ret_decay_logits"][l].reshape(1, 2 * RET_H), (P, 1)))
    for l in range(DEPTH):
        parts += [columns(a[n][l]) for n in ("b_ada_2", "norm1_g_2", "norm2_g_2")]
        parts += [columns(np.tile(a[n][l], 2)) for n in ("q_norm_g_2", "k_norm_g_2")]
        parts += [columns(a[n][l]) for n in ("ssm_conv_w_2", "ssm_conv_b_2")]
        parts += [rows_padded(a["dt_bias_2"][l]), rows_padded(a["a_log_2"][l])]
        parts += [columns(np.repeat(a["d_skip_2"][l], 64)), columns(a["ssm_norm_g_2"][l]),
                  columns(a["ffn_conv_w_2"][l]), columns(a["ffn_conv_b_2"][l])]
    host = {
        "consts": constants(),
        "spread": spreader(),
        "vectors": np.ascontiguousarray(np.concatenate(parts, 1)),
        "x": np.ascontiguousarray(a["x"][0].T.reshape(DT, P, S).transpose(1, 0, 2).reshape(P, DT * S)),
        "positions": np.ascontiguousarray(
            np.tile(np.concatenate([a["positions"], a["positions_2"]], 1), (P, 1))),
        "c": columns(a["c_2"][0]),
    }
    for name, source in WEIGHTS.items():
        host[name] = np.ascontiguousarray(a[source])

    nc = bacc.Bacc("TRN2", target_bir_lowering=False, num_devices=1)
    A = {n: nc.dram_tensor(f"in_{n}", v.shape, mybir.dt.from_np(v.dtype), kind="ExternalInput").ap()
         for n, v in host.items()}
    A["out"] = nc.dram_tensor("out_x", (P, DT * S), F32, kind="ExternalOutput").ap()
    build(nc, A)
    r = run_bass_kernel_spmd(nc, [{f"in_{n}": v for n, v in host.items()}], core_ids=[0])
    y = r.results[0]["out_x"].reshape(P, DT, S).transpose(2, 1, 0).reshape(1, S, D)
    return np.ascontiguousarray(y)
```
